# Optimizing a Trainium2 kernel written in Bass

```python
import math
import jax, jax.numpy as jnp
from jax import lax
import numpy as np

D_MODEL = 1024
BATCH = 1
SEQ = 2048
DEPTH = 1

CHUNK = 64
HEAD_DIM = 64
ROPE_THETA = 10000.0
EPS = 1e-6
NEG = -1e30
MIX_W = D_MODEL
SWA_WIDTH = MIX_W // 2
SWA_Q_HEADS = SWA_WIDTH // HEAD_DIM
SWA_KV_HEADS = 2
SWA_GROUP = SWA_Q_HEADS // SWA_KV_HEADS
SWA_WINDOW = 128
SWA_WIN_CHUNKS = SWA_WINDOW // CHUNK
DIFF_WIDTH = MIX_W - SWA_WIDTH
DIFF_V_DIM = 2 * HEAD_DIM
DIFF_HEADS = DIFF_WIDTH // DIFF_V_DIM
Q_BLOCK = 128
D_FF = -(-8 * D_MODEL // (3 * 256)) * 256

IN_WIDTHS = [SWA_Q_HEADS * HEAD_DIM, SWA_KV_HEADS * HEAD_DIM, SWA_KV_HEADS * HEAD_DIM,
             DIFF_HEADS * 2 * HEAD_DIM, DIFF_HEADS * 2 * HEAD_DIM, DIFF_HEADS * DIFF_V_DIM]
IN_W = sum(IN_WIDTHS)
IN_SPLITS = [int(v) for v in np.cumsum(IN_WIDTHS)[:-1]]

kernel_name = "hybrid_swa_sink_diff_attn_block"

def rms_norm(x, g):
    xf = x.astype(jnp.float32)
    y = xf * lax.rsqrt(jnp.mean(xf * xf, axis=-1, keepdims=True) + EPS)
    return (y * g.astype(jnp.float32)).astype(x.dtype)

def rope_tables(seq):
    inv = 1.0 / (ROPE_THETA ** (jnp.arange(0, HEAD_DIM, 2, dtype=jnp.float32) / HEAD_DIM))
    pos = jnp.arange(seq, dtype=jnp.float32)
    ang = pos[:, None] * inv[None, :]
    return jnp.cos(ang), jnp.sin(ang)

def apply_rope(t, cos, sin):
    x1, x2 = jnp.split(t.astype(jnp.float32), 2, axis=-1)
    c = cos[None, :, None, :]
    s = sin[None, :, None, :]
    return jnp.concatenate([x1 * c - x2 * s, x2 * c + x1 * s], axis=-1).astype(t.dtype)

def swa_sink_attention(q, k, v, sinks):
    b, s, hq, d = q.shape
    nc = s // CHUNK
    qb = q.reshape(b, nc, CHUNK, SWA_KV_HEADS, SWA_GROUP, d)

    def band(t):
        tc = t.reshape(b, nc, CHUNK, SWA_KV_HEADS, d)
        pad = jnp.pad(tc, ((0, 0), (SWA_WIN_CHUNKS - 1, 0), (0, 0), (0, 0), (0, 0)))
        return jnp.concatenate([pad[:, i:i + nc] for i in range(SWA_WIN_CHUNKS)], axis=2)

    kb, vb = band(k), band(v)
    scores = jnp.einsum('bncugd,bnmud->bnugcm', qb, kb).astype(jnp.float32) * (HEAD_DIM ** -0.5)
    slot_chunk = jnp.arange(SWA_WIN_CHUNKS * CHUNK) // CHUNK
    key_chunk = jnp.arange(nc)[:, None] - (SWA_WIN_CHUNKS - 1) + slot_chunk[None, :]
    valid = key_chunk >= 0
    scores = jnp.where(valid[None, :, None, None, None, :], scores, NEG)
    sink = sinks.astype(jnp.float32).reshape(SWA_KV_HEADS, SWA_GROUP)[None, None, :, :, None, None]
    sink = jnp.broadcast_to(sink, scores.shape[:-1] + (1,))
    p = jax.nn.softmax(jnp.concatenate([scores, sink], axis=-1), axis=-1)[..., :-1]
    out = jnp.einsum('bnugcm,bnmud->bncugd', p.astype(v.dtype), vb)
    return out.reshape(b, s, hq * d)

def diff_attention(q, k, v, lam, subln_g, lambda_init):
    b, s, h2, d = q.shape
    h = h2 // 2
    nqb = s // Q_BLOCK
    qb = q.reshape(b, nqb, Q_BLOCK, h2, d).transpose(1, 0, 3, 2, 4)
    kt = k.transpose(0, 2, 1, 3)
    vt = v.transpose(0, 2, 1, 3)
    key_chunk = jnp.arange(s) // CHUNK

    def block(args):
        qi, idx = args
        q_chunk = (idx * Q_BLOCK + jnp.arange(Q_BLOCK)) // CHUNK
        sc = jnp.einsum('bhqd,bhkd->bhqk', qi, kt).astype(jnp.float32) * (HEAD_DIM ** -0.5)
        mask = key_chunk[None, :] <= q_chunk[:, None]
        sc = jnp.where(mask[None, None], sc, NEG)
        p = jax.nn.softmax(sc, axis=-1).reshape(b, h, 2, Q_BLOCK, s)
        a = p[:, :, 0] - lam * p[:, :, 1]
        return jnp.einsum('bhqk,bhkv->bhqv', a.astype(vt.dtype), vt)

    o = lax.map(block, (qb, jnp.arange(nqb)))
    o = o.transpose(1, 0, 3, 2, 4).reshape(b, s, h, DIFF_V_DIM)
    o = rms_norm(o, subln_g) * (1.0 - lambda_init)
    return o.reshape(b, s, h * DIFF_V_DIM)

def setup_inputs(seed: int = 0) -> dict:
    key = jax.random.key(seed)
    ks = jax.random.split(key, 16)
    nrm = lambda k, shape, scale: jax.random.normal(k, shape, dtype=jnp.float32) * scale
    gain = lambda k, shape: 1.0 + 0.02 * jax.random.normal(k, shape, dtype=jnp.float32)
    return {
        "x": nrm(ks[0], (BATCH, SEQ, D_MODEL), 1.0),
        "w_in": nrm(ks[1], (DEPTH, D_MODEL, IN_W), D_MODEL ** -0.5),
        "swa_sinks": nrm(ks[2], (DEPTH, SWA_Q_HEADS), 1.0),
        "diff_lambda_q1": nrm(ks[3], (DEPTH, HEAD_DIM), 0.1),
        "diff_lambda_k1": nrm(ks[4], (DEPTH, HEAD_DIM), 0.1),
        "diff_lambda_q2": nrm(ks[5], (DEPTH, HEAD_DIM), 0.1),
        "diff_lambda_k2": nrm(ks[6], (DEPTH, HEAD_DIM), 0.1),
        "diff_subln": gain(ks[7], (DEPTH, DIFF_V_DIM)),
        "w_out": nrm(ks[8], (DEPTH, MIX_W, D_MODEL), MIX_W ** -0.5),
        "norm_mix_pre": gain(ks[9], (DEPTH, D_MODEL)),
        "norm_mix_post": gain(ks[10], (DEPTH, D_MODEL)),
        "norm_ffn_pre": gain(ks[11], (DEPTH, D_MODEL)),
        "norm_ffn_post": gain(ks[12], (DEPTH, D_MODEL)),
        "w_gate": nrm(ks[13], (DEPTH, D_MODEL, D_FF), D_MODEL ** -0.5),
        "w_up": nrm(ks[14], (DEPTH, D_MODEL, D_FF), D_MODEL ** -0.5),
        "w_down": nrm(ks[15], (DEPTH, D_FF, D_MODEL), D_FF ** -0.5),
    }

def reference(x, w_in, swa_sinks, diff_lambda_q1, diff_lambda_k1, diff_lambda_q2, diff_lambda_k2,
              diff_subln, w_out, norm_mix_pre, norm_mix_post, norm_ffn_pre, norm_ffn_post,
              w_gate, w_up, w_down):
    b, s, _ = x.shape
    cos, sin = rope_tables(s)
    for l in range(DEPTH):
        lambda_init = 0.8 - 0.6 * math.exp(-0.3 * l)
        h = rms_norm(x, norm_mix_pre[l])
        proj = h @ w_in[l]
        qa, ka, va, qd, kd, vd = jnp.split(proj, IN_SPLITS, axis=-1)
        qa = apply_rope(qa.reshape(b, s, SWA_Q_HEADS, HEAD_DIM), cos, sin)
        ka = apply_rope(ka.reshape(b, s, SWA_KV_HEADS, HEAD_DIM), cos, sin)
        va = va.reshape(b, s, SWA_KV_HEADS, HEAD_DIM)
        out_a = swa_sink_attention(qa, ka, va, swa_sinks[l])
        qd = apply_rope(qd.reshape(b, s, 2 * DIFF_HEADS, HEAD_DIM), cos, sin)
        kd = apply_rope(kd.reshape(b, s, 2 * DIFF_HEADS, HEAD_DIM), cos, sin)
        vd = vd.reshape(b, s, DIFF_HEADS, DIFF_V_DIM)
        lam = (jnp.exp(jnp.sum(diff_lambda_q1[l].astype(jnp.float32) * diff_lambda_k1[l].astype(jnp.float32)))
               - jnp.exp(jnp.sum(diff_lambda_q2[l].astype(jnp.float32) * diff_lambda_k2[l].astype(jnp.float32)))
               + lambda_init)
        out_b = diff_attention(qd, kd, vd, lam, diff_subln[l], lambda_init)
        mixed = jnp.concatenate([out_a, out_b], axis=-1) @ w_out[l]
        x = x + rms_norm(mixed, norm_mix_post[l])
        h = rms_norm(x, norm_ffn_pre[l])
        f = (jax.nn.silu(h @ w_gate[l]) * (h @ w_up[l])) @ w_down[l]
        x = x + rms_norm(f, norm_ffn_post[l])
    return x


_drawn_inputs = setup_inputs


def setup_inputs(seed=0):
    import zlib

    import numpy as np

    out = dict(_drawn_inputs(seed))
    spreads = {}
    factors = {'swa_sinks': 8.0,
     'diff_lambda_q2': 8.0,
     'diff_subln': 3.296,
     'norm_mix_post': 3.53,
     'norm_ffn_pre': 3.402,
     'norm_ffn_post': 5.009}
    for name, (base, spread) in spreads.items():
        noise = np.random.default_rng([zlib.crc32(name.encode()), seed]).standard_normal(out[name].shape)
        drawn = base * np.exp(spread * noise) if base else spread * noise
        out[name] = __import__('jax').numpy.asarray(drawn.astype(out[name].dtype))
    for name, factor in factors.items():
        out[name] = (out[name] * factor).astype(out[name].dtype)
    return out
```

```python
from contextlib import ExitStack

import numpy as np

import concourse.bass as bass
from concourse import mybir

F32 = mybir.dt.float32
F32R = mybir.dt.float32r
BF16 = mybir.dt.bfloat16
ALU = mybir.AluOpType
ACT = mybir.ActivationFunctionType
AX = mybir.AxisListType

P = 128
S = 2048
D = 1024
TILES = S // P
KC = D // P
HD = 64
EPS = 1e-6
NEG = -1e30
SCALE = HD ** -0.5
QA = 512
KV = 128
WA = QA + 2 * KV
SH = QA // HD
SG = KV // HD
DW = 512
DH = 4
WB = 3 * DW
VD = 2 * HD
LAMBDA_INIT = 0.8 - 0.6
DF = 2816
FC = DF // P
TB = 512
BLOCKS = S // TB
BT = TB // P


def steady(count, k, i):
    return count(k) if i is None else (count(k + 2) - count(k)) * i + (3 * count(k) - 2 * count(k + 2))


def tiles(eng):
    yield 0, None
    yield 1, None
    with eng.Fori(1, TILES // 2 - 1) as i:
        yield 4, i
        yield 5, i
    yield TILES - 2, None
    yield TILES - 1, None


class Banks:

    def __init__(self, banks, keys):
        self.keys = keys
        self.place = {key: n for n, key in enumerate(keys)}
        self.banks = banks

    def bank(self, *key):
        return self.banks[self.place[key] % len(self.banks)]

    def free(self, pe, read_out, k, i, kind, *n):
        back = self.place[(kind, k, *n)] - len(self.banks)
        if back >= 0:
            what, tile, *rest = self.keys[back]
            semaphore, count = read_out[what]
            pe.wait_ge(semaphore, steady(lambda t: count(t, *rest), tile, i))


class Memory:

    def __init__(self, nc, ctx, phase):
        self.nc, self.ctx, self.phase = nc, ctx, phase
        self.semaphores = []

    def sb(self, name, shape, dt=F32):
        return self.ctx.enter_context(self.nc.sbuf_tensor(f"{self.phase}_{name}", shape, dt))

    def psum(self):
        return self.ctx.enter_context(self.nc.psum_tensor(f"{self.phase}_psum", [P, 8, 512], F32))

    def sem(self, name):
        self.semaphores.append(self.nc.alloc_semaphore(name=f"{self.phase}_{name}"))
        return self.semaphores[-1]

    def end(self):
        self.nc.clear_and_free_semaphores(self.semaphores)
        self.nc.all_engine_barrier()


def wait_apart(eng, met, *waits):
    values = [value if isinstance(value, int) else eng.snap(eng.to_reg(value)) for _, value in waits]
    eng.wait_ge(*met)
    for (semaphore, _), value in zip(waits, values):
        eng.wait_ge(semaphore, value)


def make_identity(pool, ident, step):
    pool.memset(ident[:, :], 0.0).then_inc(step, 1)
    pool.wait_ge(step, 1)
    pool.affine_select(out=ident[:, :], in_=ident[:, :], compare_op=ALU.not_equal, fill=1.0, base=0,
                       pattern=[[-1, P]], channel_multiplier=1).then_inc(step, 1)


def pool_rstd(pool, out, total, width, half, step, done):
    pool.tensor_scalar(out, total, 1.0 / width, EPS, ALU.mult, ALU.add).then_inc(step, 1)
    pool.wait_ge(step, done)
    return pool.tensor_tensor(out, out, half, ALU.pow)


def swa_phase(nc, x, w_in, g_pre, sinks, rope, swa_t):
    order = [("x", 0, 0), ("x", 0, 1)]
    for t in range(TILES + 1):
        if t < TILES:
            order.append(("q", t))
        if t >= 1:
            order += [("s", t - 1, j) for j in range(4)]
        if t < TILES:
            order.append(("kv", t))
        if t + 1 < TILES:
            order += [("x", t + 1, 0), ("x", t + 1, 1)]
        if t < TILES:
            order += [("qT", t), ("kT", t)]
        if t >= 1:
            order += [("a", t - 1, j) for j in range(4)] + [("o", t - 1, u) for u in range(SG)]
    banks = Banks(list(range(8)), order)

    with ExitStack() as ctx:
        m = Memory(nc, ctx, "swa")
        ps = m.psum()
        w_hi = m.sb("w_hi", [P, KC, WA], F32R)
        w_lo = m.sb("w_lo", [P, KC, WA], F32R)
        w_raw = m.sb("w_raw", [P, 4, WA])
        g_col = m.sb("g_col", [P, KC])
        rope_sb = m.sb("rope", [P, TILES, 4 * HD])
        ident = m.sb("ident", [P, P])
        half = m.sb("half", [P, 1])
        sink = m.sb("sink", [P, SH])
        xb = m.sb("x", [P, 2, D])
        junk = m.sb("junk", [P, D], BF16)
        ss = m.sb("ss", [P, 2])
        rstd = m.sb("rstd", [P, 2])
        xt_hi = m.sb("xt_hi", [P, 2, KC, P], F32R)
        xt_lo = m.sb("xt_lo", [P, 2, KC, P], F32R)
        rot_c = m.sb("rot_c", [P, QA])
        rot_s = m.sb("rot_s", [P, QA])
        rot_q = m.sb("rot_q", [P, QA])
        rot_kc = m.sb("rot_kc", [P, KV])
        rot_ks = m.sb("rot_ks", [P, KV])
        rot_k = m.sb("rot_k", [P, KV])
        v_raw = m.sb("v_raw", [P, 2, KV])
        q_hl = m.sb("q_hl", [P, SH // 2, 2, P], F32R)
        q_lh = m.sb("q_lh", [P, SH // 2, 2, P], F32R)
        k_hl = m.sb("k_hl", [P, SG, 2, P], F32R)
        v_hl = m.sb("v_hl", [P, 2, SG, 2 * HD], F32R)
        top = m.sb("top", [P, 2, SH])
        bias = m.sb("bias", [P, 2, SH])
        gap = m.sb("gap", [P, 2, SH])
        sums = m.sb("sums", [P, 2, SH])
        recip = m.sb("recip", [P, 2, SH])
        probs = m.sb("probs", [P, 2, SH, 2 * P])
        at_hi = m.sb("at_hi", [P, 4, 4 * P], F32R)
        at_lo = m.sb("at_lo", [P, 4, 4 * P], F32R)
        o_tmp = m.sb("o_tmp", [P, SH // 2, P])
        o_sum = m.sb("o_sum", [P, 2, SH // 2, P])

        w_loaded = [m.sem(f"w_loaded{n}") for n in range(4)]
        w_hi_done, w_lo_done = m.sem("w_hi_done"), m.sem("w_lo_done")
        consts_loaded, consts_made = m.sem("consts_loaded"), m.sem("consts_made")
        zeroed = m.sem("zeroed")
        x_loaded = [m.sem(f"x_loaded{n}") for n in range(2)]
        squared, pool_step, rstd_ready, x_scaled = (m.sem(n) for n in ("squared", "pool_step", "rstd_ready", "x_scaled"))
        x_turned, xt_hi_done, xt_lo_done = (m.sem(n) for n in ("x_turned", "xt_hi_done", "xt_lo_done"))
        q_projected, kv_projected = m.sem("q_projected"), m.sem("kv_projected")
        q_parts, k_parts, q_roped, k_roped = (m.sem(n) for n in ("q_parts", "k_parts", "q_roped", "k_roped"))
        v_copied, v_hi_done, v_split = (m.sem(n) for n in ("v_copied", "v_hi_done", "v_split"))
        q_turned, k_turned, q_hi_done, k_hi_done, q_split, k_split = (
            m.sem(n) for n in ("q_turned", "k_turned", "q_hi_done", "k_hi_done", "q_split", "k_split"))
        scores_read = m.sem("scores_read")
        scored, dve_step, max_ready, exp_done, recip_ready, scaled = (
            m.sem(n) for n in ("scored", "dve_step", "max_ready", "exp_done", "recip_ready", "scaled"))
        a_turned, at_hi_done, at_lo_done = (m.sem(n) for n in ("a_turned", "at_hi_done", "at_lo_done"))
        attended, o_copied, o_added = (m.sem(n) for n in ("attended", "o_copied", "o_added"))
        stored = [m.sem(f"stored{n}") for n in range(2)]
        read_out = {
            "x": (xt_lo_done, lambda t, h: 2 * t + h + 1), "q": (q_parts, lambda t: t + 1),
            "kv": (v_copied, lambda t: t + 1), "s": (scores_read, lambda t, j: 4 * t + j + 1),
            "qT": (q_split, lambda t: t + 1), "kT": (k_split, lambda t: t + 1),
            "a": (at_lo_done, lambda t, j: 4 * t + j + 1), "o": (o_added, lambda t, u: 2 * (SG * t + u + 1)),
        }

        def chunks_seen(k):
            own = 2 * (k % 2)
            return slice(own, own + 1) if k == 0 else (slice(0, 4, 3) if k % 2 == 0 else slice(1, 3))

        with nc.Block() as block:
            @block.sync
            def _(sp):
                w_view = w_in.rearrange("(c p) n -> c p n", p=P)
                with nc.allow_non_contiguous_dma(reason="gains by column"):
                    sp.dma_start(g_col[:, :], g_pre.rearrange("(c p) -> p c", p=P)).then_inc(consts_loaded, 16)
                sp.dma_start(xb[:, 0, :], x[0:P, :]).then_inc(x_loaded[0], 16)
                sp.dma_start(sink[:, :], sinks.unsqueeze(0).broadcast_to([P, SH])).then_inc(consts_loaded, 16)
                for c in range(KC):
                    if c >= 4:
                        sp.wait_ge(w_lo_done, c - 3)
                    sp.dma_start(w_raw[:, c % 4, :], w_view[c, :, 0:WA]).then_inc(w_loaded[c % 4], 16)
                    if c == 3:
                        sp.dma_start(rope_sb[:, :, :], rope.rearrange("(t p) n -> p t n", p=P)).then_inc(consts_loaded, 16)
                sp.dma_start(xb[:, 1, :], x[P:2 * P, :]).then_inc(x_loaded[1], 16)
                for k, i in tiles(sp):
                    p = k % 2
                    if k + 2 < TILES:
                        row = steady(lambda t: (t + 2) * P, k, i)
                        wait_apart(sp, (consts_loaded, 48), (x_turned, steady(lambda t: 2 * t + 2, k, i)))
                        sp.dma_start(xb[:, p, :], x[bass.ds(row, P), :]).then_inc(x_loaded[p], 16)
                    if k >= 1:
                        col = steady(lambda t: (t - 1) * P, k, i)
                        wait_apart(sp, (consts_loaded, 48), (o_added, steady(lambda t: 2 * SG * t, k, i)))
                        sp.dma_start(swa_t[:, :, bass.ds(col, P)], o_sum[:, 1 - p, :, :]).then_inc(stored[1 - p], 16)
                sp.wait_ge(o_added, 2 * SG * TILES)
                sp.dma_start(swa_t[:, :, (TILES - 1) * P:S], o_sum[:, 1, :, :]).then_inc(stored[1], 16)
                for q in stored:
                    sp.wait_ge(q, 16 * TILES // 2)

            @block.gpsimd
            def _(pool):
                make_identity(pool, ident, consts_made)
                pool.memset(half[:, :], -0.5).then_inc(consts_made, 1)
                pool.wait_ge(consts_made, 3)
                pool.memset(probs[:, :, :, :], 0.0).then_inc(zeroed, 1)

                def rstd_of(k, i):
                    waits = [(squared, steady(lambda t: t + 1, k, i))]
                    if k >= 2:
                        waits.append((x_scaled, steady(lambda t: t - 1, k, i)))
                    wait_apart(pool, (consts_made, 3), *waits)
                    q = k % 2
                    pool_rstd(pool, rstd[:, q:q + 1], ss[:, q:q + 1], D, half[:, :], pool_step,
                              steady(lambda t: t + 1, k, i)).then_inc(rstd_ready, 1)

                def rotate(k, i, parts, turned, out, a, b, roped):
                    pool.wait_ge(parts, steady(lambda t: t + 1, k, i))
                    if k >= 1:
                        pool.wait_ge(turned, steady(lambda t: t, k, i))
                    pool.tensor_tensor(out[:, :], a[:, :], b[:, :], ALU.add).then_inc(roped, 1)

                def scale_probs(k, i):
                    q = k % 2
                    pool.wait_ge(recip_ready, steady(lambda t: t + 1, k, i))
                    pool.tensor_tensor(probs[:, q, :, :], probs[:, q, :, :],
                                       recip[:, q, :].unsqueeze(2).broadcast_to([P, SH, 2 * P]), ALU.mult)\
                        .then_inc(scaled, 1)

                def split_v(k, i):
                    q = k % 2
                    waits = [(v_copied, steady(lambda t: t + 1, k, i))]
                    if k >= 1:
                        waits.append((attended, steady(lambda t: SG * t, k, i)))
                    wait_apart(pool, (consts_made, 3), *waits)
                    v = v_raw[:, q, :].rearrange("p (u d) -> p u d", u=SG)
                    pool.tensor_copy(v_hl[:, q, :, 0:HD], v).then_inc(v_hi_done, 1)
                    pool.wait_ge(v_hi_done, steady(lambda t: t + 1, k, i))
                    pool.tensor_tensor(v_hl[:, q, :, HD:2 * HD], v, v_hl[:, q, :, 0:HD].bitcast(F32), ALU.subtract)\
                        .then_inc(v_split, 1)

                rstd_of(0, None)
                for k, i in tiles(pool):
                    if k + 1 < TILES:
                        rstd_of(k + 1, i)
                    rotate(k, i, q_parts, q_turned, rot_q, rot_c, rot_s, q_roped)
                    rotate(k, i, k_parts, k_turned, rot_k, rot_kc, rot_ks, k_roped)
                    if k >= 1:
                        scale_probs(k - 1, i)
                    split_v(k, i)
                scale_probs(TILES - 1, None)

            @block.scalar
            def _(act):
                def square(k, i):
                    q = k % 2
                    act.wait_ge(x_loaded[q], steady(lambda t: 16 * (t // 2 + 1), k, i))
                    if k >= 2:
                        act.wait_ge(rstd_ready, steady(lambda t: t - 1, k, i))
                    act.activation(junk[:, :], xb[:, q, :], ACT.Square, accum_out=ss[:, q:q + 1]).then_inc(squared, 1)

                def turned_hi(k, i):
                    q = k % 2
                    for h in range(2):
                        act.wait_ge(x_turned, steady(lambda t: 2 * t + h + 1, k, i))
                        if k >= 2 and h == 0:
                            act.wait_ge(kv_projected, steady(lambda t: t - 1, k, i))
                        b = banks.bank("x", k, h)
                        act.activation(xt_hi[:, q, 4 * h:4 * h + 4, :], ps[:, b, :].rearrange("p (c n) -> p c n", n=P),
                                       ACT.Copy).then_inc(xt_hi_done, 1)

                def exps(k, i):
                    q = k % 2
                    act.wait_ge(max_ready, steady(lambda t: t + 1, k, i))
                    if k == 0:
                        act.wait_ge(zeroed, 1)
                    if k >= 2:
                        act.wait_ge(a_turned, steady(lambda t: 4 * (t - 1), k, i))
                        act.wait_ge(recip_ready, steady(lambda t: t - 1, k, i))
                    for j in range(4):
                        sc = ps[:, banks.bank("s", k, j), :].rearrange("p (h c n) -> p h c n", h=2, c=4)
                        pr = probs[:, q, 2 * j:2 * j + 2, :].rearrange("p h (c n) -> p h c n", c=4)
                        for h in range(2):
                            hh = 2 * j + h
                            seen, own = chunks_seen(k), slice(2 * q, 2 * q + 2)
                            for lo, cs in ((0, seen), (HD, own)):
                                part = slice(lo, lo + HD)
                                last = act.activation(pr[part, h, cs, :], sc[part, h, cs, :], ACT.Exp,
                                                      bias=bias[part, q, hh:hh + 1], accum_out=sums[part, q, hh:hh + 1])
                        last.then_inc(scores_read, 1)
                    act.activation(gap[:, q, :], gap[:, q, :], ACT.Exp).then_inc(exp_done, 1)

                def hi_qk(k, i):
                    q = k % 2
                    act.wait_ge(q_turned, steady(lambda t: t + 1, k, i))
                    src = ps[:, banks.bank("qT", k), :].rearrange("p (j n) -> p j n", n=P)
                    act.activation(q_hl[0:HD, :, 0, :], src[0:HD, :, :], ACT.Copy)
                    act.activation(q_hl[0:HD, :, 1, :], src[HD:P, :, :], ACT.Copy)
                    act.activation(q_lh[HD:P, :, 0, :], src[0:HD, :, :], ACT.Copy)
                    act.activation(q_lh[HD:P, :, 1, :], src[HD:P, :, :], ACT.Copy).then_inc(q_hi_done, 1)
                    act.wait_ge(k_turned, steady(lambda t: t + 1, k, i))
                    src = ps[:, banks.bank("kT", k), 0:P]
                    act.activation(k_hl[0:HD, 0, q, :], src[0:HD, :], ACT.Copy)
                    act.activation(k_hl[0:HD, 1, q, :], src[HD:P, :], ACT.Copy).then_inc(k_hi_done, 1)

                def copy_v(k, i):
                    act.wait_ge(k_parts, steady(lambda t: t + 1, k, i))
                    if k >= 2:
                        act.wait_ge(v_split, steady(lambda t: t - 1, k, i))
                    b = banks.bank("kv", k)
                    act.activation(v_raw[:, k % 2, :], ps[:, b, KV:2 * KV], ACT.Copy).then_inc(v_copied, 1)

                def hi_a(k, i):
                    for j in range(4):
                        act.wait_ge(a_turned, steady(lambda t: 4 * t + j + 1, k, i))
                        if k >= 1 and j == 0:
                            act.wait_ge(attended, steady(lambda t: SG * t, k, i))
                        b = banks.bank("a", k, j)
                        act.activation(at_hi[:, j, :], ps[:, b, :], ACT.Copy).then_inc(at_hi_done, 1)

                def copy_o(k, i):
                    for u in range(SG):
                        act.wait_ge(attended, steady(lambda t: SG * t + u + 1, k, i))
                        if k >= 1 and u == 0:
                            act.wait_ge(o_added, steady(lambda t: 2 * SG * t, k, i))
                        src = ps[:, banks.bank("o", k, u), :].rearrange("p (j e n) -> p j e n", e=2, n=P)
                        act.activation(o_tmp[0:HD, 2 * u:2 * u + 2, :], src[HD:P, :, 0, :], ACT.Copy)
                        act.activation(o_tmp[HD:P, 2 * u:2 * u + 2, :], src[0:HD, :, 1, :], ACT.Copy).then_inc(o_copied, 1)

                act.wait_ge(consts_loaded, 48)
                square(0, None)
                for c in range(KC):
                    act.wait_ge(w_loaded[c % 4], 16 * (c // 4 + 1))
                    act.activation(w_hi[:, c, :], w_raw[:, c % 4, :], ACT.Copy, scale=g_col[:, c:c + 1])\
                        .then_inc(w_hi_done, 1)
                turned_hi(0, None)
                for k, i in tiles(act):
                    if k + 1 < TILES:
                        square(k + 1, i)
                    if k >= 1:
                        exps(k - 1, i)
                    copy_v(k, i)
                    if k + 1 < TILES:
                        turned_hi(k + 1, i)
                    hi_qk(k, i)
                    if k >= 1:
                        hi_a(k - 1, i)
                        copy_o(k - 1, i)
                exps(TILES - 1, None)
                hi_a(TILES - 1, None)
                copy_o(TILES - 1, None)

            @block.vector
            def _(dve):
                def scale_x(k, i):
                    q = k % 2
                    dve.wait_ge(rstd_ready, steady(lambda t: t + 1, k, i))
                    dve.tensor_scalar(xb[:, q, :], xb[:, q, :], rstd[:, q:q + 1], None, ALU.mult).then_inc(x_scaled, 1)

                def turned_lo(k, i):
                    q = k % 2
                    for h in range(2):
                        dve.wait_ge(xt_hi_done, steady(lambda t: 2 * t + h + 1, k, i))
                        b = banks.bank("x", k, h)
                        dve.tensor_tensor(xt_lo[:, q, 4 * h:4 * h + 4, :], ps[:, b, :].rearrange("p (c n) -> p c n", n=P),
                                          xt_hi[:, q, 4 * h:4 * h + 4, :].bitcast(F32), ALU.subtract)\
                            .then_inc(xt_lo_done, 1)

                def rope_parts(k, i, src, heads, c_out, s_out, scaled_by, tok):
                    cos = rope_sb[:, tok, scaled_by:scaled_by + HD]
                    sin = rope_sb[:, tok, scaled_by + HD:scaled_by + 2 * HD]
                    view = src.rearrange("p (h d) -> p h d", d=HD)
                    dve.tensor_tensor(c_out[:, :].rearrange("p (h d) -> p h d", d=HD), view,
                                      cos.broadcast_to([P, heads, HD]), ALU.mult)
                    for a in range(2):
                        to, frm = slice(a * HD // 2, (a + 1) * HD // 2), slice((1 - a) * HD // 2, (2 - a) * HD // 2)
                        last = dve.tensor_tensor(
                            s_out[:, :].rearrange("p (h d) -> p h d", d=HD)[:, :, to], view[:, :, frm],
                            sin[:, :, to].broadcast_to([P, heads, HD // 2]), ALU.mult)
                    return last

                def rope_q(k, i):
                    dve.wait_ge(q_projected, steady(lambda t: t + 1, k, i))
                    if k >= 1:
                        dve.wait_ge(q_roped, steady(lambda t: t, k, i))
                    tok = bass.ds(steady(lambda t: t, k, i), 1)
                    b = banks.bank("q", k)
                    rope_parts(k, i, ps[:, b, :], SH, rot_c, rot_s, 2 * HD, tok).then_inc(q_parts, 1)

                def rope_k(k, i):
                    dve.wait_ge(kv_projected, steady(lambda t: t + 1, k, i))
                    if k >= 1:
                        dve.wait_ge(k_roped, steady(lambda t: t, k, i))
                    tok = bass.ds(steady(lambda t: t, k, i), 1)
                    rope_parts(k, i, ps[:, banks.bank("kv", k), 0:KV], SG, rot_kc, rot_ks, 0, tok).then_inc(k_parts, 1)

                def maxima(k, i):
                    q = k % 2
                    if k >= 2:
                        dve.wait_ge(exp_done, steady(lambda t: t - 1, k, i))
                    for j in range(4):
                        dve.wait_ge(scored, steady(lambda t: 4 * t + j + 1, k, i))
                        sc = ps[:, banks.bank("s", k, j), :].rearrange("p (h c n) -> p h c n", h=2, c=4)
                        for lo, cs in ((0, chunks_seen(k)), (HD, slice(2 * q, 2 * q + 2))):
                            part = slice(lo, lo + HD)
                            last = dve.tensor_reduce(top[part, q, 2 * j:2 * j + 2], sc[part, :, cs, :], AX.XY, ALU.max)
                    last.then_inc(dve_step, 1)
                    dve.wait_ge(dve_step, steady(lambda t: 3 * t + 1, k, i))
                    dve.tensor_tensor(top[:, q, :], top[:, q, :], sink[:, :], ALU.max).then_inc(dve_step, 1)
                    dve.wait_ge(dve_step, steady(lambda t: 3 * t + 2, k, i))
                    dve.tensor_scalar(bias[:, q, :], top[:, q, :], -1.0, None, ALU.mult)
                    dve.tensor_tensor(gap[:, q, :], sink[:, :], top[:, q, :], ALU.subtract).then_inc(max_ready, 1)

                def recips(k, i):
                    q = k % 2
                    dve.wait_ge(exp_done, steady(lambda t: t + 1, k, i))
                    if k >= 2:
                        dve.wait_ge(scaled, steady(lambda t: t - 1, k, i))
                    dve.tensor_tensor(sums[:, q, :], sums[:, q, :], gap[:, q, :], ALU.add).then_inc(dve_step, 1)
                    dve.wait_ge(dve_step, steady(lambda t: 3 * t + 3, k, i))
                    dve.reciprocal(recip[:, q, :], sums[:, q, :]).then_inc(recip_ready, 1)

                def lo_qk(k, i):
                    q = k % 2
                    dve.wait_ge(q_hi_done, steady(lambda t: t + 1, k, i))
                    b = banks.bank("qT", k)
                    src = ps[:, b, :].rearrange("p (j n) -> p j n", n=P)
                    even, odd = q_hl[0:HD, :, 0, :].bitcast(F32), q_lh[HD:P, :, 1, :].bitcast(F32)
                    dve.tensor_tensor(q_hl[HD:P, :, 0, :], src[0:HD, :, :], even, ALU.subtract)
                    dve.tensor_tensor(q_lh[0:HD, :, 0, :], src[0:HD, :, :], even, ALU.subtract)
                    dve.tensor_tensor(q_hl[HD:P, :, 1, :], src[HD:P, :, :], odd, ALU.subtract)
                    dve.tensor_tensor(q_lh[0:HD, :, 1, :], src[HD:P, :, :], odd, ALU.subtract).then_inc(q_split, 1)
                    dve.wait_ge(k_hi_done, steady(lambda t: t + 1, k, i))
                    b = banks.bank("kT", k)
                    dve.tensor_tensor(k_hl[HD:P, 0, q, :], ps[0:HD, b, 0:P], k_hl[0:HD, 0, q, :].bitcast(F32), ALU.subtract)
                    dve.tensor_tensor(k_hl[HD:P, 1, q, :], ps[HD:P, b, 0:P], k_hl[0:HD, 1, q, :].bitcast(F32),
                                      ALU.subtract).then_inc(k_split, 1)

                def lo_a(k, i):
                    for j in range(4):
                        dve.wait_ge(at_hi_done, steady(lambda t: 4 * t + j + 1, k, i))
                        b = banks.bank("a", k, j)
                        dve.tensor_tensor(at_lo[:, j, :], ps[:, b, :], at_hi[:, j, :].bitcast(F32), ALU.subtract)\
                            .then_inc(at_lo_done, 1)

                def add_o(k, i):
                    q = k % 2
                    for u in range(SG):
                        dve.wait_ge(o_copied, steady(lambda t: SG * t + u + 1, k, i))
                        if k >= 2 and u == 0:
                            dve.wait_ge(stored[q], steady(lambda t: 16 * (t // 2), k, i))
                        b = banks.bank("o", k, u)
                        src = ps[:, b, :].rearrange("p (j e n) -> p j e n", e=2, n=P)
                        dve.tensor_tensor(o_sum[0:HD, q, 2 * u:2 * u + 2, :], src[0:HD, :, 0, :],
                                          o_tmp[0:HD, 2 * u:2 * u + 2, :], ALU.add).then_inc(o_added, 1)
                        dve.tensor_tensor(o_sum[HD:P, q, 2 * u:2 * u + 2, :], src[HD:P, :, 1, :],
                                          o_tmp[HD:P, 2 * u:2 * u + 2, :], ALU.add).then_inc(o_added, 1)

                scale_x(0, None)
                for c in range(KC):
                    dve.wait_ge(w_hi_done, c + 1)
                    dve.scalar_tensor_tensor(w_lo[:, c, :], w_raw[:, c % 4, :], g_col[:, c:c + 1],
                                             w_hi[:, c, :].bitcast(F32), ALU.mult, ALU.subtract).then_inc(w_lo_done, 1)
                turned_lo(0, None)
                for k, i in tiles(dve):
                    rope_q(k, i)
                    if k >= 1:
                        maxima(k - 1, i)
                    if k + 1 < TILES:
                        scale_x(k + 1, i)
                    rope_k(k, i)
                    if k + 1 < TILES:
                        turned_lo(k + 1, i)
                    if k >= 1:
                        recips(k - 1, i)
                    lo_qk(k, i)
                    if k >= 1:
                        lo_a(k - 1, i)
                        add_o(k - 1, i)
                maxima(TILES - 1, None)
                recips(TILES - 1, None)
                lo_a(TILES - 1, None)
                add_o(TILES - 1, None)

            @block.tensor
            def _(pe):
                def free(k, i, kind, *n):
                    banks.free(pe, read_out, k, i, kind, *n)
                    return banks.bank(kind, k, *n)

                def turn_x(k, i):
                    pe.wait_ge(x_scaled, steady(lambda t: t + 1, k, i))
                    for h in range(2):
                        b = free(k, i, "x", h)
                        for c in range(4):
                            last = pe.transpose(ps[:, b, c * P:(c + 1) * P],
                                                xb[:, k % 2, (4 * h + c) * P:(4 * h + c + 1) * P], ident[:, :])
                        last.then_inc(x_turned, 1)

                def project(k, i, kind, first, width, done):
                    q = k % 2
                    b = free(k, i, kind)
                    for c in range(KC):
                        if kind == "q" and c % 4 == 0:
                            pe.wait_ge(xt_lo_done, steady(lambda t: 2 * t + c // 4 + 1, k, i))
                        if k == 0 and kind == "q":
                            pe.wait_ge(w_lo_done, c + 1)
                        for n, (lhs, rhs) in enumerate(((xt_hi, w_hi), (xt_hi, w_lo), (xt_lo, w_hi))):
                            last = pe.matmul(ps[:, b, 0:width], lhs[:, q, c, :], rhs[:, c, first:first + width],
                                             start=(c == 0 and n == 0), stop=(c == KC - 1 and n == 2))
                    last.then_inc(done, 1)

                def turn_qk(k, i):
                    pe.wait_ge(q_roped, steady(lambda t: t + 1, k, i))
                    b = free(k, i, "qT")
                    for j in range(4):
                        last = pe.transpose(ps[:, b, j * P:(j + 1) * P], rot_q[:, j * P:(j + 1) * P], ident[:, :])
                    last.then_inc(q_turned, 1)
                    pe.wait_ge(k_roped, steady(lambda t: t + 1, k, i))
                    b = free(k, i, "kT")
                    pe.transpose(ps[:, b, 0:P], rot_k[:, :], ident[:, :]).then_inc(k_turned, 1)

                def score(k, i):
                    pe.wait_ge(q_split, steady(lambda t: t + 1, k, i))
                    pe.wait_ge(k_split, steady(lambda t: t + 1, k, i))
                    slots = 1 if k == 0 else 2
                    for j in range(4):
                        b = free(k, i, "s", j)
                        for h in range(2):
                            for n, stack in enumerate((q_hl, q_lh)):
                                last = pe.matmul(ps[:, b, 2 * P * h:2 * P * h + slots * P], stack[:, j, h, :],
                                                 k_hl[:, j // 2, 0:slots, :], start=(n == 0), stop=(n == 1))
                        last.then_inc(scored, 1)

                def turn_a(k, i):
                    pe.wait_ge(scaled, steady(lambda t: t + 1, k, i))
                    for j in range(4):
                        u, slot = j // 2, j % 2
                        b = free(k, i, "a", j)
                        for h in range(4):
                            last = pe.transpose(ps[:, b, h * P:(h + 1) * P],
                                                probs[:, k % 2, 4 * u + h, slot * P:(slot + 1) * P], ident[:, :])
                        last.then_inc(a_turned, 1)

                def attend(k, i):
                    pe.wait_ge(v_split, steady(lambda t: t + 1, k, i))
                    slots = (0,) if k == 0 else (0, 1)
                    for u in range(SG):
                        b = free(k, i, "o", u)
                        for slot in slots:
                            pe.wait_ge(at_lo_done, steady(lambda t: 4 * t + 2 * u + slot + 1, k, i))
                            for n, a in enumerate((at_hi, at_lo)):
                                last = pe.matmul(ps[:, b, :], v_hl[:, slot, u, :], a[:, 2 * u + slot, :],
                                                 start=(slot == 0 and n == 0), stop=(slot == slots[-1] and n == 1))
                        last.then_inc(attended, 1)

                pe.wait_ge(consts_made, 2)
                turn_x(0, None)
                for k, i in tiles(pe):
                    project(k, i, "q", 0, QA, q_projected)
                    if k >= 1:
                        score(k - 1, i)
                    project(k, i, "kv", QA, 2 * KV, kv_projected)
                    if k + 1 < TILES:
                        turn_x(k + 1, i)
                    turn_qk(k, i)
                    if k >= 1:
                        turn_a(k - 1, i)
                        attend(k - 1, i)
                score(TILES - 1, None)
                turn_a(TILES - 1, None)
                attend(TILES - 1, None)
        m.end()


def diff_proj(nc, x, w_in, g_pre, rope, q_s, k_s, v_s):
    order = [("x", 0, 0), ("x", 0, 1)]
    for t in range(TILES + 1):
        if t < TILES:
            order.append(("q", t))
        if t >= 1:
            order.append(("kT", t - 1))
        if t < TILES:
            order += [("k", t), ("qT", t), ("v", t)]
        if t + 1 < TILES:
            order += [("x", t + 1, 0), ("x", t + 1, 1)]
    banks = Banks(list(range(7)), order)
    first = WA

    with ExitStack() as ctx:
        m = Memory(nc, ctx, "dp")
        ps = m.psum()
        w_hi = m.sb("w_hi", [P, KC, WB], F32R)
        w_lo = m.sb("w_lo", [P, KC, WB], F32R)
        w_raw = m.sb("w_raw", [P, 4, WB])
        g_col = m.sb("g_col", [P, KC])
        rope_sb = m.sb("rope", [P, 2, 4 * HD])
        ident = m.sb("ident", [P, P])
        half = m.sb("half", [P, 1])
        xb = m.sb("x", [P, 2, D])
        junk = m.sb("junk", [P, D], BF16)
        ss = m.sb("ss", [P, 2])
        rstd = m.sb("rstd", [P, 2])
        xt_hi = m.sb("xt_hi", [P, 2, KC, P], F32R)
        xt_lo = m.sb("xt_lo", [P, 2, KC, P], F32R)
        part_c = m.sb("part_c", [P, 2, DW])
        part_s = m.sb("part_s", [P, 2, DW])
        rot = m.sb("rot", [P, 2, DW])
        q_hl = m.sb("q_hl", [P, DH, 2, P], F32R)
        k_hl = m.sb("k_hl", [P, DH, 2, P], F32R)
        v_hl = m.sb("v_hl", [P, 2, DH, 2, VD], F32R)

        w_loaded = [m.sem(f"w_loaded{n}") for n in range(4)]
        w_hi_done, w_lo_done = m.sem("w_hi_done"), m.sem("w_lo_done")
        consts_loaded, consts_made = m.sem("consts_loaded"), m.sem("consts_made")
        x_loaded = [m.sem(f"x_loaded{n}") for n in range(2)]
        rope_loaded = [m.sem(f"rope_loaded{n}") for n in range(2)]
        squared, pool_step, rstd_ready, x_scaled = (m.sem(n) for n in ("squared", "pool_step", "rstd_ready", "x_scaled"))
        x_turned, xt_hi_done, xt_lo_done = (m.sem(n) for n in ("x_turned", "xt_hi_done", "xt_lo_done"))
        projected = [m.sem(n) for n in ("q_projected", "k_projected", "v_projected")]
        parts = [m.sem(n) for n in ("q_parts", "k_parts")]
        roped = [m.sem(n) for n in ("q_roped", "k_roped")]
        turned = [m.sem(n) for n in ("q_turned", "k_turned")]
        hi_done = [m.sem(n) for n in ("q_hi_done", "k_hi_done")]
        split = [m.sem(n) for n in ("q_split", "k_split")]
        v_hi_done, v_split = m.sem("v_hi_done"), m.sem("v_split")
        stored = [m.sem(n) for n in ("q_stored", "k_stored")]
        v_stored = [m.sem(f"v_stored{n}") for n in range(2)]
        read_out = {
            "x": (xt_lo_done, lambda t, h: 2 * t + h + 1), "q": (parts[0], lambda t: t + 1),
            "k": (parts[1], lambda t: t + 1), "v": (v_split, lambda t: t + 1),
            "qT": (split[0], lambda t: t + 1), "kT": (split[1], lambda t: t + 1),
        }

        with nc.Block() as block:
            @block.sync
            def _(sp):
                w_view = w_in.rearrange("(c p) n -> c p n", p=P)
                with nc.allow_non_contiguous_dma(reason="gains by column"):
                    sp.dma_start(g_col[:, :], g_pre.rearrange("(c p) -> p c", p=P)).then_inc(consts_loaded, 16)
                for n in range(2):
                    sp.dma_start(xb[:, n, :], x[n * P:(n + 1) * P, :]).then_inc(x_loaded[n], 16)
                    sp.dma_start(rope_sb[:, n, :], rope[n * P:(n + 1) * P, :]).then_inc(rope_loaded[n], 16)
                for c in range(KC):
                    if c >= 4:
                        sp.wait_ge(w_lo_done, c - 3)
                    sp.dma_start(w_raw[:, c % 4, :], w_view[c, :, first:first + WB]).then_inc(w_loaded[c % 4], 16)
                for k, i in tiles(sp):
                    p = k % 2
                    if k >= 1:
                        col = steady(lambda t: (t - 1) * P, k, i)
                        wait_apart(sp, (consts_loaded, 16), (split[1], steady(lambda t: t, k, i)))
                        sp.dma_start(k_s[:, :, :, bass.ds(col, P)], k_hl[:, :, :, :].bitcast(F32)).then_inc(stored[1], 16)
                    wait_apart(sp, (consts_loaded, 16), (split[0], steady(lambda t: t + 1, k, i)))
                    sp.dma_start(q_s[bass.ds(steady(lambda t: t, k, i), 1), :, :, :, :].rearrange("a p h m n -> p (a h) m n"),
                                 q_hl[:, :, :, :].bitcast(F32)).then_inc(stored[0], 16)
                    if k + 2 < TILES:
                        row = steady(lambda t: (t + 2) * P, k, i)
                        wait_apart(sp, (consts_loaded, 16), (x_turned, steady(lambda t: 2 * t + 2, k, i)),
                                   (parts[1], steady(lambda t: t + 1, k, i)))
                        sp.dma_start(xb[:, p, :], x[bass.ds(row, P), :]).then_inc(x_loaded[p], 16)
                        sp.dma_start(rope_sb[:, p, :], rope[bass.ds(row, P), :]).then_inc(rope_loaded[p], 16)
                    wait_apart(sp, (consts_loaded, 16), (v_split, steady(lambda t: t + 1, k, i)))
                    sp.dma_start(v_s[:, :, bass.ds(steady(lambda t: t, k, i), 1), :, :].rearrange("p h t a v -> p h (t a) v"),
                                 v_hl[:, p, :, :, :].bitcast(F32)).then_inc(v_stored[p], 16)
                sp.wait_ge(split[1], TILES)
                sp.dma_start(k_s[:, :, :, (TILES - 1) * P:S], k_hl[:, :, :, :].bitcast(F32)).then_inc(stored[1], 16)
                for s in stored:
                    sp.wait_ge(s, 16 * TILES)
                for s in v_stored:
                    sp.wait_ge(s, 16 * TILES // 2)

            @block.gpsimd
            def _(pool):
                make_identity(pool, ident, consts_made)
                pool.memset(half[:, :], -0.5).then_inc(consts_made, 1)
                pool.wait_ge(consts_made, 3)

                def rstd_of(k, i):
                    waits = [(squared, steady(lambda t: t + 1, k, i))]
                    if k >= 2:
                        waits.append((x_scaled, steady(lambda t: t - 1, k, i)))
                    wait_apart(pool, (consts_made, 3), *waits)
                    q = k % 2
                    pool_rstd(pool, rstd[:, q:q + 1], ss[:, q:q + 1], D, half[:, :], pool_step,
                              steady(lambda t: t + 1, k, i)).then_inc(rstd_ready, 1)

                def rotate(n, k, i):
                    pool.wait_ge(parts[n], steady(lambda t: t + 1, k, i))
                    if k >= 1:
                        pool.wait_ge(turned[n], steady(lambda t: t, k, i))
                    pool.tensor_tensor(rot[:, n, :], part_c[:, n, :], part_s[:, n, :], ALU.add).then_inc(roped[n], 1)

                rstd_of(0, None)
                for k, i in tiles(pool):
                    if k + 1 < TILES:
                        rstd_of(k + 1, i)
                    rotate(0, k, i)
                    rotate(1, k, i)

            @block.scalar
            def _(act):
                def square(k, i):
                    q = k % 2
                    act.wait_ge(x_loaded[q], steady(lambda t: 16 * (t // 2 + 1), k, i))
                    if k >= 2:
                        act.wait_ge(rstd_ready, steady(lambda t: t - 1, k, i))
                    act.activation(junk[:, :], xb[:, q, :], ACT.Square, accum_out=ss[:, q:q + 1]).then_inc(squared, 1)

                def turned_hi(k, i):
                    q = k % 2
                    for h in range(2):
                        act.wait_ge(x_turned, steady(lambda t: 2 * t + h + 1, k, i))
                        if k >= 2 and h == 0:
                            act.wait_ge(projected[2], steady(lambda t: t - 1, k, i))
                        b = banks.bank("x", k, h)
                        act.activation(xt_hi[:, q, 4 * h:4 * h + 4, :], ps[:, b, :].rearrange("p (c n) -> p c n", n=P),
                                       ACT.Copy).then_inc(xt_hi_done, 1)

                def hi_qk(n, k, i):
                    out = (q_hl, k_hl)[n]
                    act.wait_ge(turned[n], steady(lambda t: t + 1, k, i))
                    if k >= 1:
                        act.wait_ge(stored[n], steady(lambda t: 16 * t, k, i))
                    src = ps[:, banks.bank(("qT", "kT")[n], k), :].rearrange("p (h n) -> p h n", n=P)
                    act.activation(out[0:HD, :, 0, :], src[0:HD, :, :], ACT.Copy)
                    act.activation(out[0:HD, :, 1, :], src[HD:P, :, :], ACT.Copy).then_inc(hi_done[n], 1)

                def hi_v(k, i):
                    act.wait_ge(projected[2], steady(lambda t: t + 1, k, i))
                    if k >= 2:
                        act.wait_ge(v_stored[k % 2], steady(lambda t: 16 * (t // 2), k, i))
                    act.activation(v_hl[:, k % 2, :, 0, :], ps[:, banks.bank("v", k), :].rearrange("p (h v) -> p h v", h=DH),
                                   ACT.Copy).then_inc(v_hi_done, 1)

                act.wait_ge(consts_loaded, 16)
                square(0, None)
                for c in range(KC):
                    act.wait_ge(w_loaded[c % 4], 16 * (c // 4 + 1))
                    act.activation(w_hi[:, c, :], w_raw[:, c % 4, :], ACT.Copy, scale=g_col[:, c:c + 1])\
                        .then_inc(w_hi_done, 1)
                turned_hi(0, None)
                for k, i in tiles(act):
                    if k >= 1:
                        hi_v(k - 1, i)
                        hi_qk(1, k - 1, i)
                    if k + 1 < TILES:
                        square(k + 1, i)
                    hi_qk(0, k, i)
                    if k + 1 < TILES:
                        turned_hi(k + 1, i)
                hi_v(TILES - 1, None)
                hi_qk(1, TILES - 1, None)

            @block.vector
            def _(dve):
                def scale_x(k, i):
                    q = k % 2
                    dve.wait_ge(rstd_ready, steady(lambda t: t + 1, k, i))
                    dve.tensor_scalar(xb[:, q, :], xb[:, q, :], rstd[:, q:q + 1], None, ALU.mult).then_inc(x_scaled, 1)

                def turned_lo(k, i):
                    q = k % 2
                    for h in range(2):
                        dve.wait_ge(xt_hi_done, steady(lambda t: 2 * t + h + 1, k, i))
                        dve.tensor_tensor(xt_lo[:, q, 4 * h:4 * h + 4, :],
                                          ps[:, banks.bank("x", k, h), :].rearrange("p (c n) -> p c n", n=P),
                                          xt_hi[:, q, 4 * h:4 * h + 4, :].bitcast(F32), ALU.subtract)\
                            .then_inc(xt_lo_done, 1)

                def rope_parts(n, k, i):
                    q = k % 2
                    dve.wait_ge(projected[n], steady(lambda t: t + 1, k, i))
                    if n == 0:
                        dve.wait_ge(rope_loaded[q], steady(lambda t: 16 * (t // 2 + 1), k, i))
                    if k >= 1:
                        dve.wait_ge(roped[n], steady(lambda t: t, k, i))
                    at = 2 * HD * (1 - n)
                    cos, sin = rope_sb[:, q, at:at + HD].unsqueeze(1), rope_sb[:, q, at + HD:at + 2 * HD].unsqueeze(1)
                    view = ps[:, banks.bank(("q", "k")[n], k), :].rearrange("p (h d) -> p h d", d=HD)
                    c_out = part_c[:, n, :].rearrange("p (h d) -> p h d", d=HD)
                    s_out = part_s[:, n, :].rearrange("p (h d) -> p h d", d=HD)
                    heads = 2 * DH
                    dve.tensor_tensor(c_out, view, cos.broadcast_to([P, heads, HD]), ALU.mult)
                    for a in range(2):
                        to, frm = slice(a * HD // 2, (a + 1) * HD // 2), slice((1 - a) * HD // 2, (2 - a) * HD // 2)
                        last = dve.tensor_tensor(s_out[:, :, to], view[:, :, frm],
                                                 sin[:, :, to].broadcast_to([P, heads, HD // 2]), ALU.mult)
                    last.then_inc(parts[n], 1)

                def lo_qk(n, k, i):
                    out = (q_hl, k_hl)[n]
                    dve.wait_ge(hi_done[n], steady(lambda t: t + 1, k, i))
                    src = ps[:, banks.bank(("qT", "kT")[n], k), :].rearrange("p (h n) -> p h n", n=P)
                    dve.tensor_tensor(out[HD:P, :, 0, :], src[0:HD, :, :], out[0:HD, :, 0, :].bitcast(F32), ALU.subtract)
                    dve.tensor_tensor(out[HD:P, :, 1, :], src[HD:P, :, :], out[0:HD, :, 1, :].bitcast(F32), ALU.subtract)\
                        .then_inc(split[n], 1)

                def lo_v(k, i):
                    dve.wait_ge(v_hi_done, steady(lambda t: t + 1, k, i))
                    dve.tensor_tensor(v_hl[:, k % 2, :, 1, :],
                                      ps[:, banks.bank("v", k), :].rearrange("p (h v) -> p h v", h=DH),
                                      v_hl[:, k % 2, :, 0, :].bitcast(F32), ALU.subtract).then_inc(v_split, 1)

                scale_x(0, None)
                for c in range(KC):
                    dve.wait_ge(w_hi_done, c + 1)
                    dve.scalar_tensor_tensor(w_lo[:, c, :], w_raw[:, c % 4, :], g_col[:, c:c + 1],
                                             w_hi[:, c, :].bitcast(F32), ALU.mult, ALU.subtract).then_inc(w_lo_done, 1)
                turned_lo(0, None)
                for k, i in tiles(dve):
                    if k >= 1:
                        lo_v(k - 1, i)
                    rope_parts(0, k, i)
                    if k >= 1:
                        lo_qk(1, k - 1, i)
                    if k + 1 < TILES:
                        scale_x(k + 1, i)
                    rope_parts(1, k, i)
                    lo_qk(0, k, i)
                    if k + 1 < TILES:
                        turned_lo(k + 1, i)
                lo_v(TILES - 1, None)
                lo_qk(1, TILES - 1, None)

            @block.tensor
            def _(pe):
                def free(k, i, kind, *n):
                    banks.free(pe, read_out, k, i, kind, *n)
                    return banks.bank(kind, k, *n)

                def turn_x(k, i):
                    pe.wait_ge(x_scaled, steady(lambda t: t + 1, k, i))
                    for h in range(2):
                        b = free(k, i, "x", h)
                        for c in range(4):
                            last = pe.transpose(ps[:, b, c * P:(c + 1) * P],
                                                xb[:, k % 2, (4 * h + c) * P:(4 * h + c + 1) * P], ident[:, :])
                        last.then_inc(x_turned, 1)

                def project(n, k, i):
                    q = k % 2
                    b = free(k, i, "qkv"[n])
                    for c in range(KC):
                        if n == 0 and c % 4 == 0:
                            pe.wait_ge(xt_lo_done, steady(lambda t: 2 * t + c // 4 + 1, k, i))
                        if k == 0 and n == 0:
                            pe.wait_ge(w_lo_done, c + 1)
                        for j, (lhs, rhs) in enumerate(((xt_hi, w_hi), (xt_hi, w_lo), (xt_lo, w_hi))):
                            last = pe.matmul(ps[:, b, :], lhs[:, q, c, :], rhs[:, c, n * DW:(n + 1) * DW],
                                             start=(c == 0 and j == 0), stop=(c == KC - 1 and j == 2))
                    last.then_inc(projected[n], 1)

                def turn_qk(n, k, i):
                    pe.wait_ge(roped[n], steady(lambda t: t + 1, k, i))
                    b = free(k, i, ("qT", "kT")[n])
                    for j in range(DH):
                        last = pe.transpose(ps[:, b, j * P:(j + 1) * P], rot[:, n, j * P:(j + 1) * P], ident[:, :])
                    last.then_inc(turned[n], 1)

                pe.wait_ge(consts_made, 2)
                turn_x(0, None)
                for k, i in tiles(pe):
                    project(0, k, i)
                    if k >= 1:
                        turn_qk(1, k - 1, i)
                    project(1, k, i)
                    turn_qk(0, k, i)
                    project(2, k, i)
                    if k + 1 < TILES:
                        turn_x(k + 1, i)
                turn_qk(1, TILES - 1, None)
        m.end()


def attention_plan():
    tiles_in_turn = list(range(1, TILES, 2)) + list(range(TILES - 2, -1, -2))
    chunks = [-(-(t + 1) // 4) for t in tiles_in_turn]

    def front(s):
        for m in range(2):
            for c in range(chunks[s]):
                yield "S", s, m, c
            yield "M", s, m
            for c in range(chunks[s]):
                yield "E", s, m, c
        yield "C", s
        for c in range(chunks[s]):
            yield "A", s, c

    def back(s):
        for c in range(chunks[s]):
            yield "T", s, c
            if c:
                yield "L", s, c - 1
                yield "V", s, c - 1
        yield "L", s, chunks[s] - 1
        yield "V", s, chunks[s] - 1
        yield "O", s

    order = list(front(0))
    for s in range(len(tiles_in_turn)):
        a = list(front(s + 1)) if s + 1 < len(tiles_in_turn) else []
        b = list(back(s))
        merged = sorted([((n + 0.5) / len(a), 0, n, e) for n, e in enumerate(a)] +
                        [((n + 0.5) / len(b), 1, n, e) for n, e in enumerate(b)])
        order += [e for *_, e in merged]
    return tiles_in_turn, chunks, order


def diff_attn(nc, q_s, k_s, v_s, lambdas, mixed):
    tiles_in_turn, chunks, order = attention_plan()
    steps = len(tiles_in_turn)
    ordinal, total = {}, {}
    for e in order:
        ordinal[e] = total[e[0]] = total.get(e[0], 0) + 1
    S_BANKS, T_BANKS, O_BANK, A_SLOTS, Q_SLOTS = range(5), (5, 6), 7, 3, 4
    assert total["S"] % len(S_BANKS) == 0 and total["T"] % len(T_BANKS) == 0

    def width(s, c):
        return min(4, tiles_in_turn[s] + 1 - 4 * c) * P

    with ExitStack() as ctx:
        m_ = Memory(nc, ctx, "da")
        ps = m_.psum()
        keys = m_.sb("keys", [P, DH, 2, S], F32R)
        values = m_.sb("values", [P, DH, TILES, 2 * VD], F32R)
        q_hl = m_.sb("q_hl", [P, Q_SLOTS, 2, P], F32R)
        q_lh = m_.sb("q_lh", [P, Q_SLOTS, 2, P], F32R)
        probs = m_.sb("probs", [P, 2, 2, S])
        at_hi = m_.sb("at_hi", [P, A_SLOTS, 4, P], F32R)
        at_lo = m_.sb("at_lo", [P, A_SLOTS, 4, P], F32R)
        ident = m_.sb("ident", [P, P])
        half = m_.sb("half", [P, 1])
        lam_in = m_.sb("lam_in", [P, 4, HD])
        lam_prod = m_.sb("lam_prod", [P, 2, HD])
        lam_dot = m_.sb("lam_dot", [P, 2])
        neg_lam = m_.sb("neg_lam", [P, 1])
        tops = m_.sb("tops", [P, 2, 2, 4])
        bias = m_.sb("bias", [P, 2, 2])
        sums = m_.sb("sums", [P, 2, 2, 4])
        row_sum = m_.sb("row_sum", [P, 2, 2])
        recip = m_.sb("recip", [P, 2, 2])
        factor = m_.sb("factor", [P, 2])
        o_part = m_.sb("o_part", [P, 2, VD])
        o_row = m_.sb("o_row", [P, 2, VD])
        o_norm = m_.sb("o_norm", [P, 2, VD])
        junk = m_.sb("junk", [P, VD], BF16)
        ss = m_.sb("ss", [P, 2])
        rstd = m_.sb("rstd", [P, 2])

        consts_made, lam_loaded, lam_step = m_.sem("consts_made"), m_.sem("lam_loaded"), m_.sem("lam_step")
        keys_loaded, values_loaded = m_.sem("keys_loaded"), m_.sem("values_loaded")
        q_loaded = [m_.sem(f"q_loaded{n}") for n in range(Q_SLOTS)]
        scored, dve_step, bias_ready, exp_done = (m_.sem(n) for n in ("scored", "dve_step", "bias_ready", "exp_done"))
        combined, turned, hi_done, lo_done, attended = (
            m_.sem(n) for n in ("combined", "turned", "hi_done", "lo_done", "attended"))
        o_copied, o_ready, squared, pool_step, rstd_ready, normed = (
            m_.sem(n) for n in ("o_copied", "o_ready", "squared", "pool_step", "rstd_ready", "normed"))
        stored = [m_.sem(f"stored{n}") for n in range(2)]

        def kind_done(eng, semaphore, h, event):
            eng.wait_ge(semaphore, h * total[event[0]] + ordinal[event])

        def heads(eng, head):
            head(0)
            with eng.Fori(1, DH) as h:
                head(h)

        def slot_left(eng, semaphore, h, kind, turn):
            eng.wait_ge(semaphore, h * total[kind] + max(turn, 0))

        with nc.Block() as block:
            @block.sync
            def _(sp):
                def load_head(h):
                    sp.dma_start(keys[:, bass.ds(h, 1), :, :].bitcast(F32), k_s[:, bass.ds(h, 1), :, :]).then_inc(keys_loaded, 16)
                    sp.dma_start(values[:, bass.ds(h, 1), :, :].bitcast(F32),
                                 v_s[:, bass.ds(h, 1), :, :, :].rearrange("p h t a v -> p h t (a v)")).then_inc(values_loaded, 16)

                def load_q(h, s):
                    slot, t = s % Q_SLOTS, tiles_in_turn[s]
                    src = q_s[t, :, bass.ds(h, 1), :, :].rearrange("p h m n -> p (h m) n")
                    sp.dma_start(q_hl[:, slot, :, :].bitcast(F32), src).then_inc(q_loaded[slot], 16)
                    sp.dma_start(q_lh[0:HD, slot, :, :].bitcast(F32), src[HD:P, :, :]).then_inc(q_loaded[slot], 16)
                    sp.dma_start(q_lh[HD:P, slot, :, :].bitcast(F32), src[0:HD, :, :]).then_inc(q_loaded[slot], 16)

                def head(h, last):
                    for s in range(Q_SLOTS):
                        wait_apart(sp, (lam_loaded, 64), (scored, h * total["S"]))
                        load_q(h, s)
                    if not last:
                        wait_apart(sp, (lam_loaded, 64), (keys_loaded, 16 * h + 16), (values_loaded, 16 * h + 16))
                        load_head(h + 1)
                    for s in range(steps):
                        if s + Q_SLOTS < steps:
                            wait_apart(sp, (lam_loaded, 64), (scored, h * total["S"] + ordinal["S", s, 1, chunks[s] - 1]))
                            load_q(h, s + Q_SLOTS)
                        row = tiles_in_turn[s] * P
                        wait_apart(sp, (lam_loaded, 64), (normed, h * steps + s + 1))
                        sp.dma_start(mixed[row:row + P, bass.ds(h * VD, VD)], o_norm[:, s % 2, :]).then_inc(stored[s % 2], 16)

                for n, vec in enumerate(lambdas):
                    sp.dma_start(lam_in[:, n, :], vec.unsqueeze(0).broadcast_to([P, HD])).then_inc(lam_loaded, 16)
                sp.wait_ge(lam_loaded, 64)
                load_head(0)
                head(0, False)
                with sp.Fori(1, DH - 1) as h:
                    head(h, False)
                head(DH - 1, True)
                for q in stored:
                    sp.wait_ge(q, 16 * DH * steps // 2)

            @block.gpsimd
            def _(pool):
                make_identity(pool, ident, consts_made)
                pool.memset(half[:, :], -0.5).then_inc(consts_made, 1)
                pool.wait_ge(consts_made, 3)

                def head(h):
                    for s in range(steps):
                        q = s % 2
                        wait_apart(pool, (consts_made, 3), (squared, h * steps + s + 1))
                        pool_rstd(pool, rstd[:, q:q + 1], ss[:, q:q + 1], VD, half[:, :], pool_step,
                                  h * steps + s + 1).then_inc(rstd_ready, 1)
                        wait_apart(pool, (consts_made, 3), (rstd_ready, h * steps + s + 1),
                                   (stored[q], 16 * (h * (steps // 2) + s // 2)))
                        pool.tensor_scalar(o_norm[:, q, :], o_row[:, q, :], rstd[:, q:q + 1], 1.0, ALU.mult, ALU.mult)\
                            .then_inc(normed, 1)

                heads(pool, head)

            @block.scalar
            def _(act):
                act.wait_ge(lam_step, 3)
                act.activation(lam_dot[:, :], lam_dot[:, :], ACT.Exp).then_inc(lam_step, 1)

                def head(h):
                    for e in order:
                        what, s = e[0], e[1]
                        q = s % 2
                        if what == "E":
                            m, c = e[2], e[3]
                            w = width(s, c)
                            if c == 0:
                                act.wait_ge(bias_ready, h * 2 * steps + 2 * s + m + 1)
                                if m == 0:
                                    slot_left(act, turned, h, "T", ordinal["T", s - 2, chunks[s - 2] - 1] if s >= 2 else 0)
                            b = S_BANKS[(ordinal["S", s, m, c] - 1) % len(S_BANKS)]
                            act.activation(probs[:, q, m, 4 * P * c:4 * P * c + w], ps[:, b, 0:w], ACT.Exp,
                                           bias=bias[:, q, m:m + 1], accum_out=sums[:, q, m, c:c + 1]).then_inc(exp_done, 1)
                        elif what == "T":
                            n = ordinal[e] - 1
                            kind_done(act, turned, h, e)
                            slot_left(act, attended, h, "V", n + 1 - A_SLOTS)
                            w = width(s, e[2])
                            act.activation(at_hi[:, n % A_SLOTS, 0:w // P, :],
                                           ps[:, T_BANKS[n % 2], 0:w].rearrange("p (j n) -> p j n", n=P), ACT.Copy)\
                                .then_inc(hi_done, 1)
                        elif what == "O":
                            kind_done(act, attended, h, ("V", s, chunks[s] - 1))
                            act.activation(o_part[:, q, :], ps[:, O_BANK, VD:2 * VD], ACT.Copy,
                                           scale=recip[:, q, 0:1]).then_inc(o_copied, 1)
                            act.wait_ge(o_ready, h * steps + s + 1)
                            act.activation(junk[:, :], o_row[:, q, :], ACT.Square, accum_out=ss[:, q:q + 1])\
                                .then_inc(squared, 1)

                heads(act, head)

            @block.vector
            def _(dve):
                dve.wait_ge(lam_loaded, 64)
                dve.tensor_tensor(lam_prod[:, 0, :], lam_in[:, 0, :], lam_in[:, 1, :], ALU.mult).then_inc(lam_step, 1)
                dve.tensor_tensor(lam_prod[:, 1, :], lam_in[:, 2, :], lam_in[:, 3, :], ALU.mult).then_inc(lam_step, 1)
                dve.wait_ge(lam_step, 2)
                dve.tensor_reduce(lam_dot[:, :], lam_prod[:, :, :], AX.X, ALU.add).then_inc(lam_step, 1)
                dve.wait_ge(lam_step, 4)
                dve.scalar_tensor_tensor(neg_lam[:, :], lam_dot[:, 1:2], LAMBDA_INIT, lam_dot[:, 0:1],
                                         ALU.subtract, ALU.subtract).then_inc(lam_step, 1)
                dve.wait_ge(lam_step, 5)
                dve_steps = [0]
                per_head = sum(2 * (1 + (n > 1)) + 2 + (n > 1) for n in chunks)

                def head(h):
                    dve_steps[0] = 0

                    def step(instruction):
                        dve_steps[0] += 1
                        instruction.then_inc(dve_step, 1)
                        dve.wait_ge(dve_step, h * per_head + dve_steps[0])

                    for e in order:
                        what, s = e[0], e[1]
                        q, n_chunks = s % 2, chunks[s]
                        if what == "S":
                            m, c = e[2], e[3]
                            w = width(s, c)
                            b = S_BANKS[(ordinal[e] - 1) % len(S_BANKS)]
                            kind_done(dve, scored, h, e)
                            if c == n_chunks - 1:
                                step(dve.memset(ps[0:HD, b, w - HD:w], NEG))
                            if n_chunks == 1:
                                dve.tensor_reduce(bias[:, q, m:m + 1], ps[:, b, 0:w], AX.X, ALU.max, negate=True)\
                                    .then_inc(bias_ready, 1)
                            else:
                                last_top = dve.tensor_reduce(tops[:, q, m, c:c + 1], ps[:, b, 0:w], AX.X, ALU.max)
                        elif what == "M" and n_chunks > 1:
                            step(last_top)
                            dve.tensor_reduce(bias[:, q, e[2]:e[2] + 1], tops[:, q, e[2], 0:n_chunks], AX.X, ALU.max,
                                              negate=True).then_inc(bias_ready, 1)
                        elif what == "C":
                            kind_done(dve, exp_done, h, ("E", s, 1, n_chunks - 1))
                            total_of = sums[:, q, :, 0:1]
                            if n_chunks > 1:
                                step(dve.tensor_reduce(row_sum[:, q, :], sums[:, q, :, 0:n_chunks], AX.X, ALU.add))
                                total_of = row_sum[:, q, :].unsqueeze(2)
                            step(dve.reciprocal(recip[:, q, :].unsqueeze(2), total_of))
                            step(dve.scalar_tensor_tensor(factor[:, q:q + 1], recip[:, q, 1:2], neg_lam[:, 0:1],
                                                          total_of[:, 0, :], ALU.mult, ALU.mult))
                        elif what == "A":
                            c = e[2]
                            at = slice(4 * P * c, 4 * P * c + width(s, c))
                            dve.scalar_tensor_tensor(probs[:, q, 0, at], probs[:, q, 1, at], factor[:, q:q + 1],
                                                     probs[:, q, 0, at], ALU.mult, ALU.add).then_inc(combined, 1)
                        elif what == "L":
                            n = ordinal["T", s, e[2]] - 1
                            w = width(s, e[2])
                            kind_done(dve, hi_done, h, ("T", s, e[2]))
                            dve.tensor_tensor(at_lo[:, n % A_SLOTS, 0:w // P, :],
                                              ps[:, T_BANKS[n % 2], 0:w].rearrange("p (j n) -> p j n", n=P),
                                              at_hi[:, n % A_SLOTS, 0:w // P, :].bitcast(F32), ALU.subtract)\
                                .then_inc(lo_done, 1)
                        elif what == "O":
                            dve.wait_ge(o_copied, h * steps + s + 1)
                            if s >= 2:
                                dve.wait_ge(normed, h * steps + s - 1)
                            else:
                                dve.wait_ge(normed, h * steps)
                            dve.scalar_tensor_tensor(o_row[:, q, :], ps[:, O_BANK, 0:VD], recip[:, q, 0:1],
                                                     o_part[:, q, :], ALU.mult, ALU.add).then_inc(o_ready, 1)
                    assert dve_steps[0] == per_head, (dve_steps, per_head)

                heads(dve, head)

            @block.tensor
            def _(pe):
                pe.wait_ge(consts_made, 2)

                def head(h):
                    pe.wait_ge(keys_loaded, 16 * h + 16)
                    pe.wait_ge(values_loaded, 16 * h + 16)
                    for e in order:
                        what, s = e[0], e[1]
                        if what == "S":
                            m, c = e[2], e[3]
                            n, w = ordinal[e] - 1, width(s, c)
                            if m == 0 and c == 0:
                                slot_uses = steps // Q_SLOTS
                                pe.wait_ge(q_loaded[s % Q_SLOTS], 48 * (h * slot_uses + s // Q_SLOTS + 1))
                            slot_left(pe, exp_done, h, "S", n + 1 - len(S_BANKS))
                            b = S_BANKS[n % len(S_BANKS)]
                            for j, stack in enumerate((q_hl, q_lh)):
                                last = pe.matmul(ps[:, b, 0:w], stack[:, s % Q_SLOTS, m, :],
                                                 keys[:, bass.ds(h, 1), m, 4 * P * c:4 * P * c + w].squeeze(1),
                                                 start=(j == 0), stop=(j == 1))
                            last.then_inc(scored, 1)
                        elif what == "T":
                            n, w = ordinal[e] - 1, width(s, e[2])
                            kind_done(pe, combined, h, ("A", s, e[2]))
                            slot_left(pe, lo_done, h, "L", n + 1 - len(T_BANKS))
                            for j in range(w // P):
                                at = 4 * P * e[2] + j * P
                                last = pe.transpose(ps[:, T_BANKS[n % 2], j * P:(j + 1) * P],
                                                    probs[:, s % 2, 0, at:at + P], ident[:, :])
                            last.then_inc(turned, 1)
                        elif what == "V":
                            c = e[2]
                            n = ordinal[e] - 1
                            kind_done(pe, lo_done, h, ("L", s, c))
                            if c == 0:
                                pe.wait_ge(o_ready, h * steps + s)
                            for j in range(width(s, c) // P):
                                for i, a in enumerate((at_hi, at_lo)):
                                    last = pe.matmul(ps[:, O_BANK, 0:2 * VD], a[:, n % A_SLOTS, j, :],
                                                     values[:, bass.ds(h, 1), 4 * c + j, :].squeeze(1),
                                                     start=(c == 0 and j == 0 and i == 0),
                                                     stop=(4 * c + j == tiles_in_turn[s] and i == 1))
                            last.then_inc(attended, 1)

                heads(pe, head)
        m_.end()


def out_proj(nc, x, swa_t, mixed, w_out, subln, g_post, g_ffn, x_mid, h_s):
    y_order, t_order = [], [("m", 0)]
    for t in range(TILES + 1):
        if t < TILES:
            y_order += [("y", t, 0), ("y", t, 1)]
        if t + 1 < TILES:
            t_order.append(("m", t + 1))
        if t >= 1:
            t_order += [("h", t - 1, 0), ("h", t - 1, 1)]
    y_banks, t_banks = Banks([0, 1, 2, 3], y_order), Banks([4, 5, 6], t_order)
    SC = QA // P
    HW = D // 2

    with ExitStack() as ctx:
        m = Memory(nc, ctx, "op")
        ps = m.psum()
        w_hi = m.sb("w_hi", [P, KC, D], F32R)
        w_lo = m.sb("w_lo", [P, KC, D], F32R)
        w_raw = m.sb("w_raw", [P, 4, D])
        sub_col = m.sb("sub_col", [P, 1])
        post_row = m.sb("post_row", [P, D])
        ffn_row = m.sb("ffn_row", [P, D])
        ident = m.sb("ident", [P, P])
        half = m.sb("half", [P, 1])
        xb = m.sb("x", [P, 2, D])
        swa_in = m.sb("swa_in", [P, 2, SC, P])
        mix_in = m.sb("mix_in", [P, 2, DW])
        mt_hi = m.sb("mt_hi", [P, 2, KC, P], F32R)
        mt_lo = m.sb("mt_lo", [P, 2, KC, P], F32R)
        y_junk = m.sb("y_junk", [P, D], BF16)
        x_junk = m.sb("x_junk", [P, D], BF16)
        y_ss = m.sb("y_ss", [P, 2, 2])
        y_rstd = m.sb("y_rstd", [P, 2])
        x_ss = m.sb("x_ss", [P, 2])
        x_rstd = m.sb("x_rstd", [P, 2])
        y_norm = m.sb("y_norm", [P, 2, D])
        x_new = m.sb("x_new", [P, 2, D])
        h_row = m.sb("h_row", [P, D])
        ht = m.sb("ht", [P, 2, KC, 2, P], F32R)

        w_loaded = [m.sem(f"w_loaded{n}") for n in range(4)]
        w_hi_done, w_lo_done = m.sem("w_hi_done"), m.sem("w_lo_done")
        consts_loaded, consts_made, sub_scaled = m.sem("consts_loaded"), m.sem("consts_made"), m.sem("sub_scaled")
        in_loaded = [m.sem(f"in_loaded{n}") for n in range(2)]
        x_loaded = [m.sem(f"x_loaded{n}") for n in range(2)]
        m_turned, swa_hi, swa_lo, m_hi, m_lo = (m.sem(n) for n in ("m_turned", "swa_hi", "swa_lo", "m_hi", "m_lo"))
        multiplied, y_squared, y_normed, pool_step, y_rstd_ready = (
            m.sem(n) for n in ("multiplied", "y_squared", "y_normed", "pool_step", "y_rstd_ready"))
        x_added, x_squared, x_rstd_ready, h_ready = (m.sem(n) for n in ("x_added", "x_squared", "x_rstd_ready", "h_ready"))
        h_turned, h_hi, h_lo = (m.sem(n) for n in ("h_turned", "h_hi", "h_lo"))
        x_stored = [m.sem(f"x_stored{n}") for n in range(2)]
        h_stored = [m.sem(f"h_stored{n}") for n in range(2)]
        read_out = {"y": (y_normed, lambda t, n: 2 * t + n + 1), "m": (m_lo, lambda t: t + 1),
                    "h": (h_lo, lambda t, n: 2 * t + n + 1)}

        with nc.Block() as block:
            @block.sync
            def _(sp):
                met = (consts_loaded, 48)

                def load_in(k, i, ahead):
                    p = k % 2
                    at = steady(lambda t: (t + ahead) * P, k, i)
                    sp.dma_start(swa_in[:, p, :, :], swa_t[:, :, bass.ds(at, P)]).then_inc(in_loaded[p], 16)
                    sp.dma_start(mix_in[:, p, :], mixed[bass.ds(at, P), :]).then_inc(in_loaded[p], 16)

                def store_tile(sp, k, i):
                    p = k % 2
                    at = steady(lambda t: t * P, k, i)
                    wait_apart(sp, (consts_loaded, 48), (x_added, steady(lambda t: t + 1, k, i)))
                    sp.dma_start(x_mid[bass.ds(at, P), :], x_new[:, p, :]).then_inc(x_stored[p], 16)
                    wait_apart(sp, (consts_loaded, 48), (h_lo, steady(lambda t: 2 * t + 2, k, i)))
                    sp.dma_start(h_s[:, :, :, bass.ds(at, P)], ht[:, p, :, :, :].bitcast(F32)).then_inc(h_stored[p], 16)

                with nc.allow_non_contiguous_dma(reason="gains by column"):
                    sp.dma_start(sub_col[:, :], subln.rearrange("(c p) -> p c", p=P)).then_inc(consts_loaded, 16)
                for n in range(2):
                    load_in(n, None, 0)
                for c in range(KC):
                    if c >= 4:
                        sp.wait_ge(w_lo_done, c - 3)
                    sp.dma_start(w_raw[:, c % 4, :], w_out[c * P:(c + 1) * P, :]).then_inc(w_loaded[c % 4], 16)
                    if c == 3:
                        sp.dma_start(post_row[:, :], g_post.unsqueeze(0).broadcast_to([P, D])).then_inc(consts_loaded, 16)
                        sp.dma_start(ffn_row[:, :], g_ffn.unsqueeze(0).broadcast_to([P, D])).then_inc(consts_loaded, 16)
                for n in range(2):
                    sp.dma_start(xb[:, n, :], x[n * P:(n + 1) * P, :]).then_inc(x_loaded[n], 16)
                for k, i in tiles(sp):
                    p = k % 2
                    if k + 2 < TILES:
                        wait_apart(sp, met, (swa_lo, steady(lambda t: t + 1, k, i)), (m_turned, steady(lambda t: t + 1, k, i)))
                        load_in(k, i, 2)
                    if k >= 1:
                        store_tile(sp, k - 1, i)
                        if k + 1 < TILES:
                            at = steady(lambda t: (t + 1) * P, k, i)
                            sp.dma_start(xb[:, 1 - p, :], x[bass.ds(at, P), :]).then_inc(x_loaded[1 - p], 16)
                store_tile(sp, TILES - 1, None)
                for s in x_stored + h_stored:
                    sp.wait_ge(s, 16 * TILES // 2)

            @block.gpsimd
            def _(pool):
                make_identity(pool, ident, consts_made)
                pool.memset(half[:, :], -0.5).then_inc(consts_made, 1)
                pool.wait_ge(consts_made, 3)

                def split_swa(k, i):
                    q = k % 2
                    pool.wait_ge(swa_hi, steady(lambda t: t + 1, k, i))
                    pool.tensor_tensor(mt_lo[:, q, 0:SC, :], swa_in[:, q, :, :], mt_hi[:, q, 0:SC, :].bitcast(F32),
                                       ALU.subtract).then_inc(swa_lo, 1)

                def y_rstd_of(k, i):
                    q = k % 2
                    pool.wait_ge(y_squared, steady(lambda t: 2 * t + 2, k, i))
                    if k >= 2:
                        pool.wait_ge(y_normed, steady(lambda t: 2 * t - 2, k, i))
                    pool.tensor_tensor(y_rstd[:, q:q + 1], y_ss[:, q, 0:1], y_ss[:, q, 1:2], ALU.add).then_inc(pool_step, 1)
                    wait_apart(pool, (consts_made, 3), (pool_step, steady(lambda t: 3 * t + 1, k, i)))
                    pool_rstd(pool, y_rstd[:, q:q + 1], y_rstd[:, q:q + 1], D, half[:, :], pool_step,
                              steady(lambda t: 3 * t + 2, k, i)).then_inc(y_rstd_ready, 1)

                def add_x(k, i):
                    q = k % 2
                    pool.wait_ge(x_loaded[q], steady(lambda t: 16 * (t // 2 + 1), k, i))
                    if k >= 2:
                        pool.wait_ge(x_stored[q], steady(lambda t: 16 * (t // 2), k, i))
                        pool.wait_ge(h_ready, steady(lambda t: t - 1, k, i))
                    pool.wait_ge(y_normed, steady(lambda t: 2 * t + 2, k, i))
                    pool.tensor_tensor(x_new[:, q, :], y_norm[:, q, :], xb[:, q, :], ALU.add).then_inc(x_added, 1)

                def x_rstd_of(k, i):
                    q = k % 2
                    waits = [(x_squared, steady(lambda t: t + 1, k, i))]
                    if k >= 2:
                        waits.append((h_ready, steady(lambda t: t - 1, k, i)))
                    wait_apart(pool, (consts_made, 3), *waits)
                    pool_rstd(pool, x_rstd[:, q:q + 1], x_ss[:, q:q + 1], D, half[:, :], pool_step,
                              steady(lambda t: 3 * t + 3, k, i)).then_inc(x_rstd_ready, 1)

                split_swa(0, None)
                for k, i in tiles(pool):
                    if k >= 1:
                        y_rstd_of(k - 1, i)
                        add_x(k - 1, i)
                    if k + 1 < TILES:
                        split_swa(k + 1, i)
                    if k >= 1:
                        x_rstd_of(k - 1, i)
                y_rstd_of(TILES - 1, None)
                add_x(TILES - 1, None)
                x_rstd_of(TILES - 1, None)

            @block.scalar
            def _(act):
                def hi_m(k, i):
                    q = k % 2
                    act.wait_ge(in_loaded[q], steady(lambda t: 32 * (t // 2 + 1), k, i))
                    if k >= 2:
                        act.wait_ge(multiplied, steady(lambda t: 2 * t - 2, k, i))
                    act.activation(mt_hi[:, q, 0:SC, :], swa_in[:, q, :, :], ACT.Copy).then_inc(swa_hi, 1)
                    act.wait_ge(m_turned, steady(lambda t: t + 1, k, i))
                    act.activation(mt_hi[:, q, SC:KC, :], ps[:, t_banks.bank("m", k), :].rearrange("p (c n) -> p c n", n=P),
                                   ACT.Copy).then_inc(m_hi, 1)

                def square_y(k, i):
                    q = k % 2
                    for n in range(2):
                        act.wait_ge(multiplied, steady(lambda t: 2 * t + n + 1, k, i))
                        if k >= 1 and n == 0:
                            act.wait_ge(y_rstd_ready, steady(lambda t: t, k, i))
                        act.activation(y_junk[:, n * HW:(n + 1) * HW], ps[:, y_banks.bank("y", k, n), :], ACT.Square,
                                       accum_out=y_ss[:, q, n:n + 1]).then_inc(y_squared, 1)

                def square_x(k, i):
                    q = k % 2
                    act.wait_ge(x_added, steady(lambda t: t + 1, k, i))
                    if k >= 1:
                        act.wait_ge(x_rstd_ready, steady(lambda t: t, k, i))
                    act.activation(x_junk[:, :], x_new[:, q, :], ACT.Square, accum_out=x_ss[:, q:q + 1]).then_inc(x_squared, 1)

                def hi_h(k, i):
                    q = k % 2
                    for n in range(2):
                        act.wait_ge(h_turned, steady(lambda t: 2 * t + n + 1, k, i))
                        if k >= 2 and n == 0:
                            act.wait_ge(h_stored[q], steady(lambda t: 16 * (t // 2), k, i))
                        act.activation(ht[:, q, 4 * n:4 * n + 4, 0, :],
                                       ps[:, t_banks.bank("h", k, n), :].rearrange("p (c n) -> p c n", n=P), ACT.Copy)\
                            .then_inc(h_hi, 1)

                act.wait_ge(consts_loaded, 48)
                act.wait_ge(sub_scaled, 1)
                hi_m(0, None)
                for c in range(KC):
                    act.wait_ge(w_loaded[c % 4], 16 * (c // 4 + 1))
                    act.activation(w_hi[:, c, :], w_raw[:, c % 4, :], ACT.Copy, scale=1.0 if c < SC else sub_col[:, 0:1])\
                        .then_inc(w_hi_done, 1)
                for k, i in tiles(act):
                    if k >= 1:
                        square_y(k - 1, i)
                    if k + 1 < TILES:
                        hi_m(k + 1, i)
                    if k >= 1:
                        square_x(k - 1, i)
                        hi_h(k - 1, i)
                square_y(TILES - 1, None)
                square_x(TILES - 1, None)
                hi_h(TILES - 1, None)

            @block.vector
            def _(dve):
                def lo_m(k, i):
                    q = k % 2
                    dve.wait_ge(m_hi, steady(lambda t: t + 1, k, i))
                    dve.tensor_tensor(mt_lo[:, q, SC:KC, :], ps[:, t_banks.bank("m", k), :].rearrange("p (c n) -> p c n", n=P),
                                      mt_hi[:, q, SC:KC, :].bitcast(F32), ALU.subtract).then_inc(m_lo, 1)

                def norm_y(k, i):
                    q = k % 2
                    dve.wait_ge(y_rstd_ready, steady(lambda t: t + 1, k, i))
                    if k >= 2:
                        dve.wait_ge(x_added, steady(lambda t: t - 1, k, i))
                    for n in range(2):
                        at = slice(n * HW, (n + 1) * HW)
                        dve.scalar_tensor_tensor(y_norm[:, q, at], ps[:, y_banks.bank("y", k, n), :], y_rstd[:, q:q + 1],
                                                 post_row[:, at], ALU.mult, ALU.mult).then_inc(y_normed, 1)

                def norm_x(k, i):
                    q = k % 2
                    dve.wait_ge(x_rstd_ready, steady(lambda t: t + 1, k, i))
                    if k >= 1:
                        dve.wait_ge(h_turned, steady(lambda t: 2 * t, k, i))
                    dve.scalar_tensor_tensor(h_row[:, :], x_new[:, q, :], x_rstd[:, q:q + 1], ffn_row[:, :],
                                             ALU.mult, ALU.mult).then_inc(h_ready, 1)

                def lo_h(k, i):
                    q = k % 2
                    for n in range(2):
                        dve.wait_ge(h_hi, steady(lambda t: 2 * t + n + 1, k, i))
                        dve.tensor_tensor(ht[:, q, 4 * n:4 * n + 4, 1, :],
                                          ps[:, t_banks.bank("h", k, n), :].rearrange("p (c n) -> p c n", n=P),
                                          ht[:, q, 4 * n:4 * n + 4, 0, :].bitcast(F32), ALU.subtract).then_inc(h_lo, 1)

                dve.wait_ge(consts_loaded, 48)
                dve.tensor_scalar(sub_col[:, :], sub_col[:, :], 1.0 - LAMBDA_INIT, None, ALU.mult).then_inc(sub_scaled, 1)
                dve.wait_ge(sub_scaled, 1)
                lo_m(0, None)
                for c in range(KC):
                    dve.wait_ge(w_hi_done, c + 1)
                    dve.scalar_tensor_tensor(w_lo[:, c, :], w_raw[:, c % 4, :], 1.0 if c < SC else sub_col[:, 0:1],
                                             w_hi[:, c, :].bitcast(F32), ALU.mult, ALU.subtract).then_inc(w_lo_done, 1)
                for k, i in tiles(dve):
                    if k >= 1:
                        norm_y(k - 1, i)
                    if k + 1 < TILES:
                        lo_m(k + 1, i)
                    if k >= 1:
                        norm_x(k - 1, i)
                        lo_h(k - 1, i)
                norm_y(TILES - 1, None)
                norm_x(TILES - 1, None)
                lo_h(TILES - 1, None)

            @block.tensor
            def _(pe):
                def turn_m(k, i):
                    pe.wait_ge(in_loaded[k % 2], steady(lambda t: 32 * (t // 2 + 1), k, i))
                    t_banks.free(pe, read_out, k, i, "m")
                    for j in range(DW // P):
                        last = pe.transpose(ps[:, t_banks.bank("m", k), j * P:(j + 1) * P],
                                            mix_in[:, k % 2, j * P:(j + 1) * P], ident[:, :])
                    last.then_inc(m_turned, 1)

                def multiply(n, k, i):
                    q = k % 2
                    if n == 0:
                        pe.wait_ge(swa_lo, steady(lambda t: t + 1, k, i))
                    y_banks.free(pe, read_out, k, i, "y", n)
                    for c in range(KC):
                        if n == 0 and c == SC:
                            pe.wait_ge(m_lo, steady(lambda t: t + 1, k, i))
                        if k == 0 and n == 0:
                            pe.wait_ge(w_lo_done, c + 1)
                        for j, (lhs, rhs) in enumerate(((mt_hi, w_hi), (mt_hi, w_lo), (mt_lo, w_hi))):
                            last = pe.matmul(ps[:, y_banks.bank("y", k, n), :], lhs[:, q, c, :],
                                             rhs[:, c, n * HW:(n + 1) * HW],
                                             start=(c == 0 and j == 0), stop=(c == KC - 1 and j == 2))
                    last.then_inc(multiplied, 1)

                def turn_h(k, i):
                    pe.wait_ge(h_ready, steady(lambda t: t + 1, k, i))
                    for n in range(2):
                        t_banks.free(pe, read_out, k, i, "h", n)
                        for j in range(4):
                            at = (4 * n + j) * P
                            last = pe.transpose(ps[:, t_banks.bank("h", k, n), j * P:(j + 1) * P], h_row[:, at:at + P],
                                                ident[:, :])
                        last.then_inc(h_turned, 1)

                pe.wait_ge(consts_made, 2)
                turn_m(0, None)
                for k, i in tiles(pe):
                    multiply(0, k, i)
                    if k + 1 < TILES:
                        turn_m(k + 1, i)
                    multiply(1, k, i)
                    if k >= 1:
                        turn_h(k - 1, i)
                turn_h(TILES - 1, None)
        m.end()


def ffn(nc, h_s, x_mid, w_gate, w_up, w_down, g_post, out):
    HW = D // 2
    UP = 2 * FC
    DOWN = FC
    UNITS = UP + DOWN
    R = 4
    slot_uses = [len(range(s, UNITS, R)) for s in range(R)]
    ENDS = (UP + DOWN // 2 - 1, UNITS - 1)
    USED = UNITS - len(ENDS)

    with ExitStack() as ctx:
        m = Memory(nc, ctx, "ff")
        ps = m.psum()
        h_hl = m.sb("h_hl", [P, KC, 2, TB], F32R)
        g_hi = m.sb("g_hi", [P, FC, TB], F32R)
        g_lo = m.sb("g_lo", [P, FC, TB], F32R)
        w_raw = m.sb("w_raw", [P, R, D])
        w_hi = m.sb("w_hi", [P, R, D], F32R)
        w_lo = m.sb("w_lo", [P, R, D], F32R)
        y = m.sb("y", [P, BT, D])
        xm = m.sb("xm", [P, D])
        post_row = m.sb("post_row", [P, D])
        silu = m.sb("silu", [P, 2, TB])
        gated = m.sb("gated", [P, 2, TB])
        junk = m.sb("junk", [P, BT, HW], BF16)
        half = m.sb("half", [P, BT])
        ss = m.sb("ss", [P, 2, BT])
        rstd = m.sb("rstd", [P, BT])

        consts_made, post_loaded = m.sem("consts_made"), m.sem("post_loaded")
        h_loaded = m.sem("h_loaded")
        w_loaded = [m.sem(f"w_loaded{n}") for n in range(R)]
        w_hi_done, w_split, unit_used = m.sem("w_hi_done"), m.sem("w_split"), m.sem("unit_used")
        silu_done, gate_done, g_hi_done, g_split = (m.sem(n) for n in ("silu_done", "gate_done", "g_hi_done", "g_split"))
        y_done, y_squared, y_copied = m.sem("y_done"), m.sem("y_squared"), m.sem("y_copied")
        pool_step, rstd_ready, y_normed = m.sem("pool_step"), m.sem("rstd_ready"), m.sem("y_normed")
        xm_loaded, x_added, stored = m.sem("xm_loaded"), m.sem("x_added"), m.sem("stored")

        def used(b, u):
            if u in ENDS:
                return y_done, (b * 2 + ENDS.index(u) + 1) * BT
            return unit_used, b * USED + u + 1 - sum(e < u for e in ENDS)

        def blocks(eng, body):
            body(0, True, False)
            with eng.Fori(1, BLOCKS - 1) as b:
                body(b, False, False)
            body(BLOCKS - 1, False, True)

        def pairs(eng, body):
            body(0, True)
            with eng.Fori(1, FC // 2) as j:
                body(j, False)

        with nc.Block() as block:
            @block.sync
            def _(sp):
                met = (post_loaded, 16)

                def load_h(b):
                    sp.dma_start(h_hl[:, :, :, :].bitcast(F32), h_s[:, :, :, bass.ds(b * TB, TB)]).then_inc(h_loaded, 16)

                def body(b, first, last):
                    def up_pair(j, peeled):
                        for u in range(4):
                            w = (w_gate, w_up)[u % 2]
                            wait_apart(sp, met, (w_split, b * UNITS if peeled else b * UNITS + 4 * j + u - R + 1))
                            sp.dma_start(w_raw[:, u, :], w[bass.ds(2 * j + u // 2, 1), :, :].rearrange("f p n -> p (f n)"))\
                                .then_inc(w_loaded[u], 16)

                    pairs(sp, up_pair)
                    for d in range(DOWN):
                        u = UP + d
                        wait_apart(sp, met, (w_split, b * UNITS + u - R + 1))
                        sp.dma_start(w_raw[:, u % R, :], w_down[d // (FC // 2), d % (FC // 2), :, :])\
                            .then_inc(w_loaded[u % R], 16)
                        if d == R + 2 and not last:
                            wait_apart(sp, met, (unit_used, b * USED + UP))
                            load_h(b + 1)

                sp.dma_start(post_row[:, :], g_post.unsqueeze(0).broadcast_to([P, D])).then_inc(post_loaded, 16)
                load_h(0)
                sp.wait_ge(post_loaded, 16)
                blocks(sp, body)

            @block.gpsimd
            def _(pool):
                met = (consts_made, 1)
                pool.memset(half[:, :], -0.5).then_inc(consts_made, 1)
                pool.wait_ge(*met)
                pool.memset(junk[:, 0, 0:1], 0.0).then_inc(g_split, 1)

                def body(b, first, last):
                    def split_g(f, q):
                        wait_apart(pool, met, (g_hi_done, b * FC + f + 1))
                        pool.tensor_tensor(g_lo[:, bass.ds(f, 1), :].squeeze(1), gated[:, q, :],
                                           g_hi[:, bass.ds(f, 1), :].squeeze(1).bitcast(F32), ALU.subtract).then_inc(g_split, 1)

                    with pool.Fori(0, FC // 2) as j:
                        for q in range(2):
                            split_g(2 * j + q, q)
                    pool.wait_ge(y_squared, (b + 1) * 2 * BT)
                    if not first:
                        pool.wait_ge(y_normed, b * BT)
                    pool.tensor_tensor(rstd[:, :], ss[:, 0, :], ss[:, 1, :], ALU.add).then_inc(pool_step, 1)
                    wait_apart(pool, met, (pool_step, 2 * b + 1))
                    pool_rstd(pool, rstd[:, :], rstd[:, :], D, half[:, :], pool_step, 2 * b + 2).then_inc(rstd_ready, 1)
                    for j in range(BT):
                        row = b * TB + j * P
                        wait_apart(pool, met, (x_added, b * BT + j))
                        pool.dma_start(xm[:, :], x_mid[bass.ds(row, P), :]).then_inc(xm_loaded, 16)
                        pool.wait_ge(xm_loaded, 16 * (b * BT + j + 1))
                        pool.wait_ge(y_normed, b * BT + j + 1)
                        pool.tensor_tensor(y[:, j, :], y[:, j, :], xm[:, :], ALU.add).then_inc(x_added, 1)
                        wait_apart(pool, met, (x_added, b * BT + j + 1))
                        pool.dma_start(out[bass.ds(row, P), :], y[:, j, :]).then_inc(stored, 16)

                blocks(pool, body)
                pool.wait_ge(stored, 16 * TILES)

            @block.scalar
            def _(act):
                def hi_unit(b, slot, turn, semaphore, count):
                    act.wait_ge(w_loaded[slot], 16 * (b * slot_uses[slot] + turn + 1))
                    act.wait_ge(semaphore, count)
                    act.activation(w_hi[:, slot, :], w_raw[:, slot, :], ACT.Copy).then_inc(w_hi_done, 1)

                def silu_of(b, f, q):
                    act.wait_ge(unit_used, b * USED + 2 * f + 1)
                    act.activation(silu[:, q, :], ps[:, 2 * q, :], ACT.Silu).then_inc(silu_done, 1)
                    wait_apart(act, (post_loaded, 16), (gate_done, b * FC + f + 1), (y_done, b * 2 * BT))
                    act.activation(g_hi[:, bass.ds(f, 1), :].squeeze(1), gated[:, q, :], ACT.Copy).then_inc(g_hi_done, 1)

                def square(b, n):
                    for j in range(BT):
                        act.wait_ge(y_done, b * 2 * BT + n * BT + j + 1)
                        if j == 0:
                            act.wait_ge(y_squared, (b * 2 + n) * BT)
                            if n == 0:
                                act.wait_ge(rstd_ready, b)
                        act.activation(junk[:, j, :], ps[:, (4 if n == 0 else 0) + j, :], ACT.Square,
                                       accum_out=ss[:, n, j:j + 1]).then_inc(y_squared, 1)

                def body(b, first, last):
                    def up_pair(j, peeled):
                        for u in range(4):
                            if not peeled:
                                hi_unit(b, u, j, unit_used, b * USED + 4 * j + u - R + 1)
                            elif u > 0:
                                hi_unit(b, u, j, y_done, b * 2 * BT)
                            if u % 2 == 1 and not peeled:
                                silu_of(b, 2 * j - 2 + u // 2, u // 2)

                    pairs(act, up_pair)
                    for d in range(DOWN):
                        u = UP + d
                        hi_unit(b, u % R, u // R, *used(b, u - R))
                        if d in (1, 3):
                            silu_of(b, FC - 2 + d // 2, d // 2)
                        if d == FC // 2 + R - 1:
                            square(b, 0)
                    if not last:
                        hi_unit(b + 1, 0, 0, *used(b, UNITS - 2))
                    square(b, 1)

                act.wait_ge(post_loaded, 16)
                act.wait_ge(w_loaded[0], 16)
                act.activation(w_hi[:, 0, :], w_raw[:, 0, :], ACT.Copy).then_inc(w_hi_done, 1)
                blocks(act, body)

            @block.vector
            def _(dve):
                def split_unit(slot, count):
                    dve.wait_ge(w_hi_done, count)
                    dve.tensor_tensor(w_lo[:, slot, :], w_raw[:, slot, :], w_hi[:, slot, :].bitcast(F32), ALU.subtract)\
                        .then_inc(w_split, 1)

                def gate(b, f, q):
                    dve.wait_ge(silu_done, b * FC + f + 1)
                    dve.wait_ge(unit_used, b * USED + 2 * f + 2)
                    dve.wait_ge(g_split, b * FC + f - q + 1)
                    dve.tensor_tensor(gated[:, q, :], silu[:, q, :], ps[:, 2 * q + 1, :], ALU.mult).then_inc(gate_done, 1)

                def copy_y(b, n):
                    for j in range(BT):
                        dve.wait_ge(y_squared, b * 2 * BT + n * BT + j + 1)
                        if n == 0 and j == 0:
                            dve.wait_ge(stored, 16 * BT * b)
                        dve.tensor_copy(y[:, j, n * HW:(n + 1) * HW], ps[:, (4 if n == 0 else 0) + j, :]).then_inc(y_copied, 1)

                def norm_y(b, j):
                    if j == 0:
                        dve.wait_ge(rstd_ready, b + 1)
                        dve.wait_ge(y_copied, (b + 1) * 2 * BT)
                    dve.scalar_tensor_tensor(y[:, j, :], y[:, j, :], rstd[:, j:j + 1], post_row[:, :], ALU.mult, ALU.mult)\
                        .then_inc(y_normed, 1)

                def body(b, first, last):
                    def up_pair(j, peeled):
                        for u in range(4):
                            if not (peeled and u == 0):
                                split_unit(u, b * UNITS + 4 * j + u + 1)
                            if u % 2 == 1 and not peeled:
                                gate(b, 2 * j - 2 + u // 2, u // 2)
                            if peeled and not first:
                                norm_y(b - 1, u)

                    pairs(dve, up_pair)
                    for d in range(DOWN):
                        u = UP + d
                        split_unit(u % R, b * UNITS + u + 1)
                        if d in (1, 3):
                            gate(b, FC - 2 + d // 2, d // 2)
                        if d == FC // 2 + R - 1:
                            copy_y(b, 0)
                    if not last:
                        split_unit(0, (b + 1) * UNITS + 1)
                    copy_y(b, 1)

                dve.wait_ge(post_loaded, 16)
                split_unit(0, 1)
                blocks(dve, body)
                for j in range(BT):
                    norm_y(BLOCKS - 1, j)

            @block.tensor
            def _(pe):
                def multiply_up(b, j, u, peeled):
                    pe.wait_ge(w_split, b * UNITS + 4 * j + u + 1)
                    if peeled:
                        pe.wait_ge(y_copied, b * 2 * BT)
                    else:
                        pe.wait_ge(gate_done, b * FC + 2 * j + u // 2 - 1)
                    for c in range(KC):
                        at = slice(c * P, (c + 1) * P)
                        for n, (w, a) in enumerate(((w_hi, 0), (w_hi, 1), (w_lo, 0))):
                            last = pe.matmul(ps[:, u, :], w[:, u, at], h_hl[:, c, a, :],
                                             start=(c == 0 and n == 0), stop=(c == KC - 1 and n == 2))
                    last.then_inc(unit_used, 1)

                pe.wait_ge(post_loaded, 16)

                def body(b, first, last):
                    pe.wait_ge(h_loaded, 16 * (b + 1))

                    def up_pair(j, peeled):
                        for u in range(4):
                            multiply_up(b, j, u, peeled)

                    pairs(pe, up_pair)
                    for d in range(DOWN):
                        u = UP + d
                        n, pair = d // (FC // 2), d % (FC // 2)
                        pe.wait_ge(w_split, b * UNITS + u + 1)
                        if pair == 0:
                            if n == 0:
                                pe.wait_ge(y_copied, b * 2 * BT)
                            else:
                                pe.wait_ge(gate_done, (b + 1) * FC)
                        if n == 0:
                            pe.wait_ge(g_split, b * FC + 2 * pair + 2 + 1)
                        for j in range(BT):
                            bank = (4 if n == 0 else 0) + j
                            for e in range(2):
                                f = 2 * pair + e
                                rhs = slice(e * HW, (e + 1) * HW)
                                for i, (g, w) in enumerate(((g_hi, w_hi), (g_hi, w_lo), (g_lo, w_hi))):
                                    last = pe.matmul(ps[:, bank, :], g[:, f, j * P:(j + 1) * P], w[:, u % R, rhs],
                                                     start=(f == 0 and i == 0), stop=(f == FC - 1 and i == 2))
                            if pair == FC // 2 - 1:
                                last.then_inc(y_done, 1)
                        if pair < FC // 2 - 1:
                            last.then_inc(unit_used, 1)

                blocks(pe, body)
        m.end()


def hybrid_block(nc, x, w_in, sinks, lambda_q1, lambda_k1, lambda_q2, lambda_k2, subln, w_out, g_mix_pre, g_mix_post,
                 g_ffn_pre, g_ffn_post, w_gate, w_up, w_down, rope, out):
    def scratch(name, shape):
        return nc.dram_tensor(name, shape, F32, kind="Internal").ap()

    swa_t = scratch("swa_t", (P, QA // P, S))
    q_s = scratch("q_s", (TILES, P, DH, 2, P))
    k_s = scratch("k_s", (P, DH, 2, S))
    v_s = scratch("v_s", (P, DH, TILES, 2, P))
    mixed = scratch("mixed", (S, DW))
    x_mid = scratch("x_mid", (S, D))
    h_s = scratch("h_s", (P, KC, 2, S))
    swa_phase(nc, x, w_in, g_mix_pre, sinks, rope, swa_t)
    diff_proj(nc, x, w_in, g_mix_pre, rope, q_s, k_s, v_s)
    diff_attn(nc, q_s, k_s, v_s, [lambda_q1, lambda_k1, lambda_q2, lambda_k2], mixed)
    out_proj(nc, x, swa_t, mixed, w_out, subln, g_mix_post, g_ffn_pre, x_mid, h_s)
    ffn(nc, h_s, x_mid, w_gate, w_up, w_down, g_ffn_post, out)


def rope_table():
    inv = 1.0 / (10000.0 ** (np.arange(0, HD, 2, dtype=np.float32) / HD))
    angle = np.arange(S, dtype=np.float32)[:, None] * inv.astype(np.float32)[None, :]
    cos, sin = np.cos(angle), np.sin(angle)
    table = np.concatenate([cos, cos, -sin, sin], axis=1).astype(np.float32)
    return np.concatenate([table, table * np.float32(SCALE)], axis=1)


_INS = ['x', 'w_in', 'swa_sinks', 'diff_lambda_q1', 'diff_lambda_k1', 'diff_lambda_q2', 'diff_lambda_k2', 'diff_subln',
        'w_out', 'norm_mix_pre', 'norm_mix_post', 'norm_ffn_pre', 'norm_ffn_post', 'w_gate', 'w_up', 'w_down']


def kernel(**inputs):
    import numpy as _np
    import concourse.bacc as _bacc
    from concourse import mybir as _mybir
    from concourse.bass_utils import run_bass_kernel_spmd as _run

    laid_out = {name: _np.asarray(inputs[name])[0] for name in _INS}
    for name in ('w_gate', 'w_up'):
        laid_out[name] = laid_out[name].reshape(KC, P, FC, P).transpose(2, 1, 0, 3).reshape(FC, P, D)
    laid_out['w_down'] = laid_out['w_down'].reshape(FC // 2, 2, P, 2, D // 2).transpose(3, 0, 2, 1, 4)\
        .reshape(2, FC // 2, P, D)
    laid_out['rope'] = rope_table()

    nc = _bacc.Bacc("TRN2", target_bir_lowering=False, num_devices=1)
    arrays, args = {}, []
    for name in _INS + ['rope']:
        a = _np.ascontiguousarray(laid_out[name])
        arrays[f"in_{name}_dram"] = a
        args.append(nc.dram_tensor(f"in_{name}_dram", a.shape, _mybir.dt.from_np(a.dtype), kind="ExternalInput").ap())
    args.append(nc.dram_tensor("out_0_dram", (S, D), _mybir.dt.float32, kind="ExternalOutput").ap())
    hybrid_block(nc, *args)
    r = _run(nc, [arrays], core_ids=[0])
    return r.results[0]["out_0_dram"].reshape(1, S, D)
```

```python
from contextlib import ExitStack

import numpy as np

import concourse.bass as bass
from concourse import mybir

F32 = mybir.dt.float32
F32R = mybir.dt.float32r
BF16 = mybir.dt.bfloat16
ALU = mybir.AluOpType
ACT = mybir.ActivationFunctionType
AX = mybir.AxisListType

P = 128
S = 2048
D = 1024
TILES = S // P
KC = D // P
HD = 64
EPS = 1e-6
NEG = -1e30
SCALE = HD ** -0.5
QA = 512
KV = 128
WA = QA + 2 * KV
SH = QA // HD
SG = KV // HD
DW = 512
DH = 4
WB = 3 * DW
VD = 2 * HD
LAMBDA_INIT = 0.8 - 0.6
DF = 2816
FC = DF // P
TB = 512
BLOCKS = S // TB
BT = TB // P


def steady(count, k, i):
    return count(k) if i is None else (count(k + 2) - count(k)) * i + (3 * count(k) - 2 * count(k + 2))


def tiles(eng):
    for k in range(4):
        yield k, None
    with eng.Fori(2, TILES // 2 - 1) as i:
        yield 4, i
        yield 5, i
    yield TILES - 2, None
    yield TILES - 1, None


class Banks:

    def __init__(self, banks, keys):
        self.keys = keys
        self.place = {key: n for n, key in enumerate(keys)}
        self.banks = banks

    def bank(self, *key):
        return self.banks[self.place[key] % len(self.banks)]

    def free(self, pe, read_out, k, i, kind, *n):
        back = self.place[(kind, k, *n)] - len(self.banks)
        if back >= 0:
            what, tile, *rest = self.keys[back]
            semaphore, count = read_out[what]
            pe.wait_ge(semaphore, steady(lambda t: count(t, *rest), tile, i))


class Memory:

    def __init__(self, nc, ctx, phase):
        self.nc, self.ctx, self.phase = nc, ctx, phase
        self.semaphores = []

    def sb(self, name, shape, dt=F32):
        return self.ctx.enter_context(self.nc.sbuf_tensor(f"{self.phase}_{name}", shape, dt))

    def psum(self):
        return self.ctx.enter_context(self.nc.psum_tensor(f"{self.phase}_psum", [P, 8, 512], F32))

    def sem(self, name):
        self.semaphores.append(self.nc.alloc_semaphore(name=f"{self.phase}_{name}"))
        return self.semaphores[-1]

    def end(self):
        self.nc.clear_and_free_semaphores(self.semaphores)
        self.nc.all_engine_barrier()


def wait_apart(eng, met, *waits):
    values = [value if isinstance(value, int) else eng.snap(eng.to_reg(value)) for _, value in waits]
    eng.wait_ge(*met)
    for (semaphore, _), value in zip(waits, values):
        eng.wait_ge(semaphore, value)


def make_identity(pool, ident, step):
    pool.memset(ident[:, :], 0.0).then_inc(step, 1)
    pool.wait_ge(step, 1)
    pool.affine_select(out=ident[:, :], in_=ident[:, :], compare_op=ALU.not_equal, fill=1.0, base=0,
                       pattern=[[-1, P]], channel_multiplier=1).then_inc(step, 1)


def pool_rstd(pool, out, total, width, half, step, done):
    pool.tensor_scalar(out, total, 1.0 / width, EPS, ALU.mult, ALU.add).then_inc(step, 1)
    pool.wait_ge(step, done)
    return pool.tensor_tensor(out, out, half, ALU.pow)


def swa_phase(nc, x, w_in, g_pre, sinks, rope, swa_t):
    order = [("x", 0, 0), ("x", 0, 1)]
    for t in range(TILES + 1):
        if t < TILES:
            order.append(("q", t))
        if t >= 1:
            order += [("s", t - 1, j) for j in range(4)]
        if t < TILES:
            order.append(("kv", t))
        if t + 1 < TILES:
            order += [("x", t + 1, 0), ("x", t + 1, 1)]
        if t < TILES:
            order += [("qT", t), ("kT", t)]
        if t >= 1:
            order += [("a", t - 1, j) for j in range(4)] + [("o", t - 1, u) for u in range(SG)]
    banks = Banks(list(range(8)), order)

    with ExitStack() as ctx:
        m = Memory(nc, ctx, "swa")
        ps = m.psum()
        w_hi = m.sb("w_hi", [P, KC, WA], F32R)
        w_lo = m.sb("w_lo", [P, KC, WA], F32R)
        w_raw = m.sb("w_raw", [P, 4, WA])
        g_col = m.sb("g_col", [P, KC])
        rope_sb = m.sb("rope", [P, TILES, 4 * HD])
        ident = m.sb("ident", [P, P])
        half = m.sb("half", [P, 1])
        sink = m.sb("sink", [P, SH])
        xb = m.sb("x", [P, 2, D])
        junk = m.sb("junk", [P, D], BF16)
        ss = m.sb("ss", [P, 2])
        rstd = m.sb("rstd", [P, 2])
        xt_hi = m.sb("xt_hi", [P, 2, KC, P], F32R)
        xt_lo = m.sb("xt_lo", [P, 2, KC, P], F32R)
        rot_c = m.sb("rot_c", [P, QA])
        rot_s = m.sb("rot_s", [P, QA])
        rot_q = m.sb("rot_q", [P, QA])
        rot_kc = m.sb("rot_kc", [P, KV])
        rot_ks = m.sb("rot_ks", [P, KV])
        rot_k = m.sb("rot_k", [P, KV])
        v_raw = m.sb("v_raw", [P, 2, KV])
        q_hl = m.sb("q_hl", [P, SH // 2, 2, P], F32R)
        q_lh = m.sb("q_lh", [P, SH // 2, 2, P], F32R)
        k_hl = m.sb("k_hl", [P, SG, 2, P], F32R)
        v_hl = m.sb("v_hl", [P, 2, SG, 2 * HD], F32R)
        top = m.sb("top", [P, 2, SH])
        bias = m.sb("bias", [P, 2, SH])
        gap = m.sb("gap", [P, 2, SH])
        sums = m.sb("sums", [P, 2, SH])
        recip = m.sb("recip", [P, 2, SH])
        probs = m.sb("probs", [P, 2, SH, 2 * P])
        at_hi = m.sb("at_hi", [P, 4, 4 * P], F32R)
        at_lo = m.sb("at_lo", [P, 4, 4 * P], F32R)
        o_tmp = m.sb("o_tmp", [P, SH // 2, P])
        o_sum = m.sb("o_sum", [P, 2, SH // 2, P])

        w_loaded = [m.sem(f"w_loaded{n}") for n in range(4)]
        w_hi_done, w_lo_done = m.sem("w_hi_done"), m.sem("w_lo_done")
        consts_loaded, consts_made = m.sem("consts_loaded"), m.sem("consts_made")
        zeroed = m.sem("zeroed")
        x_loaded = [m.sem(f"x_loaded{n}") for n in range(2)]
        squared, pool_step, rstd_ready, x_scaled = (m.sem(n) for n in ("squared", "pool_step", "rstd_ready", "x_scaled"))
        x_turned, xt_hi_done, xt_lo_done = (m.sem(n) for n in ("x_turned", "xt_hi_done", "xt_lo_done"))
        q_projected, kv_projected = m.sem("q_projected"), m.sem("kv_projected")
        q_parts, k_parts, q_roped, k_roped = (m.sem(n) for n in ("q_parts", "k_parts", "q_roped", "k_roped"))
        v_copied, v_hi_done, v_split = (m.sem(n) for n in ("v_copied", "v_hi_done", "v_split"))
        q_turned, k_turned, q_hi_done, k_hi_done, q_split, k_split = (
            m.sem(n) for n in ("q_turned", "k_turned", "q_hi_done", "k_hi_done", "q_split", "k_split"))
        scores_read = m.sem("scores_read")
        scored, dve_step, max_ready, exp_done, recip_ready, scaled = (
            m.sem(n) for n in ("scored", "dve_step", "max_ready", "exp_done", "recip_ready", "scaled"))
        a_turned, at_hi_done, at_lo_done = (m.sem(n) for n in ("a_turned", "at_hi_done", "at_lo_done"))
        attended, o_copied, o_added = (m.sem(n) for n in ("attended", "o_copied", "o_added"))
        stored = [m.sem(f"stored{n}") for n in range(2)]
        read_out = {
            "x": (xt_lo_done, lambda t, h: 2 * t + h + 1), "q": (q_parts, lambda t: t + 1),
            "kv": (v_copied, lambda t: t + 1), "s": (scores_read, lambda t, j: 4 * t + j + 1),
            "qT": (q_split, lambda t: t + 1), "kT": (k_split, lambda t: t + 1),
            "a": (at_lo_done, lambda t, j: 4 * t + j + 1), "o": (o_added, lambda t, u: 2 * (SG * t + u + 1)),
        }

        def chunks_seen(k):
            own = 2 * (k % 2)
            return slice(own, own + 1) if k == 0 else (slice(0, 4, 3) if k % 2 == 0 else slice(1, 3))

        with nc.Block() as block:
            @block.sync
            def _(sp):
                w_view = w_in.rearrange("(c p) n -> c p n", p=P)
                with nc.allow_non_contiguous_dma(reason="gains by column"):
                    sp.dma_start(g_col[:, :], g_pre.rearrange("(c p) -> p c", p=P)).then_inc(consts_loaded, 16)
                sp.dma_start(xb[:, 0, :], x[0:P, :]).then_inc(x_loaded[0], 16)
                sp.dma_start(sink[:, :], sinks.unsqueeze(0).broadcast_to([P, SH])).then_inc(consts_loaded, 16)
                for c in range(KC):
                    if c >= 4:
                        sp.wait_ge(w_lo_done, c - 3)
                    sp.dma_start(w_raw[:, c % 4, :], w_view[c, :, 0:WA]).then_inc(w_loaded[c % 4], 16)
                    if c == 3:
                        sp.dma_start(rope_sb[:, :, :], rope.rearrange("(t p) n -> p t n", p=P)).then_inc(consts_loaded, 16)
                sp.dma_start(xb[:, 1, :], x[P:2 * P, :]).then_inc(x_loaded[1], 16)
                for k, i in tiles(sp):
                    p = k % 2
                    if k + 2 < TILES:
                        row = steady(lambda t: (t + 2) * P, k, i)
                        wait_apart(sp, (consts_loaded, 48), (x_turned, steady(lambda t: 2 * t + 2, k, i)))
                        sp.dma_start(xb[:, p, :], x[bass.ds(row, P), :]).then_inc(x_loaded[p], 16)
                    if k >= 1:
                        col = steady(lambda t: (t - 1) * P, k, i)
                        wait_apart(sp, (consts_loaded, 48), (o_added, steady(lambda t: 2 * SG * t, k, i)))
                        sp.dma_start(swa_t[:, :, bass.ds(col, P)], o_sum[:, 1 - p, :, :]).then_inc(stored[1 - p], 16)
                sp.wait_ge(o_added, 2 * SG * TILES)
                sp.dma_start(swa_t[:, :, (TILES - 1) * P:S], o_sum[:, 1, :, :]).then_inc(stored[1], 16)
                for q in stored:
                    sp.wait_ge(q, 16 * TILES // 2)

            @block.gpsimd
            def _(pool):
                make_identity(pool, ident, consts_made)
                pool.memset(half[:, :], -0.5).then_inc(consts_made, 1)
                pool.wait_ge(consts_made, 3)
                pool.memset(probs[:, :, :, :], 0.0).then_inc(zeroed, 1)

                def rstd_of(k, i):
                    waits = [(squared, steady(lambda t: t + 1, k, i))]
                    if k >= 2:
                        waits.append((x_scaled, steady(lambda t: t - 1, k, i)))
                    wait_apart(pool, (consts_made, 3), *waits)
                    q = k % 2
                    pool_rstd(pool, rstd[:, q:q + 1], ss[:, q:q + 1], D, half[:, :], pool_step,
                              steady(lambda t: t + 1, k, i)).then_inc(rstd_ready, 1)

                def rotate(k, i, parts, turned, out, a, b, roped):
                    pool.wait_ge(parts, steady(lambda t: t + 1, k, i))
                    if k >= 1:
                        pool.wait_ge(turned, steady(lambda t: t, k, i))
                    pool.tensor_tensor(out[:, :], a[:, :], b[:, :], ALU.add).then_inc(roped, 1)

                def scale_probs(k, i):
                    q = k % 2
                    pool.wait_ge(recip_ready, steady(lambda t: t + 1, k, i))
                    pool.tensor_tensor(probs[:, q, :, :], probs[:, q, :, :],
                                       recip[:, q, :].unsqueeze(2).broadcast_to([P, SH, 2 * P]), ALU.mult)\
                        .then_inc(scaled, 1)

                def split_v(k, i):
                    q = k % 2
                    waits = [(v_copied, steady(lambda t: t + 1, k, i))]
                    if k >= 1:
                        waits.append((attended, steady(lambda t: SG * t, k, i)))
                    wait_apart(pool, (consts_made, 3), *waits)
                    v = v_raw[:, q, :].rearrange("p (u d) -> p u d", u=SG)
                    pool.tensor_copy(v_hl[:, q, :, 0:HD], v).then_inc(v_hi_done, 1)
                    pool.wait_ge(v_hi_done, steady(lambda t: t + 1, k, i))
                    pool.tensor_tensor(v_hl[:, q, :, HD:2 * HD], v, v_hl[:, q, :, 0:HD].bitcast(F32), ALU.subtract)\
                        .then_inc(v_split, 1)

                rstd_of(0, None)
                for k, i in tiles(pool):
                    if k + 1 < TILES:
                        rstd_of(k + 1, i)
                    rotate(k, i, q_parts, q_turned, rot_q, rot_c, rot_s, q_roped)
                    rotate(k, i, k_parts, k_turned, rot_k, rot_kc, rot_ks, k_roped)
                    if k >= 1:
                        scale_probs(k - 1, i)
                    split_v(k, i)
                scale_probs(TILES - 1, None)

            @block.scalar
            def _(act):
                def square(k, i):
                    q = k % 2
                    act.wait_ge(x_loaded[q], steady(lambda t: 16 * (t // 2 + 1), k, i))
                    if k >= 2:
                        act.wait_ge(rstd_ready, steady(lambda t: t - 1, k, i))
                    act.activation(junk[:, :], xb[:, q, :], ACT.Square, accum_out=ss[:, q:q + 1]).then_inc(squared, 1)

                def turned_hi(k, i):
                    q = k % 2
                    for h in range(2):
                        act.wait_ge(x_turned, steady(lambda t: 2 * t + h + 1, k, i))
                        if k >= 2 and h == 0:
                            act.wait_ge(kv_projected, steady(lambda t: t - 1, k, i))
                        b = banks.bank("x", k, h)
                        act.activation(xt_hi[:, q, 4 * h:4 * h + 4, :], ps[:, b, :].rearrange("p (c n) -> p c n", n=P),
                                       ACT.Copy).then_inc(xt_hi_done, 1)

                def exps(k, i):
                    q = k % 2
                    act.wait_ge(max_ready, steady(lambda t: t + 1, k, i))
                    if k == 0:
                        act.wait_ge(zeroed, 1)
                    if k >= 2:
                        act.wait_ge(a_turned, steady(lambda t: 4 * (t - 1), k, i))
                        act.wait_ge(recip_ready, steady(lambda t: t - 1, k, i))
                    for j in range(4):
                        sc = ps[:, banks.bank("s", k, j), :].rearrange("p (h c n) -> p h c n", h=2, c=4)
                        pr = probs[:, q, 2 * j:2 * j + 2, :].rearrange("p h (c n) -> p h c n", c=4)
                        for h in range(2):
                            hh = 2 * j + h
                            seen, own = chunks_seen(k), slice(2 * q, 2 * q + 2)
                            for lo, cs in ((0, seen), (HD, own)):
                                part = slice(lo, lo + HD)
                                last = act.activation(pr[part, h, cs, :], sc[part, h, cs, :], ACT.Exp,
                                                      bias=bias[part, q, hh:hh + 1], accum_out=sums[part, q, hh:hh + 1])
                        last.then_inc(scores_read, 1)
                    act.activation(gap[:, q, :], gap[:, q, :], ACT.Exp).then_inc(exp_done, 1)

                def hi_qk(k, i):
                    q = k % 2
                    act.wait_ge(q_turned, steady(lambda t: t + 1, k, i))
                    src = ps[:, banks.bank("qT", k), :].rearrange("p (j n) -> p j n", n=P)
                    act.activation(q_hl[0:HD, :, 0, :], src[0:HD, :, :], ACT.Copy)
                    act.activation(q_hl[0:HD, :, 1, :], src[HD:P, :, :], ACT.Copy)
                    act.activation(q_lh[HD:P, :, 0, :], src[0:HD, :, :], ACT.Copy)
                    act.activation(q_lh[HD:P, :, 1, :], src[HD:P, :, :], ACT.Copy).then_inc(q_hi_done, 1)
                    act.wait_ge(k_turned, steady(lambda t: t + 1, k, i))
                    src = ps[:, banks.bank("kT", k), 0:P]
                    act.activation(k_hl[0:HD, 0, q, :], src[0:HD, :], ACT.Copy)
                    act.activation(k_hl[0:HD, 1, q, :], src[HD:P, :], ACT.Copy).then_inc(k_hi_done, 1)

                def copy_v(k, i):
                    act.wait_ge(k_parts, steady(lambda t: t + 1, k, i))
                    if k >= 2:
                        act.wait_ge(v_split, steady(lambda t: t - 1, k, i))
                    b = banks.bank("kv", k)
                    act.activation(v_raw[:, k % 2, :], ps[:, b, KV:2 * KV], ACT.Copy).then_inc(v_copied, 1)

                def hi_a(k, i):
                    for j in range(4):
                        act.wait_ge(a_turned, steady(lambda t: 4 * t + j + 1, k, i))
                        if k >= 1 and j == 0:
                            act.wait_ge(attended, steady(lambda t: SG * t, k, i))
                        b = banks.bank("a", k, j)
                        act.activation(at_hi[:, j, :], ps[:, b, :], ACT.Copy).then_inc(at_hi_done, 1)

                def copy_o(k, i):
                    for u in range(SG):
                        act.wait_ge(attended, steady(lambda t: SG * t + u + 1, k, i))
                        if k >= 1 and u == 0:
                            act.wait_ge(o_added, steady(lambda t: 2 * SG * t, k, i))
                        src = ps[:, banks.bank("o", k, u), :].rearrange("p (j e n) -> p j e n", e=2, n=P)
                        act.activation(o_tmp[0:HD, 2 * u:2 * u + 2, :], src[HD:P, :, 0, :], ACT.Copy)
                        act.activation(o_tmp[HD:P, 2 * u:2 * u + 2, :], src[0:HD, :, 1, :], ACT.Copy).then_inc(o_copied, 1)

                act.wait_ge(consts_loaded, 48)
                square(0, None)
                for c in range(KC):
                    act.wait_ge(w_loaded[c % 4], 16 * (c // 4 + 1))
                    act.activation(w_hi[:, c, :], w_raw[:, c % 4, :], ACT.Copy, scale=g_col[:, c:c + 1])\
                        .then_inc(w_hi_done, 1)
                turned_hi(0, None)
                for k, i in tiles(act):
                    if k + 1 < TILES:
                        square(k + 1, i)
                    if k >= 1:
                        exps(k - 1, i)
                    copy_v(k, i)
                    if k + 1 < TILES:
                        turned_hi(k + 1, i)
                    hi_qk(k, i)
                    if k >= 1:
                        hi_a(k - 1, i)
                        copy_o(k - 1, i)
                exps(TILES - 1, None)
                hi_a(TILES - 1, None)
                copy_o(TILES - 1, None)

            @block.vector
            def _(dve):
                def scale_x(k, i):
                    q = k % 2
                    dve.wait_ge(rstd_ready, steady(lambda t: t + 1, k, i))
                    dve.tensor_scalar(xb[:, q, :], xb[:, q, :], rstd[:, q:q + 1], None, ALU.mult).then_inc(x_scaled, 1)

                def turned_lo(k, i):
                    q = k % 2
                    for h in range(2):
                        dve.wait_ge(xt_hi_done, steady(lambda t: 2 * t + h + 1, k, i))
                        b = banks.bank("x", k, h)
                        dve.tensor_tensor(xt_lo[:, q, 4 * h:4 * h + 4, :], ps[:, b, :].rearrange("p (c n) -> p c n", n=P),
                                          xt_hi[:, q, 4 * h:4 * h + 4, :].bitcast(F32), ALU.subtract)\
                            .then_inc(xt_lo_done, 1)

                def rope_parts(k, i, src, heads, c_out, s_out, scaled_by, tok):
                    cos = rope_sb[:, tok, scaled_by:scaled_by + HD]
                    sin = rope_sb[:, tok, scaled_by + HD:scaled_by + 2 * HD]
                    view = src.rearrange("p (h d) -> p h d", d=HD)
                    dve.tensor_tensor(c_out[:, :].rearrange("p (h d) -> p h d", d=HD), view,
                                      cos.broadcast_to([P, heads, HD]), ALU.mult)
                    for a in range(2):
                        to, frm = slice(a * HD // 2, (a + 1) * HD // 2), slice((1 - a) * HD // 2, (2 - a) * HD // 2)
                        last = dve.tensor_tensor(
                            s_out[:, :].rearrange("p (h d) -> p h d", d=HD)[:, :, to], view[:, :, frm],
                            sin[:, :, to].broadcast_to([P, heads, HD // 2]), ALU.mult)
                    return last

                def rope_q(k, i):
                    dve.wait_ge(q_projected, steady(lambda t: t + 1, k, i))
                    if k >= 1:
                        dve.wait_ge(q_roped, steady(lambda t: t, k, i))
                    tok = bass.ds(steady(lambda t: t, k, i), 1)
                    b = banks.bank("q", k)
                    rope_parts(k, i, ps[:, b, :], SH, rot_c, rot_s, 2 * HD, tok).then_inc(q_parts, 1)

                def rope_k(k, i):
                    dve.wait_ge(kv_projected, steady(lambda t: t + 1, k, i))
                    if k >= 1:
                        dve.wait_ge(k_roped, steady(lambda t: t, k, i))
                    tok = bass.ds(steady(lambda t: t, k, i), 1)
                    rope_parts(k, i, ps[:, banks.bank("kv", k), 0:KV], SG, rot_kc, rot_ks, 0, tok).then_inc(k_parts, 1)

                def maxima(k, i):
                    q = k % 2
                    if k >= 2:
                        dve.wait_ge(exp_done, steady(lambda t: t - 1, k, i))
                    for j in range(4):
                        dve.wait_ge(scored, steady(lambda t: 4 * t + j + 1, k, i))
                        sc = ps[:, banks.bank("s", k, j), :].rearrange("p (h c n) -> p h c n", h=2, c=4)
                        for lo, cs in ((0, chunks_seen(k)), (HD, slice(2 * q, 2 * q + 2))):
                            part = slice(lo, lo + HD)
                            last = dve.tensor_reduce(top[part, q, 2 * j:2 * j + 2], sc[part, :, cs, :], AX.XY, ALU.max)
                    last.then_inc(dve_step, 1)
                    dve.wait_ge(dve_step, steady(lambda t: 3 * t + 1, k, i))
                    dve.tensor_tensor(top[:, q, :], top[:, q, :], sink[:, :], ALU.max).then_inc(dve_step, 1)
                    dve.wait_ge(dve_step, steady(lambda t: 3 * t + 2, k, i))
                    dve.tensor_scalar(bias[:, q, :], top[:, q, :], -1.0, None, ALU.mult)
                    dve.tensor_tensor(gap[:, q, :], sink[:, :], top[:, q, :], ALU.subtract).then_inc(max_ready, 1)

                def recips(k, i):
                    q = k % 2
                    dve.wait_ge(exp_done, steady(lambda t: t + 1, k, i))
                    if k >= 2:
                        dve.wait_ge(scaled, steady(lambda t: t - 1, k, i))
                    dve.tensor_tensor(sums[:, q, :], sums[:, q, :], gap[:, q, :], ALU.add).then_inc(dve_step, 1)
                    dve.wait_ge(dve_step, steady(lambda t: 3 * t + 3, k, i))
                    dve.reciprocal(recip[:, q, :], sums[:, q, :]).then_inc(recip_ready, 1)

                def lo_qk(k, i):
                    q = k % 2
                    dve.wait_ge(q_hi_done, steady(lambda t: t + 1, k, i))
                    b = banks.bank("qT", k)
                    src = ps[:, b, :].rearrange("p (j n) -> p j n", n=P)
                    even, odd = q_hl[0:HD, :, 0, :].bitcast(F32), q_lh[HD:P, :, 1, :].bitcast(F32)
                    dve.tensor_tensor(q_hl[HD:P, :, 0, :], src[0:HD, :, :], even, ALU.subtract)
                    dve.tensor_tensor(q_lh[0:HD, :, 0, :], src[0:HD, :, :], even, ALU.subtract)
                    dve.tensor_tensor(q_hl[HD:P, :, 1, :], src[HD:P, :, :], odd, ALU.subtract)
                    dve.tensor_tensor(q_lh[0:HD, :, 1, :], src[HD:P, :, :], odd, ALU.subtract).then_inc(q_split, 1)
                    dve.wait_ge(k_hi_done, steady(lambda t: t + 1, k, i))
                    b = banks.bank("kT", k)
                    dve.tensor_tensor(k_hl[HD:P, 0, q, :], ps[0:HD, b, 0:P], k_hl[0:HD, 0, q, :].bitcast(F32), ALU.subtract)
                    dve.tensor_tensor(k_hl[HD:P, 1, q, :], ps[HD:P, b, 0:P], k_hl[0:HD, 1, q, :].bitcast(F32),
                                      ALU.subtract).then_inc(k_split, 1)

                def lo_a(k, i):
                    for j in range(4):
                        dve.wait_ge(at_hi_done, steady(lambda t: 4 * t + j + 1, k, i))
                        b = banks.bank("a", k, j)
                        dve.tensor_tensor(at_lo[:, j, :], ps[:, b, :], at_hi[:, j, :].bitcast(F32), ALU.subtract)\
                            .then_inc(at_lo_done, 1)

                def add_o(k, i):
                    q = k % 2
                    for u in range(SG):
                        dve.wait_ge(o_copied, steady(lambda t: SG * t + u + 1, k, i))
                        if k >= 2 and u == 0:
                            dve.wait_ge(stored[q], steady(lambda t: 16 * (t // 2), k, i))
                        b = banks.bank("o", k, u)
                        src = ps[:, b, :].rearrange("p (j e n) -> p j e n", e=2, n=P)
                        dve.tensor_tensor(o_sum[0:HD, q, 2 * u:2 * u + 2, :], src[0:HD, :, 0, :],
                                          o_tmp[0:HD, 2 * u:2 * u + 2, :], ALU.add).then_inc(o_added, 1)
                        dve.tensor_tensor(o_sum[HD:P, q, 2 * u:2 * u + 2, :], src[HD:P, :, 1, :],
                                          o_tmp[HD:P, 2 * u:2 * u + 2, :], ALU.add).then_inc(o_added, 1)

                scale_x(0, None)
                for c in range(KC):
                    dve.wait_ge(w_hi_done, c + 1)
                    dve.scalar_tensor_tensor(w_lo[:, c, :], w_raw[:, c % 4, :], g_col[:, c:c + 1],
                                             w_hi[:, c, :].bitcast(F32), ALU.mult, ALU.subtract).then_inc(w_lo_done, 1)
                turned_lo(0, None)
                for k, i in tiles(dve):
                    rope_q(k, i)
                    if k >= 1:
                        maxima(k - 1, i)
                    if k + 1 < TILES:
                        scale_x(k + 1, i)
                    rope_k(k, i)
                    if k + 1 < TILES:
                        turned_lo(k + 1, i)
                    if k >= 1:
                        recips(k - 1, i)
                    lo_qk(k, i)
                    if k >= 1:
                        lo_a(k - 1, i)
                        add_o(k - 1, i)
                maxima(TILES - 1, None)
                recips(TILES - 1, None)
                lo_a(TILES - 1, None)
                add_o(TILES - 1, None)

            @block.tensor
            def _(pe):
                def free(k, i, kind, *n):
                    banks.free(pe, read_out, k, i, kind, *n)
                    return banks.bank(kind, k, *n)

                def turn_x(k, i):
                    pe.wait_ge(x_scaled, steady(lambda t: t + 1, k, i))
                    for h in range(2):
                        b = free(k, i, "x", h)
                        for c in range(4):
                            last = pe.transpose(ps[:, b, c * P:(c + 1) * P],
                                                xb[:, k % 2, (4 * h + c) * P:(4 * h + c + 1) * P], ident[:, :])
                        last.then_inc(x_turned, 1)

                def project(k, i, kind, first, width, done):
                    q = k % 2
                    b = free(k, i, kind)
                    for c in range(KC):
                        if kind == "q" and c % 4 == 0:
                            pe.wait_ge(xt_lo_done, steady(lambda t: 2 * t + c // 4 + 1, k, i))
                        if k == 0 and kind == "q":
                            pe.wait_ge(w_lo_done, c + 1)
                        for n, (lhs, rhs) in enumerate(((xt_hi, w_hi), (xt_hi, w_lo), (xt_lo, w_hi))):
                            last = pe.matmul(ps[:, b, 0:width], lhs[:, q, c, :], rhs[:, c, first:first + width],
                                             start=(c == 0 and n == 0), stop=(c == KC - 1 and n == 2))
                    last.then_inc(done, 1)

                def turn_qk(k, i):
                    pe.wait_ge(q_roped, steady(lambda t: t + 1, k, i))
                    b = free(k, i, "qT")
                    for j in range(4):
                        last = pe.transpose(ps[:, b, j * P:(j + 1) * P], rot_q[:, j * P:(j + 1) * P], ident[:, :])
                    last.then_inc(q_turned, 1)
                    pe.wait_ge(k_roped, steady(lambda t: t + 1, k, i))
                    b = free(k, i, "kT")
                    pe.transpose(ps[:, b, 0:P], rot_k[:, :], ident[:, :]).then_inc(k_turned, 1)

                def score(k, i):
                    pe.wait_ge(q_split, steady(lambda t: t + 1, k, i))
                    pe.wait_ge(k_split, steady(lambda t: t + 1, k, i))
                    slots = 1 if k == 0 else 2
                    for j in range(4):
                        b = free(k, i, "s", j)
                        for h in range(2):
                            for n, stack in enumerate((q_hl, q_lh)):
                                last = pe.matmul(ps[:, b, 2 * P * h:2 * P * h + slots * P], stack[:, j, h, :],
                                                 k_hl[:, j // 2, 0:slots, :], start=(n == 0), stop=(n == 1))
                        last.then_inc(scored, 1)

                def turn_a(k, i):
                    pe.wait_ge(scaled, steady(lambda t: t + 1, k, i))
                    for j in range(4):
                        u, slot = j // 2, j % 2
                        b = free(k, i, "a", j)
                        for h in range(4):
                            last = pe.transpose(ps[:, b, h * P:(h + 1) * P],
                                                probs[:, k % 2, 4 * u + h, slot * P:(slot + 1) * P], ident[:, :])
                        last.then_inc(a_turned, 1)

                def attend(k, i):
                    pe.wait_ge(v_split, steady(lambda t: t + 1, k, i))
                    slots = (0,) if k == 0 else (0, 1)
                    for u in range(SG):
                        b = free(k, i, "o", u)
                        for slot in slots:
                            pe.wait_ge(at_lo_done, steady(lambda t: 4 * t + 2 * u + slot + 1, k, i))
                            for n, a in enumerate((at_hi, at_lo)):
                                last = pe.matmul(ps[:, b, :], v_hl[:, slot, u, :], a[:, 2 * u + slot, :],
                                                 start=(slot == 0 and n == 0), stop=(slot == slots[-1] and n == 1))
                        last.then_inc(attended, 1)

                pe.wait_ge(consts_made, 2)
                turn_x(0, None)
                for k, i in tiles(pe):
                    project(k, i, "q", 0, QA, q_projected)
                    if k >= 1:
                        score(k - 1, i)
                    project(k, i, "kv", QA, 2 * KV, kv_projected)
                    if k + 1 < TILES:
                        turn_x(k + 1, i)
                    turn_qk(k, i)
                    if k >= 1:
                        turn_a(k - 1, i)
                        attend(k - 1, i)
                score(TILES - 1, None)
                turn_a(TILES - 1, None)
                attend(TILES - 1, None)
        m.end()


def diff_proj(nc, x, w_in, g_pre, rope, q_s, k_s, v_s):
    order = [("x", 0, 0), ("x", 0, 1)]
    for t in range(TILES + 1):
        if t < TILES:
            order.append(("q", t))
        if t >= 1:
            order.append(("kT", t - 1))
        if t < TILES:
            order += [("k", t), ("qT", t), ("v", t)]
        if t + 1 < TILES:
            order += [("x", t + 1, 0), ("x", t + 1, 1)]
    banks = Banks(list(range(7)), order)
    first = WA

    with ExitStack() as ctx:
        m = Memory(nc, ctx, "dp")
        ps = m.psum()
        w_hi = m.sb("w_hi", [P, KC, WB], F32R)
        w_lo = m.sb("w_lo", [P, KC, WB], F32R)
        w_raw = m.sb("w_raw", [P, 4, WB])
        g_col = m.sb("g_col", [P, KC])
        rope_sb = m.sb("rope", [P, 2, 4 * HD])
        ident = m.sb("ident", [P, P])
        half = m.sb("half", [P, 1])
        xb = m.sb("x", [P, 2, D])
        junk = m.sb("junk", [P, D], BF16)
        ss = m.sb("ss", [P, 2])
        rstd = m.sb("rstd", [P, 2])
        xt_hi = m.sb("xt_hi", [P, 2, KC, P], F32R)
        xt_lo = m.sb("xt_lo", [P, 2, KC, P], F32R)
        part_c = m.sb("part_c", [P, 2, DW])
        part_s = m.sb("part_s", [P, 2, DW])
        rot = m.sb("rot", [P, 2, DW])
        q_hl = m.sb("q_hl", [P, DH, 2, P], F32R)
        k_hl = m.sb("k_hl", [P, DH, 2, P], F32R)
        v_hl = m.sb("v_hl", [P, 2, DH, 2, VD], F32R)

        w_loaded = [m.sem(f"w_loaded{n}") for n in range(4)]
        w_hi_done, w_lo_done = m.sem("w_hi_done"), m.sem("w_lo_done")
        consts_loaded, consts_made = m.sem("consts_loaded"), m.sem("consts_made")
        x_loaded = [m.sem(f"x_loaded{n}") for n in range(2)]
        rope_loaded = [m.sem(f"rope_loaded{n}") for n in range(2)]
        squared, pool_step, rstd_ready, x_scaled = (m.sem(n) for n in ("squared", "pool_step", "rstd_ready", "x_scaled"))
        x_turned, xt_hi_done, xt_lo_done = (m.sem(n) for n in ("x_turned", "xt_hi_done", "xt_lo_done"))
        projected = [m.sem(n) for n in ("q_projected", "k_projected", "v_projected")]
        parts = [m.sem(n) for n in ("q_parts", "k_parts")]
        roped = [m.sem(n) for n in ("q_roped", "k_roped")]
        turned = [m.sem(n) for n in ("q_turned", "k_turned")]
        hi_done = [m.sem(n) for n in ("q_hi_done", "k_hi_done")]
        split = [m.sem(n) for n in ("q_split", "k_split")]
        v_hi_done, v_split = m.sem("v_hi_done"), m.sem("v_split")
        stored = [m.sem(n) for n in ("q_stored", "k_stored")]
        v_stored = [m.sem(f"v_stored{n}") for n in range(2)]
        read_out = {
            "x": (xt_lo_done, lambda t, h: 2 * t + h + 1), "q": (parts[0], lambda t: t + 1),
            "k": (parts[1], lambda t: t + 1), "v": (v_split, lambda t: t + 1),
            "qT": (split[0], lambda t: t + 1), "kT": (split[1], lambda t: t + 1),
        }

        with nc.Block() as block:
            @block.sync
            def _(sp):
                w_view = w_in.rearrange("(c p) n -> c p n", p=P)
                with nc.allow_non_contiguous_dma(reason="gains by column"):
                    sp.dma_start(g_col[:, :], g_pre.rearrange("(c p) -> p c", p=P)).then_inc(consts_loaded, 16)
                for n in range(2):
                    sp.dma_start(xb[:, n, :], x[n * P:(n + 1) * P, :]).then_inc(x_loaded[n], 16)
                    sp.dma_start(rope_sb[:, n, :], rope[n * P:(n + 1) * P, :]).then_inc(rope_loaded[n], 16)
                for c in range(KC):
                    if c >= 4:
                        sp.wait_ge(w_lo_done, c - 3)
                    sp.dma_start(w_raw[:, c % 4, :], w_view[c, :, first:first + WB]).then_inc(w_loaded[c % 4], 16)
                for k, i in tiles(sp):
                    p = k % 2
                    if k >= 1:
                        col = steady(lambda t: (t - 1) * P, k, i)
                        wait_apart(sp, (consts_loaded, 16), (split[1], steady(lambda t: t, k, i)))
                        sp.dma_start(k_s[:, :, :, bass.ds(col, P)], k_hl[:, :, :, :].bitcast(F32)).then_inc(stored[1], 16)
                    wait_apart(sp, (consts_loaded, 16), (split[0], steady(lambda t: t + 1, k, i)))
                    sp.dma_start(q_s[bass.ds(steady(lambda t: t, k, i), 1), :, :, :, :].rearrange("a p h m n -> p (a h) m n"),
                                 q_hl[:, :, :, :].bitcast(F32)).then_inc(stored[0], 16)
                    if k + 2 < TILES:
                        row = steady(lambda t: (t + 2) * P, k, i)
                        wait_apart(sp, (consts_loaded, 16), (x_turned, steady(lambda t: 2 * t + 2, k, i)),
                                   (parts[1], steady(lambda t: t + 1, k, i)))
                        sp.dma_start(xb[:, p, :], x[bass.ds(row, P), :]).then_inc(x_loaded[p], 16)
                        sp.dma_start(rope_sb[:, p, :], rope[bass.ds(row, P), :]).then_inc(rope_loaded[p], 16)
                    wait_apart(sp, (consts_loaded, 16), (v_split, steady(lambda t: t + 1, k, i)))
                    sp.dma_start(v_s[:, :, bass.ds(steady(lambda t: t, k, i), 1), :, :].rearrange("p h t a v -> p h (t a) v"),
                                 v_hl[:, p, :, :, :].bitcast(F32)).then_inc(v_stored[p], 16)
                sp.wait_ge(split[1], TILES)
                sp.dma_start(k_s[:, :, :, (TILES - 1) * P:S], k_hl[:, :, :, :].bitcast(F32)).then_inc(stored[1], 16)
                for s in stored:
                    sp.wait_ge(s, 16 * TILES)
                for s in v_stored:
                    sp.wait_ge(s, 16 * TILES // 2)

            @block.gpsimd
            def _(pool):
                make_identity(pool, ident, consts_made)
                pool.memset(half[:, :], -0.5).then_inc(consts_made, 1)
                pool.wait_ge(consts_made, 3)

                def rstd_of(k, i):
                    waits = [(squared, steady(lambda t: t + 1, k, i))]
                    if k >= 2:
                        waits.append((x_scaled, steady(lambda t: t - 1, k, i)))
                    wait_apart(pool, (consts_made, 3), *waits)
                    q = k % 2
                    pool_rstd(pool, rstd[:, q:q + 1], ss[:, q:q + 1], D, half[:, :], pool_step,
                              steady(lambda t: t + 1, k, i)).then_inc(rstd_ready, 1)

                def rotate(n, k, i):
                    pool.wait_ge(parts[n], steady(lambda t: t + 1, k, i))
                    if k >= 1:
                        pool.wait_ge(turned[n], steady(lambda t: t, k, i))
                    pool.tensor_tensor(rot[:, n, :], part_c[:, n, :], part_s[:, n, :], ALU.add).then_inc(roped[n], 1)

                rstd_of(0, None)
                for k, i in tiles(pool):
                    if k + 1 < TILES:
                        rstd_of(k + 1, i)
                    rotate(0, k, i)
                    rotate(1, k, i)

            @block.scalar
            def _(act):
                def square(k, i):
                    q = k % 2
                    act.wait_ge(x_loaded[q], steady(lambda t: 16 * (t // 2 + 1), k, i))
                    if k >= 2:
                        act.wait_ge(rstd_ready, steady(lambda t: t - 1, k, i))
                    act.activation(junk[:, :], xb[:, q, :], ACT.Square, accum_out=ss[:, q:q + 1]).then_inc(squared, 1)

                def turned_hi(k, i):
                    q = k % 2
                    for h in range(2):
                        act.wait_ge(x_turned, steady(lambda t: 2 * t + h + 1, k, i))
                        if k >= 2 and h == 0:
                            act.wait_ge(projected[2], steady(lambda t: t - 1, k, i))
                        b = banks.bank("x", k, h)
                        act.activation(xt_hi[:, q, 4 * h:4 * h + 4, :], ps[:, b, :].rearrange("p (c n) -> p c n", n=P),
                                       ACT.Copy).then_inc(xt_hi_done, 1)

                def hi_qk(n, k, i):
                    out = (q_hl, k_hl)[n]
                    act.wait_ge(turned[n], steady(lambda t: t + 1, k, i))
                    if k >= 1:
                        act.wait_ge(stored[n], steady(lambda t: 16 * t, k, i))
                    src = ps[:, banks.bank(("qT", "kT")[n], k), :].rearrange("p (h n) -> p h n", n=P)
                    act.activation(out[0:HD, :, 0, :], src[0:HD, :, :], ACT.Copy)
                    act.activation(out[0:HD, :, 1, :], src[HD:P, :, :], ACT.Copy).then_inc(hi_done[n], 1)

                def hi_v(k, i):
                    act.wait_ge(projected[2], steady(lambda t: t + 1, k, i))
                    if k >= 2:
                        act.wait_ge(v_stored[k % 2], steady(lambda t: 16 * (t // 2), k, i))
                    act.activation(v_hl[:, k % 2, :, 0, :], ps[:, banks.bank("v", k), :].rearrange("p (h v) -> p h v", h=DH),
                                   ACT.Copy).then_inc(v_hi_done, 1)

                act.wait_ge(consts_loaded, 16)
                square(0, None)
                for c in range(KC):
                    act.wait_ge(w_loaded[c % 4], 16 * (c // 4 + 1))
                    act.activation(w_hi[:, c, :], w_raw[:, c % 4, :], ACT.Copy, scale=g_col[:, c:c + 1])\
                        .then_inc(w_hi_done, 1)
                turned_hi(0, None)
                for k, i in tiles(act):
                    if k >= 1:
                        hi_v(k - 1, i)
                        hi_qk(1, k - 1, i)
                    if k + 1 < TILES:
                        square(k + 1, i)
                    hi_qk(0, k, i)
                    if k + 1 < TILES:
                        turned_hi(k + 1, i)
                hi_v(TILES - 1, None)
                hi_qk(1, TILES - 1, None)

            @block.vector
            def _(dve):
                def scale_x(k, i):
                    q = k % 2
                    dve.wait_ge(rstd_ready, steady(lambda t: t + 1, k, i))
                    dve.tensor_scalar(xb[:, q, :], xb[:, q, :], rstd[:, q:q + 1], None, ALU.mult).then_inc(x_scaled, 1)

                def turned_lo(k, i):
                    q = k % 2
                    for h in range(2):
                        dve.wait_ge(xt_hi_done, steady(lambda t: 2 * t + h + 1, k, i))
                        dve.tensor_tensor(xt_lo[:, q, 4 * h:4 * h + 4, :],
                                          ps[:, banks.bank("x", k, h), :].rearrange("p (c n) -> p c n", n=P),
                                          xt_hi[:, q, 4 * h:4 * h + 4, :].bitcast(F32), ALU.subtract)\
                            .then_inc(xt_lo_done, 1)

                def rope_parts(n, k, i):
                    q = k % 2
                    dve.wait_ge(projected[n], steady(lambda t: t + 1, k, i))
                    if n == 0:
                        dve.wait_ge(rope_loaded[q], steady(lambda t: 16 * (t // 2 + 1), k, i))
                    if k >= 1:
                        dve.wait_ge(roped[n], steady(lambda t: t, k, i))
                    at = 2 * HD * (1 - n)
                    cos, sin = rope_sb[:, q, at:at + HD].unsqueeze(1), rope_sb[:, q, at + HD:at + 2 * HD].unsqueeze(1)
                    view = ps[:, banks.bank(("q", "k")[n], k), :].rearrange("p (h d) -> p h d", d=HD)
                    c_out = part_c[:, n, :].rearrange("p (h d) -> p h d", d=HD)
                    s_out = part_s[:, n, :].rearrange("p (h d) -> p h d", d=HD)
                    heads = 2 * DH
                    dve.tensor_tensor(c_out, view, cos.broadcast_to([P, heads, HD]), ALU.mult)
                    for a in range(2):
                        to, frm = slice(a * HD // 2, (a + 1) * HD // 2), slice((1 - a) * HD // 2, (2 - a) * HD // 2)
                        last = dve.tensor_tensor(s_out[:, :, to], view[:, :, frm],
                                                 sin[:, :, to].broadcast_to([P, heads, HD // 2]), ALU.mult)
                    last.then_inc(parts[n], 1)

                def lo_qk(n, k, i):
                    out = (q_hl, k_hl)[n]
                    dve.wait_ge(hi_done[n], steady(lambda t: t + 1, k, i))
                    src = ps[:, banks.bank(("qT", "kT")[n], k), :].rearrange("p (h n) -> p h n", n=P)
                    dve.tensor_tensor(out[HD:P, :, 0, :], src[0:HD, :, :], out[0:HD, :, 0, :].bitcast(F32), ALU.subtract)
                    dve.tensor_tensor(out[HD:P, :, 1, :], src[HD:P, :, :], out[0:HD, :, 1, :].bitcast(F32), ALU.subtract)\
                        .then_inc(split[n], 1)

                def lo_v(k, i):
                    dve.wait_ge(v_hi_done, steady(lambda t: t + 1, k, i))
                    dve.tensor_tensor(v_hl[:, k % 2, :, 1, :],
                                      ps[:, banks.bank("v", k), :].rearrange("p (h v) -> p h v", h=DH),
                                      v_hl[:, k % 2, :, 0, :].bitcast(F32), ALU.subtract).then_inc(v_split, 1)

                scale_x(0, None)
                for c in range(KC):
                    dve.wait_ge(w_hi_done, c + 1)
                    dve.scalar_tensor_tensor(w_lo[:, c, :], w_raw[:, c % 4, :], g_col[:, c:c + 1],
                                             w_hi[:, c, :].bitcast(F32), ALU.mult, ALU.subtract).then_inc(w_lo_done, 1)
                turned_lo(0, None)
                for k, i in tiles(dve):
                    if k >= 1:
                        lo_v(k - 1, i)
                    rope_parts(0, k, i)
                    if k >= 1:
                        lo_qk(1, k - 1, i)
                    if k + 1 < TILES:
                        scale_x(k + 1, i)
                    rope_parts(1, k, i)
                    lo_qk(0, k, i)
                    if k + 1 < TILES:
                        turned_lo(k + 1, i)
                lo_v(TILES - 1, None)
                lo_qk(1, TILES - 1, None)

            @block.tensor
            def _(pe):
                def free(k, i, kind, *n):
                    banks.free(pe, read_out, k, i, kind, *n)
                    return banks.bank(kind, k, *n)

                def turn_x(k, i):
                    pe.wait_ge(x_scaled, steady(lambda t: t + 1, k, i))
                    for h in range(2):
                        b = free(k, i, "x", h)
                        for c in range(4):
                            last = pe.transpose(ps[:, b, c * P:(c + 1) * P],
                                                xb[:, k % 2, (4 * h + c) * P:(4 * h + c + 1) * P], ident[:, :])
                        last.then_inc(x_turned, 1)

                def project(n, k, i):
                    q = k % 2
                    b = free(k, i, "qkv"[n])
                    for c in range(KC):
                        if n == 0 and c % 4 == 0:
                            pe.wait_ge(xt_lo_done, steady(lambda t: 2 * t + c // 4 + 1, k, i))
                        if k == 0 and n == 0:
                            pe.wait_ge(w_lo_done, c + 1)
                        for j, (lhs, rhs) in enumerate(((xt_hi, w_hi), (xt_hi, w_lo), (xt_lo, w_hi))):
                            last = pe.matmul(ps[:, b, :], lhs[:, q, c, :], rhs[:, c, n * DW:(n + 1) * DW],
                                             start=(c == 0 and j == 0), stop=(c == KC - 1 and j == 2))
                    last.then_inc(projected[n], 1)

                def turn_qk(n, k, i):
                    pe.wait_ge(roped[n], steady(lambda t: t + 1, k, i))
                    b = free(k, i, ("qT", "kT")[n])
                    for j in range(DH):
                        last = pe.transpose(ps[:, b, j * P:(j + 1) * P], rot[:, n, j * P:(j + 1) * P], ident[:, :])
                    last.then_inc(turned[n], 1)

                pe.wait_ge(consts_made, 2)
                turn_x(0, None)
                for k, i in tiles(pe):
                    project(0, k, i)
                    if k >= 1:
                        turn_qk(1, k - 1, i)
                    project(1, k, i)
                    turn_qk(0, k, i)
                    project(2, k, i)
                    if k + 1 < TILES:
                        turn_x(k + 1, i)
                turn_qk(1, TILES - 1, None)
        m.end()


S_SLOTS, T_SLOTS, A_SLOTS, Q_SLOTS = 5, 2, 4, 4
KINDS = {
    "S": ("PE", (-1.33, -1.82)),
    "R": ("DVE", (-0.33, 0.02)),
    "M": ("DVE", (-1.55,)),
    "E": ("ACT", (1.72, -2.49)),
    "C": ("DVE", (-2.37,)),
    "A": ("POOL", (0.0,)),
    "B": ("DVE", (1.29,)),
    "T": ("PE", (0.04,)),
    "H": ("ACT", (0.17,)),
    "L": ("DVE", (1.99,)),
    "V": ("PE", (1.59,)),
    "O": ("ACT", (1.44,)),
    "P": ("DVE", (1.31,)),
    "Q": ("ACT", (-0.38,)),
    "N": ("POOL", (1.3,)),
}
COMBINED_BY = ("A", "B", "A", "B")


def attention_plan():
    tiles_in_turn = list(range(1, TILES, 2)) + list(range(TILES - 2, -1, -2))
    chunks = [-(-(t + 1) // 4) for t in tiles_in_turn]
    steps = len(chunks)
    heads, hop, own = 3, 0.16, 0.06
    events, turns = {}, {kind: [] for kind in KINDS}

    def add(kind, h, s, *rest, us, after):
        events[kind, h, s, *rest] = us, [e for e in after if e]
        turns[kind].append((kind, h, s, *rest))

    def slot(kind, of, n):
        back = len(turns[of]) - n
        return (kind, *turns[of][back][1:]) if back >= 0 else None

    for h in range(heads):
        for s in range(steps):
            n = chunks[s]
            part = [min(4, tiles_in_turn[s] + 1 - 4 * c) / 4 for c in range(n)]
            last, second_last = divmod(h * steps + s - 1, steps), divmod(h * steps + s - 2, steps)
            for m in range(2):
                for c in range(n):
                    add("S", h, s, m, c, us=max(0.43 * part[c], 0.32), after=[slot("E", "S", S_SLOTS)])
                    add("R", h, s, m, c, us=0.53 * part[c] + (0.34 if c == n - 1 else 0.07), after=[("S", h, s, m, c)])
                add("M", h, s, m, us=0.08, after=[("R", h, s, m, c) for c in range(n)])
                for c in range(n):
                    add("E", h, s, m, c, us=0.57 * part[c] + 0.1,
                        after=[("M", h, s, m), second_last[0] >= 0 and ("T", *second_last, chunks[second_last[1]] - 1)])
            add("C", h, s, us=0.6, after=[("E", h, s, m, c) for m in range(2) for c in range(n)])
            for c in range(n):
                combine = COMBINED_BY[c]
                add(combine, h, s, c, after=[("C", h, s)],
                    us=1.75 * part[c] + 0.3 if combine == "A" else 0.56 * part[c] + 0.1)
                add("T", h, s, c, us=0.43 * part[c], after=[(combine, h, s, c), slot("L", "T", T_SLOTS)])
                add("H", h, s, c, us=0.45 * part[c] + 0.05, after=[("T", h, s, c), slot("V", "H", A_SLOTS)])
                add("L", h, s, c, us=0.53 * part[c] + 0.07, after=[("H", h, s, c)])
                add("V", h, s, c, us=0.87 * part[c], after=[("L", h, s, c), c == 0 and last[0] >= 0 and ("P", *last)])
            add("O", h, s, us=0.25, after=[("V", h, s, n - 1)])
            add("P", h, s, us=0.25, after=[("O", h, s)])
            add("Q", h, s, us=0.3, after=[("P", h, s)])
            add("N", h, s, us=1.3, after=[("Q", h, s)])

    free = {engine: 0.0 for engine, _ in KINDS.values()}
    start, taken = {}, {kind: 0 for kind in KINDS}
    for _ in range(len(events)):
        best = {}
        for kind, (engine, shifts) in KINDS.items():
            if taken[kind] == len(turns[kind]):
                continue
            event = turns[kind][taken[kind]]
            if any(e not in start for e in events[event][1]):
                continue
            ready = max([start[e] + events[e][0] + (own if KINDS[e[0]][0] == engine else hop) for e in events[event][1]] +
                        [free[engine]])
            _, h, s, *rest = event
            pressing = h * steps + s + shifts[rest[0] if len(shifts) > 1 else 0] + 0.1 * (rest[-1] if rest else 0)
            best[engine] = min(best.get(engine, (ready, pressing, event)), (ready, pressing, event))
        time, _, event = min(best.values(), key=lambda b: b[0])
        start[event] = time
        free[KINDS[event[0]][0]] = time + events[event][0]
        taken[event[0]] += 1

    begin = start["S", heads - 1, 0, 0, 0]
    late = {(kind, *rest) for (kind, h, *rest), t in start.items() if h == heads - 2 and t >= begin}
    order = []
    for kind, h, *rest in sorted(start, key=lambda e: start[e]):
        if h == heads - 2 and (kind, *rest) in late:
            order.append((1, kind, *rest))
        elif h == heads - 1 and (kind, *rest) not in late:
            order.append((0, kind, *rest))
    return tiles_in_turn, chunks, order


def diff_attn(nc, q_s, k_s, v_s, lambdas, mixed):
    tiles_in_turn, chunks, order = attention_plan()
    steps = len(tiles_in_turn)
    ordinal, total = {}, {}
    for _, *e in sorted(order, key=lambda e: (e[2], e[0])):
        ordinal[tuple(e)] = total[e[0]] = total.get(e[0], 0) + 1
    S_BANKS, T_BANKS, O_BANK = range(S_SLOTS), range(S_SLOTS, S_SLOTS + T_SLOTS), S_SLOTS + T_SLOTS
    assert total["S"] % len(S_BANKS) == 0 and total["T"] % len(T_BANKS) == 0 and total["T"] % A_SLOTS == 0

    def width(s, c):
        return min(4, tiles_in_turn[s] + 1 - 4 * c) * P

    def tops_count(s):
        return sum(2 for n in chunks[:s] if n > 1)

    with ExitStack() as ctx:
        m_ = Memory(nc, ctx, "da")
        ps = m_.psum()
        keys = m_.sb("keys", [P, DH, 2, S], F32R)
        values = m_.sb("values", [P, DH, TILES, 2 * VD], F32R)
        q_hl = m_.sb("q_hl", [P, Q_SLOTS, 2, P], F32R)
        q_lh = m_.sb("q_lh", [P, Q_SLOTS, 2, P], F32R)
        probs = m_.sb("probs", [P, 2, 2, S])
        at_hi = m_.sb("at_hi", [P, A_SLOTS, 4, P], F32R)
        at_lo = m_.sb("at_lo", [P, A_SLOTS, 4, P], F32R)
        ident = m_.sb("ident", [P, P])
        half = m_.sb("half", [P, 1])
        lam_in = m_.sb("lam_in", [P, 4, HD])
        lam_prod = m_.sb("lam_prod", [P, 2, HD])
        lam_dot = m_.sb("lam_dot", [P, 2])
        neg_lam = m_.sb("neg_lam", [P, 1])
        tops = m_.sb("tops", [P, 4, 2, 4])
        bias = m_.sb("bias", [P, 4, 2])
        sums = m_.sb("sums", [P, 4, 2, 4])
        row_sum = m_.sb("row_sum", [P, 4, 2])
        recip = m_.sb("recip", [P, 4, 2])
        factor = m_.sb("factor", [P, 4])
        o_part = m_.sb("o_part", [P, 2, VD])
        o_row = m_.sb("o_row", [P, 2, VD])
        o_norm = m_.sb("o_norm", [P, 2, VD])
        junk = m_.sb("junk", [P, VD], BF16)
        ss = m_.sb("ss", [P, 2])
        rstd = m_.sb("rstd", [P, 2])

        consts_made, lam_loaded, lam_step = m_.sem("consts_made"), m_.sem("lam_loaded"), m_.sem("lam_step")
        keys_loaded = [m_.sem(f"keys_loaded{c}") for c in range(4)]
        values_loaded = [m_.sem(f"values_loaded{c}") for c in range(4)]
        q_loaded = [m_.sem(f"q_loaded{n}") for n in range(Q_SLOTS)]
        scored, tops_found, bias_ready, exp_done = (m_.sem(n) for n in ("scored", "tops_found", "bias_ready", "exp_done"))
        masked, summed, inverted, factor_ready, pool_scaled, pool_combined = (
            m_.sem(n) for n in ("masked", "summed", "inverted", "factor_ready", "pool_scaled", "pool_combined"))
        combined, turned, hi_done, lo_done, attended = (
            m_.sem(n) for n in ("combined", "turned", "hi_done", "lo_done", "attended"))
        o_copied, o_ready, squared, pool_step, rstd_ready, normed = (
            m_.sem(n) for n in ("o_copied", "o_ready", "squared", "pool_step", "rstd_ready", "normed"))
        stored = [m_.sem(f"stored{n}") for n in range(2)]

        def kind_done(eng, semaphore, h, event):
            eng.wait_ge(semaphore, h * total[event[0]] + ordinal[event])

        def heads(eng, perform):
            for event in order:
                if event[0] == 0:
                    perform(0, *event[1:])
            with eng.Fori(1, DH) as h:
                for ago, *event in order:
                    perform(h - ago if ago else h, *event)
            for ago, *event in order:
                if ago:
                    perform(DH - 1, *event)

        def slot_left(eng, semaphore, h, kind, turn):
            if not isinstance(h, int) or h * total[kind] + turn > 0:
                eng.wait_ge(semaphore, h * total[kind] + turn)

        with nc.Block() as block:
            @block.sync
            def _(sp):
                met = (lam_loaded, 64)
                STORE_LAG = 3

                def load_keys(h, c):
                    at = slice(4 * P * c, 4 * P * (c + 1))
                    sp.dma_start(keys[:, bass.ds(h, 1), :, at].bitcast(F32), k_s[:, bass.ds(h, 1), :, at])\
                        .then_inc(keys_loaded[c], 16)

                def load_values(h, c):
                    at = slice(4 * c, 4 * (c + 1))
                    sp.dma_start(values[:, bass.ds(h, 1), at, :].bitcast(F32),
                                 v_s[:, bass.ds(h, 1), at, :, :].rearrange("p h t a v -> p h t (a v)"))\
                        .then_inc(values_loaded[c], 16)

                def load_q(h, s):
                    slot, t = s % Q_SLOTS, tiles_in_turn[s]
                    src = q_s[t, :, bass.ds(h, 1), :, :].rearrange("p h m n -> p (h m) n")
                    sp.dma_start(q_hl[:, slot, :, :].bitcast(F32), src).then_inc(q_loaded[slot], 16)
                    sp.dma_start(q_lh[0:HD, slot, :, :].bitcast(F32), src[HD:P, :, :]).then_inc(q_loaded[slot], 16)
                    sp.dma_start(q_lh[HD:P, slot, :, :].bitcast(F32), src[0:HD, :, :]).then_inc(q_loaded[slot], 16)

                def store(h, s):
                    row = tiles_in_turn[s] * P
                    wait_apart(sp, met, (normed, h * steps + s + 1))
                    sp.dma_start(mixed[row:row + P, bass.ds(h * VD, VD)], o_norm[:, s % 2, :]).then_inc(stored[s % 2], 16)

                def head(h, first, last):
                    for s in range(steps):
                        if s + Q_SLOTS < steps or not last:
                            wait_apart(sp, met, (scored, h * total["S"] + ordinal["S", s, 1, chunks[s] - 1]))
                            if s + Q_SLOTS < steps:
                                load_q(h, s + Q_SLOTS)
                            else:
                                load_q(h + 1, s + Q_SLOTS - steps)
                        if s >= STORE_LAG:
                            store(h, s - STORE_LAG)
                        elif not first:
                            store(h - 1, steps + s - STORE_LAG)
                        if not last and s % 2 == 1:
                            c = s // 4
                            if s % 4 == 1:
                                wait_apart(sp, met, (keys_loaded[c], 16 * h + 16))
                                load_keys(h + 1, c)
                            else:
                                wait_apart(sp, met, (values_loaded[c], 16 * h + 16))
                                load_values(h + 1, c)

                for n, vec in enumerate(lambdas):
                    sp.dma_start(lam_in[:, n, :], vec.unsqueeze(0).broadcast_to([P, HD])).then_inc(lam_loaded, 16)
                for s in range(Q_SLOTS):
                    load_q(0, s)
                    load_keys(0, s)
                    load_values(0, s)
                sp.wait_ge(*met)
                head(0, True, False)
                with sp.Fori(1, DH - 1) as h:
                    head(h, False, False)
                head(DH - 1, False, True)
                for s in range(steps - STORE_LAG, steps):
                    store(DH - 1, s)
                for q in stored:
                    sp.wait_ge(q, 16 * DH * steps // 2)

            @block.gpsimd
            def _(pool):
                met = (consts_made, 3)
                make_identity(pool, ident, consts_made)
                pool.memset(half[:, :], -0.5).then_inc(consts_made, 1)
                pool.wait_ge(*met)

                def perform(h, what, s, *rest):
                    q, r = s % 2, s % 4
                    if what == "A":
                        c, = rest
                        at = slice(4 * P * c, 4 * P * c + width(s, c))
                        if c == 0:
                            wait_apart(pool, met, (factor_ready, h * steps + s + 1))
                        n = ordinal["A", s, c]
                        pool.tensor_scalar(probs[:, q, 1, at], probs[:, q, 1, at], factor[:, r:r + 1], 1.0,
                                           ALU.mult, ALU.mult).then_inc(pool_scaled, 1)
                        pool.wait_ge(pool_scaled, h * total["A"] + n)
                        pool.tensor_tensor(probs[:, q, 0, at], probs[:, q, 1, at], probs[:, q, 0, at], ALU.add)\
                            .then_inc(pool_combined, 1)
                    elif what == "N":
                        done = h * steps + s + 1
                        wait_apart(pool, met, (squared, done))
                        pool_rstd(pool, rstd[:, q:q + 1], ss[:, q:q + 1], VD, half[:, :], pool_step, done)\
                            .then_inc(rstd_ready, 1)
                        waits = [(rstd_ready, done)]
                        if s >= 2 or not isinstance(h, int) or h > 0:
                            waits.append((stored[q], 16 * (h * (steps // 2) + s // 2)))
                        wait_apart(pool, met, *waits)
                        pool.tensor_scalar(o_norm[:, q, :], o_row[:, q, :], rstd[:, q:q + 1], 1.0, ALU.mult, ALU.mult)\
                            .then_inc(normed, 1)

                heads(pool, perform)

            @block.scalar
            def _(act):
                act.wait_ge(lam_step, 3)
                act.activation(lam_dot[:, :], lam_dot[:, :], ACT.Exp).then_inc(lam_step, 1)

                def perform(h, what, s, *rest):
                    q, r = s % 2, s % 4
                    if what == "E":
                        m, c = rest
                        w = width(s, c)
                        if c == 0:
                            act.wait_ge(bias_ready, h * 2 * steps + 2 * s + m + 1)
                            if m == 0:
                                slot_left(act, turned, h, "T", ordinal["T", s - 2, chunks[s - 2] - 1] if s >= 2 else
                                          ordinal["T", steps + s - 2, chunks[steps + s - 2] - 1] - total["T"])
                        b = S_BANKS[(ordinal["S", s, m, c] - 1) % len(S_BANKS)]
                        act.activation(probs[:, q, m, 4 * P * c:4 * P * c + w], ps[:, b, 0:w], ACT.Exp,
                                       bias=bias[:, r, m:m + 1], accum_out=sums[:, r, m, c:c + 1]).then_inc(exp_done, 1)
                    elif what == "H":
                        c, = rest
                        n = ordinal["T", s, c] - 1
                        kind_done(act, turned, h, ("T", s, c))
                        slot_left(act, attended, h, "V", n + 1 - A_SLOTS)
                        w = width(s, c)
                        act.activation(at_hi[:, n % A_SLOTS, 0:w // P, :],
                                       ps[:, T_BANKS[n % 2], 0:w].rearrange("p (j n) -> p j n", n=P), ACT.Copy)\
                            .then_inc(hi_done, 1)
                    elif what == "O":
                        kind_done(act, attended, h, ("V", s, chunks[s] - 1))
                        act.activation(o_part[:, q, :], ps[:, O_BANK, VD:2 * VD], ACT.Copy,
                                       scale=recip[:, r, 0:1]).then_inc(o_copied, 1)
                    elif what == "Q":
                        act.wait_ge(o_ready, h * steps + s + 1)
                        act.activation(junk[:, :], o_row[:, q, :], ACT.Square, accum_out=ss[:, q:q + 1])\
                            .then_inc(squared, 1)

                heads(act, perform)

            @block.vector
            def _(dve):
                dve.wait_ge(lam_loaded, 64)
                dve.tensor_tensor(lam_prod[:, 0, :], lam_in[:, 0, :], lam_in[:, 1, :], ALU.mult).then_inc(lam_step, 1)
                dve.tensor_tensor(lam_prod[:, 1, :], lam_in[:, 2, :], lam_in[:, 3, :], ALU.mult).then_inc(lam_step, 1)
                dve.wait_ge(lam_step, 2)
                dve.tensor_reduce(lam_dot[:, :], lam_prod[:, :, :], AX.X, ALU.add).then_inc(lam_step, 1)
                dve.wait_ge(lam_step, 4)
                dve.scalar_tensor_tensor(neg_lam[:, :], lam_dot[:, 1:2], LAMBDA_INIT, lam_dot[:, 0:1],
                                         ALU.subtract, ALU.subtract).then_inc(lam_step, 1)
                dve.wait_ge(lam_step, 5)

                def perform(h, what, s, *rest):
                    q, r, n_chunks = s % 2, s % 4, chunks[s]
                    if what == "R":
                        m, c = rest
                        w = width(s, c)
                        b = S_BANKS[(ordinal["S", s, m, c] - 1) % len(S_BANKS)]
                        kind_done(dve, scored, h, ("S", s, m, c))
                        if c == n_chunks - 1:
                            dve.memset(ps[0:HD, b, w - HD:w], NEG).then_inc(masked, 1)
                            dve.wait_ge(masked, h * 2 * steps + 2 * s + m + 1)
                        if n_chunks == 1:
                            dve.tensor_reduce(bias[:, r, m:m + 1], ps[:, b, 0:w], AX.X, ALU.max, negate=True)\
                                .then_inc(bias_ready, 1)
                        else:
                            top = dve.tensor_reduce(tops[:, r, m, c:c + 1], ps[:, b, 0:w], AX.X, ALU.max)
                            if c == n_chunks - 1:
                                top.then_inc(tops_found, 1)
                    elif what == "M" and n_chunks > 1:
                        m, = rest
                        dve.wait_ge(tops_found, h * tops_count(steps) + tops_count(s) + m + 1)
                        dve.tensor_reduce(bias[:, r, m:m + 1], tops[:, r, m, 0:n_chunks], AX.X, ALU.max, negate=True)\
                            .then_inc(bias_ready, 1)
                    elif what == "C":
                        kind_done(dve, exp_done, h, ("E", s, 1, n_chunks - 1))
                        total_of = sums[:, r, :, 0:1]
                        if n_chunks > 1:
                            dve.tensor_reduce(row_sum[:, r, :], sums[:, r, :, 0:n_chunks], AX.X, ALU.add).then_inc(summed, 1)
                            dve.wait_ge(summed, h * tops_count(steps) // 2 + tops_count(s) // 2 + 1)
                            total_of = row_sum[:, r, :].unsqueeze(2)
                        dve.reciprocal(recip[:, r, :].unsqueeze(2), total_of).then_inc(inverted, 1)
                        dve.wait_ge(inverted, h * steps + s + 1)
                        dve.scalar_tensor_tensor(factor[:, r:r + 1], recip[:, r, 1:2], neg_lam[:, 0:1],
                                                 total_of[:, 0, :], ALU.mult, ALU.mult).then_inc(factor_ready, 1)
                    elif what == "B":
                        c, = rest
                        at = slice(4 * P * c, 4 * P * c + width(s, c))
                        if c == 1:
                            dve.wait_ge(factor_ready, h * steps + s + 1)
                        dve.scalar_tensor_tensor(probs[:, q, 0, at], probs[:, q, 1, at], factor[:, r:r + 1],
                                                 probs[:, q, 0, at], ALU.mult, ALU.add).then_inc(combined, 1)
                    elif what == "L":
                        c, = rest
                        n = ordinal["T", s, c] - 1
                        w = width(s, c)
                        kind_done(dve, hi_done, h, ("T", s, c))
                        dve.tensor_tensor(at_lo[:, n % A_SLOTS, 0:w // P, :],
                                          ps[:, T_BANKS[n % 2], 0:w].rearrange("p (j n) -> p j n", n=P),
                                          at_hi[:, n % A_SLOTS, 0:w // P, :].bitcast(F32), ALU.subtract)\
                            .then_inc(lo_done, 1)
                    elif what == "P":
                        dve.wait_ge(o_copied, h * steps + s + 1)
                        if s >= 2 or not isinstance(h, int) or h > 0:
                            dve.wait_ge(normed, h * steps + s - 1)
                        dve.scalar_tensor_tensor(o_row[:, q, :], ps[:, O_BANK, 0:VD], recip[:, r, 0:1],
                                                 o_part[:, q, :], ALU.mult, ALU.add).then_inc(o_ready, 1)

                heads(dve, perform)

            @block.tensor
            def _(pe):
                pe.wait_ge(consts_made, 2)

                def perform(h, what, s, *rest):
                    if what == "S":
                        m, c = rest
                        n, w = ordinal["S", s, m, c] - 1, width(s, c)
                        if m == 0 and c == 0:
                            slot_uses = steps // Q_SLOTS
                            pe.wait_ge(q_loaded[s % Q_SLOTS], 48 * (h * slot_uses + s // Q_SLOTS + 1))
                        if m == 0 and s == chunks.index(c + 1):
                            pe.wait_ge(keys_loaded[c], 16 * h + 16)
                        slot_left(pe, exp_done, h, "S", n + 1 - len(S_BANKS))
                        b = S_BANKS[n % len(S_BANKS)]
                        for j, stack in enumerate((q_hl, q_lh)):
                            last = pe.matmul(ps[:, b, 0:w], stack[:, s % Q_SLOTS, m, :],
                                             keys[:, bass.ds(h, 1), m, 4 * P * c:4 * P * c + w].squeeze(1),
                                             start=(j == 0), stop=(j == 1))
                        last.then_inc(scored, 1)
                    elif what == "T":
                        c, = rest
                        n, w = ordinal["T", s, c] - 1, width(s, c)
                        kind_done(pe, {"A": pool_combined, "B": combined}[COMBINED_BY[c]], h, (COMBINED_BY[c], s, c))
                        slot_left(pe, lo_done, h, "L", n + 1 - len(T_BANKS))
                        for j in range(w // P):
                            at = 4 * P * c + j * P
                            last = pe.transpose(ps[:, T_BANKS[n % 2], j * P:(j + 1) * P],
                                                probs[:, s % 2, 0, at:at + P], ident[:, :])
                        last.then_inc(turned, 1)
                    elif what == "V":
                        c, = rest
                        n = ordinal["V", s, c] - 1
                        kind_done(pe, lo_done, h, ("L", s, c))
                        if s == chunks.index(c + 1):
                            pe.wait_ge(values_loaded[c], 16 * h + 16)
                        if c == 0 and (s > 0 or not isinstance(h, int) or h > 0):
                            pe.wait_ge(o_ready, h * steps + s)
                        for j in range(width(s, c) // P):
                            for i, a in enumerate((at_hi, at_lo)):
                                last = pe.matmul(ps[:, O_BANK, 0:2 * VD], a[:, n % A_SLOTS, j, :],
                                                 values[:, bass.ds(h, 1), 4 * c + j, :].squeeze(1),
                                                 start=(c == 0 and j == 0 and i == 0),
                                                 stop=(4 * c + j == tiles_in_turn[s] and i == 1))
                        last.then_inc(attended, 1)

                heads(pe, perform)
        m_.end()


def out_proj(nc, x, swa_t, mixed, w_out, subln, g_post, g_ffn, x_mid, h_s):
    y_order, t_order = [], [("m", 0)]
    for t in range(TILES + 1):
        if t < TILES:
            y_order += [("y", t, 0), ("y", t, 1)]
        if t + 1 < TILES:
            t_order.append(("m", t + 1))
        if t >= 1:
            t_order += [("h", t - 1, 0), ("h", t - 1, 1)]
    y_banks, t_banks = Banks([0, 1, 2, 3], y_order), Banks([4, 5, 6], t_order)
    SC = QA // P
    HW = D // 2

    with ExitStack() as ctx:
        m = Memory(nc, ctx, "op")
        ps = m.psum()
        w_hi = m.sb("w_hi", [P, KC, D], F32R)
        w_lo = m.sb("w_lo", [P, KC, D], F32R)
        w_raw = m.sb("w_raw", [P, 4, D])
        sub_col = m.sb("sub_col", [P, 1])
        post_row = m.sb("post_row", [P, D])
        ffn_row = m.sb("ffn_row", [P, D])
        ident = m.sb("ident", [P, P])
        half = m.sb("half", [P, 1])
        xb = m.sb("x", [P, 2, D])
        swa_in = m.sb("swa_in", [P, 2, SC, P])
        mix_in = m.sb("mix_in", [P, 2, DW])
        mt_hi = m.sb("mt_hi", [P, 2, KC, P], F32R)
        mt_lo = m.sb("mt_lo", [P, 2, KC, P], F32R)
        y_junk = m.sb("y_junk", [P, D], BF16)
        x_junk = m.sb("x_junk", [P, D], BF16)
        y_ss = m.sb("y_ss", [P, 2, 2])
        y_rstd = m.sb("y_rstd", [P, 2])
        x_ss = m.sb("x_ss", [P, 2])
        x_rstd = m.sb("x_rstd", [P, 2])
        y_norm = m.sb("y_norm", [P, 2, D])
        x_new = m.sb("x_new", [P, 2, D])
        h_row = m.sb("h_row", [P, D])
        ht = m.sb("ht", [P, 2, KC, 2, P], F32R)

        w_loaded = [m.sem(f"w_loaded{n}") for n in range(4)]
        w_hi_done, w_lo_done = m.sem("w_hi_done"), m.sem("w_lo_done")
        consts_loaded, consts_made, sub_scaled = m.sem("consts_loaded"), m.sem("consts_made"), m.sem("sub_scaled")
        in_loaded = [m.sem(f"in_loaded{n}") for n in range(2)]
        x_loaded = [m.sem(f"x_loaded{n}") for n in range(2)]
        m_turned, swa_hi, swa_lo, m_hi, m_lo = (m.sem(n) for n in ("m_turned", "swa_hi", "swa_lo", "m_hi", "m_lo"))
        multiplied, y_squared, y_normed, pool_step, y_rstd_ready = (
            m.sem(n) for n in ("multiplied", "y_squared", "y_normed", "pool_step", "y_rstd_ready"))
        x_added, x_squared, x_rstd_ready, h_ready = (m.sem(n) for n in ("x_added", "x_squared", "x_rstd_ready", "h_ready"))
        h_turned, h_hi, h_lo = (m.sem(n) for n in ("h_turned", "h_hi", "h_lo"))
        x_stored = [m.sem(f"x_stored{n}") for n in range(2)]
        h_stored = [m.sem(f"h_stored{n}") for n in range(2)]
        read_out = {"y": (y_normed, lambda t, n: 2 * t + n + 1), "m": (m_lo, lambda t: t + 1),
                    "h": (h_lo, lambda t, n: 2 * t + n + 1)}

        with nc.Block() as block:
            @block.sync
            def _(sp):
                met = (consts_loaded, 48)

                def load_in(k, i, ahead):
                    p = k % 2
                    at = steady(lambda t: (t + ahead) * P, k, i)
                    sp.dma_start(swa_in[:, p, :, :], swa_t[:, :, bass.ds(at, P)]).then_inc(in_loaded[p], 16)
                    sp.dma_start(mix_in[:, p, :], mixed[bass.ds(at, P), :]).then_inc(in_loaded[p], 16)

                def store_tile(sp, k, i):
                    p = k % 2
                    at = steady(lambda t: t * P, k, i)
                    wait_apart(sp, (consts_loaded, 48), (x_added, steady(lambda t: t + 1, k, i)))
                    sp.dma_start(x_mid[bass.ds(at, P), :], x_new[:, p, :]).then_inc(x_stored[p], 16)
                    wait_apart(sp, (consts_loaded, 48), (h_lo, steady(lambda t: 2 * t + 2, k, i)))
                    sp.dma_start(h_s[:, :, :, bass.ds(at, P)], ht[:, p, :, :, :].bitcast(F32)).then_inc(h_stored[p], 16)

                with nc.allow_non_contiguous_dma(reason="gains by column"):
                    sp.dma_start(sub_col[:, :], subln.rearrange("(c p) -> p c", p=P)).then_inc(consts_loaded, 16)
                for n in range(2):
                    load_in(n, None, 0)
                for c in range(KC):
                    if c >= 4:
                        sp.wait_ge(w_lo_done, c - 3)
                    sp.dma_start(w_raw[:, c % 4, :], w_out[c * P:(c + 1) * P, :]).then_inc(w_loaded[c % 4], 16)
                    if c == 3:
                        sp.dma_start(post_row[:, :], g_post.unsqueeze(0).broadcast_to([P, D])).then_inc(consts_loaded, 16)
                        sp.dma_start(ffn_row[:, :], g_ffn.unsqueeze(0).broadcast_to([P, D])).then_inc(consts_loaded, 16)
                for n in range(2):
                    sp.dma_start(xb[:, n, :], x[n * P:(n + 1) * P, :]).then_inc(x_loaded[n], 16)
                for k, i in tiles(sp):
                    p = k % 2
                    if k + 2 < TILES:
                        wait_apart(sp, met, (swa_lo, steady(lambda t: t + 1, k, i)), (m_turned, steady(lambda t: t + 1, k, i)))
                        load_in(k, i, 2)
                    if k >= 1:
                        store_tile(sp, k - 1, i)
                        if k + 1 < TILES:
                            at = steady(lambda t: (t + 1) * P, k, i)
                            sp.dma_start(xb[:, 1 - p, :], x[bass.ds(at, P), :]).then_inc(x_loaded[1 - p], 16)
                store_tile(sp, TILES - 1, None)
                for s in x_stored + h_stored:
                    sp.wait_ge(s, 16 * TILES // 2)

            @block.gpsimd
            def _(pool):
                make_identity(pool, ident, consts_made)
                pool.memset(half[:, :], -0.5).then_inc(consts_made, 1)
                pool.wait_ge(consts_made, 3)

                def split_swa(k, i):
                    q = k % 2
                    pool.wait_ge(swa_hi, steady(lambda t: t + 1, k, i))
                    pool.tensor_tensor(mt_lo[:, q, 0:SC, :], swa_in[:, q, :, :], mt_hi[:, q, 0:SC, :].bitcast(F32),
                                       ALU.subtract).then_inc(swa_lo, 1)

                def y_rstd_of(k, i):
                    q = k % 2
                    pool.wait_ge(y_squared, steady(lambda t: 2 * t + 2, k, i))
                    if k >= 2:
                        pool.wait_ge(y_normed, steady(lambda t: 2 * t - 2, k, i))
                    pool.tensor_tensor(y_rstd[:, q:q + 1], y_ss[:, q, 0:1], y_ss[:, q, 1:2], ALU.add).then_inc(pool_step, 1)
                    wait_apart(pool, (consts_made, 3), (pool_step, steady(lambda t: 3 * t + 1, k, i)))
                    pool_rstd(pool, y_rstd[:, q:q + 1], y_rstd[:, q:q + 1], D, half[:, :], pool_step,
                              steady(lambda t: 3 * t + 2, k, i)).then_inc(y_rstd_ready, 1)

                def add_x(k, i):
                    q = k % 2
                    pool.wait_ge(x_loaded[q], steady(lambda t: 16 * (t // 2 + 1), k, i))
                    if k >= 2:
                        pool.wait_ge(x_stored[q], steady(lambda t: 16 * (t // 2), k, i))
                        pool.wait_ge(h_ready, steady(lambda t: t - 1, k, i))
                    pool.wait_ge(y_normed, steady(lambda t: 2 * t + 2, k, i))
                    pool.tensor_tensor(x_new[:, q, :], y_norm[:, q, :], xb[:, q, :], ALU.add).then_inc(x_added, 1)

                def x_rstd_of(k, i):
                    q = k % 2
                    waits = [(x_squared, steady(lambda t: t + 1, k, i))]
                    if k >= 2:
                        waits.append((h_ready, steady(lambda t: t - 1, k, i)))
                    wait_apart(pool, (consts_made, 3), *waits)
                    pool_rstd(pool, x_rstd[:, q:q + 1], x_ss[:, q:q + 1], D, half[:, :], pool_step,
                              steady(lambda t: 3 * t + 3, k, i)).then_inc(x_rstd_ready, 1)

                split_swa(0, None)
                for k, i in tiles(pool):
                    if k >= 1:
                        y_rstd_of(k - 1, i)
                        add_x(k - 1, i)
                    if k + 1 < TILES:
                        split_swa(k + 1, i)
                    if k >= 1:
                        x_rstd_of(k - 1, i)
                y_rstd_of(TILES - 1, None)
                add_x(TILES - 1, None)
                x_rstd_of(TILES - 1, None)

            @block.scalar
            def _(act):
                def hi_m(k, i):
                    q = k % 2
                    act.wait_ge(in_loaded[q], steady(lambda t: 32 * (t // 2 + 1), k, i))
                    if k >= 2:
                        act.wait_ge(multiplied, steady(lambda t: 2 * t - 2, k, i))
                    act.activation(mt_hi[:, q, 0:SC, :], swa_in[:, q, :, :], ACT.Copy).then_inc(swa_hi, 1)
                    act.wait_ge(m_turned, steady(lambda t: t + 1, k, i))
                    act.activation(mt_hi[:, q, SC:KC, :], ps[:, t_banks.bank("m", k), :].rearrange("p (c n) -> p c n", n=P),
                                   ACT.Copy).then_inc(m_hi, 1)

                def square_y(k, i):
                    q = k % 2
                    for n in range(2):
                        act.wait_ge(multiplied, steady(lambda t: 2 * t + n + 1, k, i))
                        if k >= 1 and n == 0:
                            act.wait_ge(y_rstd_ready, steady(lambda t: t, k, i))
                        act.activation(y_junk[:, n * HW:(n + 1) * HW], ps[:, y_banks.bank("y", k, n), :], ACT.Square,
                                       accum_out=y_ss[:, q, n:n + 1]).then_inc(y_squared, 1)

                def square_x(k, i):
                    q = k % 2
                    act.wait_ge(x_added, steady(lambda t: t + 1, k, i))
                    if k >= 1:
                        act.wait_ge(x_rstd_ready, steady(lambda t: t, k, i))
                    act.activation(x_junk[:, :], x_new[:, q, :], ACT.Square, accum_out=x_ss[:, q:q + 1]).then_inc(x_squared, 1)

                def hi_h(k, i):
                    q = k % 2
                    for n in range(2):
                        act.wait_ge(h_turned, steady(lambda t: 2 * t + n + 1, k, i))
                        if k >= 2 and n == 0:
                            act.wait_ge(h_stored[q], steady(lambda t: 16 * (t // 2), k, i))
                        act.activation(ht[:, q, 4 * n:4 * n + 4, 0, :],
                                       ps[:, t_banks.bank("h", k, n), :].rearrange("p (c n) -> p c n", n=P), ACT.Copy)\
                            .then_inc(h_hi, 1)

                act.wait_ge(consts_loaded, 48)
                act.wait_ge(sub_scaled, 1)
                hi_m(0, None)
                for c in range(KC):
                    act.wait_ge(w_loaded[c % 4], 16 * (c // 4 + 1))
                    act.activation(w_hi[:, c, :], w_raw[:, c % 4, :], ACT.Copy, scale=1.0 if c < SC else sub_col[:, 0:1])\
                        .then_inc(w_hi_done, 1)
                for k, i in tiles(act):
                    if k >= 1:
                        square_y(k - 1, i)
                    if k + 1 < TILES:
                        hi_m(k + 1, i)
                    if k >= 1:
                        square_x(k - 1, i)
                        hi_h(k - 1, i)
                square_y(TILES - 1, None)
                square_x(TILES - 1, None)
                hi_h(TILES - 1, None)

            @block.vector
            def _(dve):
                def lo_m(k, i):
                    q = k % 2
                    dve.wait_ge(m_hi, steady(lambda t: t + 1, k, i))
                    dve.tensor_tensor(mt_lo[:, q, SC:KC, :], ps[:, t_banks.bank("m", k), :].rearrange("p (c n) -> p c n", n=P),
                                      mt_hi[:, q, SC:KC, :].bitcast(F32), ALU.subtract).then_inc(m_lo, 1)

                def norm_y(k, i):
                    q = k % 2
                    dve.wait_ge(y_rstd_ready, steady(lambda t: t + 1, k, i))
                    if k >= 2:
                        dve.wait_ge(x_added, steady(lambda t: t - 1, k, i))
                    for n in range(2):
                        at = slice(n * HW, (n + 1) * HW)
                        dve.scalar_tensor_tensor(y_norm[:, q, at], ps[:, y_banks.bank("y", k, n), :], y_rstd[:, q:q + 1],
                                                 post_row[:, at], ALU.mult, ALU.mult).then_inc(y_normed, 1)

                def norm_x(k, i):
                    q = k % 2
                    dve.wait_ge(x_rstd_ready, steady(lambda t: t + 1, k, i))
                    if k >= 1:
                        dve.wait_ge(h_turned, steady(lambda t: 2 * t, k, i))
                    dve.scalar_tensor_tensor(h_row[:, :], x_new[:, q, :], x_rstd[:, q:q + 1], ffn_row[:, :],
                                             ALU.mult, ALU.mult).then_inc(h_ready, 1)

                def lo_h(k, i):
                    q = k % 2
                    for n in range(2):
                        dve.wait_ge(h_hi, steady(lambda t: 2 * t + n + 1, k, i))
                        dve.tensor_tensor(ht[:, q, 4 * n:4 * n + 4, 1, :],
                                          ps[:, t_banks.bank("h", k, n), :].rearrange("p (c n) -> p c n", n=P),
                                          ht[:, q, 4 * n:4 * n + 4, 0, :].bitcast(F32), ALU.subtract).then_inc(h_lo, 1)

                dve.wait_ge(consts_loaded, 48)
                dve.tensor_scalar(sub_col[:, :], sub_col[:, :], 1.0 - LAMBDA_INIT, None, ALU.mult).then_inc(sub_scaled, 1)
                dve.wait_ge(sub_scaled, 1)
                lo_m(0, None)
                for c in range(KC):
                    dve.wait_ge(w_hi_done, c + 1)
                    dve.scalar_tensor_tensor(w_lo[:, c, :], w_raw[:, c % 4, :], 1.0 if c < SC else sub_col[:, 0:1],
                                             w_hi[:, c, :].bitcast(F32), ALU.mult, ALU.subtract).then_inc(w_lo_done, 1)
                for k, i in tiles(dve):
                    if k >= 1:
                        norm_y(k - 1, i)
                    if k + 1 < TILES:
                        lo_m(k + 1, i)
                    if k >= 1:
                        norm_x(k - 1, i)
                        lo_h(k - 1, i)
                norm_y(TILES - 1, None)
                norm_x(TILES - 1, None)
                lo_h(TILES - 1, None)

            @block.tensor
            def _(pe):
                def turn_m(k, i):
                    pe.wait_ge(in_loaded[k % 2], steady(lambda t: 32 * (t // 2 + 1), k, i))
                    t_banks.free(pe, read_out, k, i, "m")
                    for j in range(DW // P):
                        last = pe.transpose(ps[:, t_banks.bank("m", k), j * P:(j + 1) * P],
                                            mix_in[:, k % 2, j * P:(j + 1) * P], ident[:, :])
                    last.then_inc(m_turned, 1)

                def multiply(n, k, i):
                    q = k % 2
                    if n == 0:
                        pe.wait_ge(swa_lo, steady(lambda t: t + 1, k, i))
                    y_banks.free(pe, read_out, k, i, "y", n)
                    for c in range(KC):
                        if n == 0 and c == SC:
                            pe.wait_ge(m_lo, steady(lambda t: t + 1, k, i))
                        if k == 0 and n == 0:
                            pe.wait_ge(w_lo_done, c + 1)
                        for j, (lhs, rhs) in enumerate(((mt_hi, w_hi), (mt_hi, w_lo), (mt_lo, w_hi))):
                            last = pe.matmul(ps[:, y_banks.bank("y", k, n), :], lhs[:, q, c, :],
                                             rhs[:, c, n * HW:(n + 1) * HW],
                                             start=(c == 0 and j == 0), stop=(c == KC - 1 and j == 2))
                    last.then_inc(multiplied, 1)

                def turn_h(k, i):
                    pe.wait_ge(h_ready, steady(lambda t: t + 1, k, i))
                    for n in range(2):
                        t_banks.free(pe, read_out, k, i, "h", n)
                        for j in range(4):
                            at = (4 * n + j) * P
                            last = pe.transpose(ps[:, t_banks.bank("h", k, n), j * P:(j + 1) * P], h_row[:, at:at + P],
                                                ident[:, :])
                        last.then_inc(h_turned, 1)

                pe.wait_ge(consts_made, 2)
                turn_m(0, None)
                for k, i in tiles(pe):
                    multiply(0, k, i)
                    if k + 1 < TILES:
                        turn_m(k + 1, i)
                    multiply(1, k, i)
                    if k >= 1:
                        turn_h(k - 1, i)
                turn_h(TILES - 1, None)
        m.end()


def ffn(nc, h_s, x_mid, w_gate, w_up, w_down, g_post, out):
    HW = D // 2
    UP = 2 * FC
    DOWN = FC
    UNITS = UP + DOWN
    R = 4
    slot_uses = [len(range(s, UNITS, R)) for s in range(R)]
    ENDS = (UP + DOWN // 2 - 1, UNITS - 1)
    USED = UNITS - len(ENDS)

    with ExitStack() as ctx:
        m = Memory(nc, ctx, "ff")
        ps = m.psum()
        h_hl = m.sb("h_hl", [P, KC, 2, TB], F32R)
        g_hi = m.sb("g_hi", [P, FC, TB], F32R)
        g_lo = m.sb("g_lo", [P, FC, TB], F32R)
        w_raw = m.sb("w_raw", [P, R, D])
        w_hi = m.sb("w_hi", [P, R, D], F32R)
        w_lo = m.sb("w_lo", [P, R, D], F32R)
        y = m.sb("y", [P, BT, D])
        xm = m.sb("xm", [P, D])
        post_row = m.sb("post_row", [P, D])
        silu = m.sb("silu", [P, 2, TB])
        gated = m.sb("gated", [P, 2, TB])
        junk = m.sb("junk", [P, BT, HW], BF16)
        half = m.sb("half", [P, BT])
        ss = m.sb("ss", [P, 2, BT])
        rstd = m.sb("rstd", [P, BT])

        consts_made, post_loaded = m.sem("consts_made"), m.sem("post_loaded")
        h_loaded = m.sem("h_loaded")
        w_loaded = [m.sem(f"w_loaded{n}") for n in range(R)]
        w_hi_done, w_split, unit_used = m.sem("w_hi_done"), m.sem("w_split"), m.sem("unit_used")
        silu_done, gate_done, g_hi_done, g_split = (m.sem(n) for n in ("silu_done", "gate_done", "g_hi_done", "g_split"))
        y_done, y_squared, y_copied = m.sem("y_done"), m.sem("y_squared"), m.sem("y_copied")
        pool_step, rstd_ready, y_normed = m.sem("pool_step"), m.sem("rstd_ready"), m.sem("y_normed")
        xm_loaded, x_added, stored = m.sem("xm_loaded"), m.sem("x_added"), m.sem("stored")

        def used(b, u):
            if u in ENDS:
                return y_done, (b * 2 + ENDS.index(u) + 1) * BT
            return unit_used, b * USED + u + 1 - sum(e < u for e in ENDS)

        def blocks(eng, body):
            body(0, True, False)
            with eng.Fori(1, BLOCKS - 1) as b:
                body(b, False, False)
            body(BLOCKS - 1, False, True)

        def pairs(eng, body):
            body(0, True)
            with eng.Fori(1, FC // 2) as j:
                body(j, False)

        with nc.Block() as block:
            @block.sync
            def _(sp):
                met = (post_loaded, 16)

                def load_h(b):
                    sp.dma_start(h_hl[:, :, :, :].bitcast(F32), h_s[:, :, :, bass.ds(b * TB, TB)]).then_inc(h_loaded, 16)

                def body(b, first, last):
                    def up_pair(j, peeled):
                        for u in range(4):
                            w = (w_gate, w_up)[u % 2]
                            wait_apart(sp, met, (w_split, b * UNITS if peeled else b * UNITS + 4 * j + u - R + 1))
                            sp.dma_start(w_raw[:, u, :], w[bass.ds(2 * j + u // 2, 1), :, :].rearrange("f p n -> p (f n)"))\
                                .then_inc(w_loaded[u], 16)

                    pairs(sp, up_pair)
                    for d in range(DOWN):
                        u = UP + d
                        wait_apart(sp, met, (w_split, b * UNITS + u - R + 1))
                        sp.dma_start(w_raw[:, u % R, :], w_down[d // (FC // 2), d % (FC // 2), :, :])\
                            .then_inc(w_loaded[u % R], 16)
                        if d == R + 2 and not last:
                            wait_apart(sp, met, (unit_used, b * USED + UP))
                            load_h(b + 1)

                sp.dma_start(post_row[:, :], g_post.unsqueeze(0).broadcast_to([P, D])).then_inc(post_loaded, 16)
                load_h(0)
                sp.wait_ge(post_loaded, 16)
                blocks(sp, body)

            @block.gpsimd
            def _(pool):
                met = (consts_made, 1)
                pool.memset(half[:, :], -0.5).then_inc(consts_made, 1)
                pool.wait_ge(*met)
                pool.memset(junk[:, 0, 0:1], 0.0).then_inc(g_split, 1)

                def body(b, first, last):
                    def split_g(f, q):
                        wait_apart(pool, met, (g_hi_done, b * FC + f + 1))
                        pool.tensor_tensor(g_lo[:, bass.ds(f, 1), :].squeeze(1), gated[:, q, :],
                                           g_hi[:, bass.ds(f, 1), :].squeeze(1).bitcast(F32), ALU.subtract).then_inc(g_split, 1)

                    with pool.Fori(0, FC // 2) as j:
                        for q in range(2):
                            split_g(2 * j + q, q)
                    pool.wait_ge(y_squared, (b + 1) * 2 * BT)
                    if not first:
                        pool.wait_ge(y_normed, b * BT)
                    pool.tensor_tensor(rstd[:, :], ss[:, 0, :], ss[:, 1, :], ALU.add).then_inc(pool_step, 1)
                    wait_apart(pool, met, (pool_step, 2 * b + 1))
                    pool_rstd(pool, rstd[:, :], rstd[:, :], D, half[:, :], pool_step, 2 * b + 2).then_inc(rstd_ready, 1)
                    for j in range(BT):
                        row = b * TB + j * P
                        wait_apart(pool, met, (x_added, b * BT + j))
                        pool.dma_start(xm[:, :], x_mid[bass.ds(row, P), :]).then_inc(xm_loaded, 16)
                        pool.wait_ge(xm_loaded, 16 * (b * BT + j + 1))
                        pool.wait_ge(y_normed, b * BT + j + 1)
                        pool.tensor_tensor(y[:, j, :], y[:, j, :], xm[:, :], ALU.add).then_inc(x_added, 1)
                        wait_apart(pool, met, (x_added, b * BT + j + 1))
                        pool.dma_start(out[bass.ds(row, P), :], y[:, j, :]).then_inc(stored, 16)

                blocks(pool, body)
                pool.wait_ge(stored, 16 * TILES)

            @block.scalar
            def _(act):
                def hi_unit(b, slot, turn, semaphore, count):
                    act.wait_ge(w_loaded[slot], 16 * (b * slot_uses[slot] + turn + 1))
                    act.wait_ge(semaphore, count)
                    act.activation(w_hi[:, slot, :], w_raw[:, slot, :], ACT.Copy).then_inc(w_hi_done, 1)

                def silu_of(b, f, q):
                    act.wait_ge(unit_used, b * USED + 2 * f + 1)
                    act.activation(silu[:, q, :], ps[:, 2 * q, :], ACT.Silu).then_inc(silu_done, 1)
                    wait_apart(act, (post_loaded, 16), (gate_done, b * FC + f + 1), (y_done, b * 2 * BT))
                    act.activation(g_hi[:, bass.ds(f, 1), :].squeeze(1), gated[:, q, :], ACT.Copy).then_inc(g_hi_done, 1)

                def square(b, n):
                    for j in range(BT):
                        act.wait_ge(y_done, b * 2 * BT + n * BT + j + 1)
                        if j == 0:
                            act.wait_ge(y_squared, (b * 2 + n) * BT)
                            if n == 0:
                                act.wait_ge(rstd_ready, b)
                        act.activation(junk[:, j, :], ps[:, (4 if n == 0 else 0) + j, :], ACT.Square,
                                       accum_out=ss[:, n, j:j + 1]).then_inc(y_squared, 1)

                def body(b, first, last):
                    def up_pair(j, peeled):
                        for u in range(4):
                            if not peeled:
                                hi_unit(b, u, j, unit_used, b * USED + 4 * j + u - R + 1)
                            elif u > 0:
                                hi_unit(b, u, j, y_done, b * 2 * BT)
                            if u % 2 == 1 and not peeled:
                                silu_of(b, 2 * j - 2 + u // 2, u // 2)

                    pairs(act, up_pair)
                    for d in range(DOWN):
                        u = UP + d
                        hi_unit(b, u % R, u // R, *used(b, u - R))
                        if d in (1, 3):
                            silu_of(b, FC - 2 + d // 2, d // 2)
                        if d == FC // 2 + R - 1:
                            square(b, 0)
                    if not last:
                        hi_unit(b + 1, 0, 0, *used(b, UNITS - 2))
                    square(b, 1)

                act.wait_ge(post_loaded, 16)
                act.wait_ge(w_loaded[0], 16)
                act.activation(w_hi[:, 0, :], w_raw[:, 0, :], ACT.Copy).then_inc(w_hi_done, 1)
                blocks(act, body)

            @block.vector
            def _(dve):
                def split_unit(slot, count):
                    dve.wait_ge(w_hi_done, count)
                    dve.tensor_tensor(w_lo[:, slot, :], w_raw[:, slot, :], w_hi[:, slot, :].bitcast(F32), ALU.subtract)\
                        .then_inc(w_split, 1)

                def gate(b, f, q):
                    dve.wait_ge(silu_done, b * FC + f + 1)
                    dve.wait_ge(unit_used, b * USED + 2 * f + 2)
                    dve.wait_ge(g_split, b * FC + f - q + 1)
                    dve.tensor_tensor(gated[:, q, :], silu[:, q, :], ps[:, 2 * q + 1, :], ALU.mult).then_inc(gate_done, 1)

                def copy_y(b, n):
                    for j in range(BT):
                        dve.wait_ge(y_squared, b * 2 * BT + n * BT + j + 1)
                        if n == 0 and j == 0:
                            dve.wait_ge(stored, 16 * BT * b)
                        dve.tensor_copy(y[:, j, n * HW:(n + 1) * HW], ps[:, (4 if n == 0 else 0) + j, :]).then_inc(y_copied, 1)

                def norm_y(b, j):
                    if j == 0:
                        dve.wait_ge(rstd_ready, b + 1)
                        dve.wait_ge(y_copied, (b + 1) * 2 * BT)
                    dve.scalar_tensor_tensor(y[:, j, :], y[:, j, :], rstd[:, j:j + 1], post_row[:, :], ALU.mult, ALU.mult)\
                        .then_inc(y_normed, 1)

                def body(b, first, last):
                    def up_pair(j, peeled):
                        for u in range(4):
                            if not (peeled and u == 0):
                                split_unit(u, b * UNITS + 4 * j + u + 1)
                            if u % 2 == 1 and not peeled:
                                gate(b, 2 * j - 2 + u // 2, u // 2)
                            if peeled and not first:
                                norm_y(b - 1, u)

                    pairs(dve, up_pair)
                    for d in range(DOWN):
                        u = UP + d
                        split_unit(u % R, b * UNITS + u + 1)
                        if d in (1, 3):
                            gate(b, FC - 2 + d // 2, d // 2)
                        if d == FC // 2 + R - 1:
                            copy_y(b, 0)
                    if not last:
                        split_unit(0, (b + 1) * UNITS + 1)
                    copy_y(b, 1)

                dve.wait_ge(post_loaded, 16)
                split_unit(0, 1)
                blocks(dve, body)
                for j in range(BT):
                    norm_y(BLOCKS - 1, j)

            @block.tensor
            def _(pe):
                def multiply_up(b, j, u, peeled):
                    pe.wait_ge(w_split, b * UNITS + 4 * j + u + 1)
                    if peeled:
                        pe.wait_ge(y_copied, b * 2 * BT)
                    else:
                        pe.wait_ge(gate_done, b * FC + 2 * j + u // 2 - 1)
                    for c in range(KC):
                        at = slice(c * P, (c + 1) * P)
                        for n, (w, a) in enumerate(((w_hi, 0), (w_hi, 1), (w_lo, 0))):
                            last = pe.matmul(ps[:, u, :], w[:, u, at], h_hl[:, c, a, :],
                                             start=(c == 0 and n == 0), stop=(c == KC - 1 and n == 2))
                    last.then_inc(unit_used, 1)

                pe.wait_ge(post_loaded, 16)

                def body(b, first, last):
                    pe.wait_ge(h_loaded, 16 * (b + 1))

                    def up_pair(j, peeled):
                        for u in range(4):
                            multiply_up(b, j, u, peeled)

                    pairs(pe, up_pair)
                    for d in range(DOWN):
                        u = UP + d
                        n, pair = d // (FC // 2), d % (FC // 2)
                        pe.wait_ge(w_split, b * UNITS + u + 1)
                        if pair == 0:
                            if n == 0:
                                pe.wait_ge(y_copied, b * 2 * BT)
                            else:
                                pe.wait_ge(gate_done, (b + 1) * FC)
                        if n == 0:
                            pe.wait_ge(g_split, b * FC + 2 * pair + 2 + 1)
                        for j in range(BT):
                            bank = (4 if n == 0 else 0) + j
                            for e in range(2):
                                f = 2 * pair + e
                                rhs = slice(e * HW, (e + 1) * HW)
                                for i, (g, w) in enumerate(((g_hi, w_hi), (g_hi, w_lo), (g_lo, w_hi))):
                                    last = pe.matmul(ps[:, bank, :], g[:, f, j * P:(j + 1) * P], w[:, u % R, rhs],
                                                     start=(f == 0 and i == 0), stop=(f == FC - 1 and i == 2))
                            if pair == FC // 2 - 1:
                                last.then_inc(y_done, 1)
                        if pair < FC // 2 - 1:
                            last.then_inc(unit_used, 1)

                blocks(pe, body)
        m.end()


def hybrid_block(nc, x, w_in, sinks, lambda_q1, lambda_k1, lambda_q2, lambda_k2, subln, w_out, g_mix_pre, g_mix_post,
                 g_ffn_pre, g_ffn_post, w_gate, w_up, w_down, rope, out):
    def scratch(name, shape):
        return nc.dram_tensor(name, shape, F32, kind="Internal").ap()

    swa_t = scratch("swa_t", (P, QA // P, S))
    q_s = scratch("q_s", (TILES, P, DH, 2, P))
    k_s = scratch("k_s", (P, DH, 2, S))
    v_s = scratch("v_s", (P, DH, TILES, 2, P))
    mixed = scratch("mixed", (S, DW))
    x_mid = scratch("x_mid", (S, D))
    h_s = scratch("h_s", (P, KC, 2, S))
    swa_phase(nc, x, w_in, g_mix_pre, sinks, rope, swa_t)
    diff_proj(nc, x, w_in, g_mix_pre, rope, q_s, k_s, v_s)
    diff_attn(nc, q_s, k_s, v_s, [lambda_q1, lambda_k1, lambda_q2, lambda_k2], mixed)
    out_proj(nc, x, swa_t, mixed, w_out, subln, g_mix_post, g_ffn_pre, x_mid, h_s)
    ffn(nc, h_s, x_mid, w_gate, w_up, w_down, g_ffn_post, out)


def rope_table():
    inv = 1.0 / (10000.0 ** (np.arange(0, HD, 2, dtype=np.float32) / HD))
    angle = np.arange(S, dtype=np.float32)[:, None] * inv.astype(np.float32)[None, :]
    cos, sin = np.cos(angle), np.sin(angle)
    table = np.concatenate([cos, cos, -sin, sin], axis=1).astype(np.float32)
    return np.concatenate([table, table * np.float32(SCALE)], axis=1)


_INS = ['x', 'w_in', 'swa_sinks', 'diff_lambda_q1', 'diff_lambda_k1', 'diff_lambda_q2', 'diff_lambda_k2', 'diff_subln',
        'w_out', 'norm_mix_pre', 'norm_mix_post', 'norm_ffn_pre', 'norm_ffn_post', 'w_gate', 'w_up', 'w_down']


def kernel(**inputs):
    import numpy as _np
    import concourse.bacc as _bacc
    from concourse import mybir as _mybir
    from concourse.bass_utils import run_bass_kernel_spmd as _run

    laid_out = {name: _np.asarray(inputs[name])[0] for name in _INS}
    for name in ('w_gate', 'w_up'):
        laid_out[name] = laid_out[name].reshape(KC, P, FC, P).transpose(2, 1, 0, 3).reshape(FC, P, D)
    laid_out['w_down'] = laid_out['w_down'].reshape(FC // 2, 2, P, 2, D // 2).transpose(3, 0, 2, 1, 4)\
        .reshape(2, FC // 2, P, D)
    laid_out['rope'] = rope_table()

    nc = _bacc.Bacc("TRN2", target_bir_lowering=False, num_devices=1)
    arrays, args = {}, []
    for name in _INS + ['rope']:
        a = _np.ascontiguousarray(laid_out[name])
        arrays[f"in_{name}_dram"] = a
        args.append(nc.dram_tensor(f"in_{name}_dram", a.shape, _mybir.dt.from_np(a.dtype), kind="ExternalInput").ap())
    args.append(nc.dram_tensor("out_0_dram", (S, D), _mybir.dt.float32, kind="ExternalOutput").ap())
    hybrid_block(nc, *args)
    r = _run(nc, [arrays], core_ids=[0])
    return r.results[0]["out_0_dram"].reshape(1, S, D)
```

```python
from contextlib import ExitStack

import numpy as np

import concourse.bass as bass
from concourse import mybir

F32 = mybir.dt.float32
F32R = mybir.dt.float32r
BF16 = mybir.dt.bfloat16
ALU = mybir.AluOpType
ACT = mybir.ActivationFunctionType
AX = mybir.AxisListType

P = 128
S = 2048
D = 1024
TILES = S // P
KC = D // P
HD = 64
EPS = 1e-6
NEG = -1e30
SCALE = HD ** -0.5
QA = 512
KV = 128
WA = QA + 2 * KV
SH = QA // HD
SG = KV // HD
DW = 512
DH = 4
WB = 3 * DW
VD = 2 * HD
LAMBDA_INIT = 0.8 - 0.6
DF = 2816
FC = DF // P
TB = 512
BLOCKS = S // TB
BT = TB // P


def steady(count, k, i):
    return count(k) if i is None else (count(k + 2) - count(k)) * i + (4 * count(k) - 3 * count(k + 2))


def tiles(eng, first=0, end=TILES):
    for k in range(first, 6):
        yield k, None
    with eng.Fori(3, TILES // 2 - 1) as i:
        yield 6, i
        yield 7, i
    for k in range(TILES - 2, end):
        yield k, None


def turns(eng):
    for k, i in tiles(eng, -2, TILES + 3):
        def take(ahead, step, *args, k=k, i=i):
            if 0 <= k + ahead < TILES:
                step(k + ahead, i, *args)
        yield k, take


class Banks:

    def __init__(self, banks, keys):
        self.keys = keys
        self.place = {key: n for n, key in enumerate(keys)}
        self.banks = banks

    def bank(self, *key):
        return self.banks[self.place[key] % len(self.banks)]

    def free(self, pe, read_out, k, i, kind, *n):
        back = self.place[(kind, k, *n)] - len(self.banks)
        if back >= 0:
            what, tile, *rest = self.keys[back]
            semaphore, count = read_out[what]
            pe.wait_ge(semaphore, steady(lambda t: count(t, *rest), tile, i))


class Memory:

    def __init__(self, nc, ctx, phase):
        self.nc, self.ctx, self.phase = nc, ctx, phase
        self.semaphores = []

    def sb(self, name, shape, dt=F32):
        return self.ctx.enter_context(self.nc.sbuf_tensor(f"{self.phase}_{name}", shape, dt))

    def psum(self):
        return self.ctx.enter_context(self.nc.psum_tensor(f"{self.phase}_psum", [P, 8, 512], F32))

    def sem(self, name):
        self.semaphores.append(self.nc.alloc_semaphore(name=f"{self.phase}_{name}"))
        return self.semaphores[-1]

    def end(self):
        self.nc.clear_and_free_semaphores(self.semaphores)
        self.nc.all_engine_barrier()


def wait_apart(eng, met, *waits):
    values = [value if isinstance(value, int) else eng.snap(eng.to_reg(value)) for _, value in waits]
    eng.wait_ge(*met)
    for (semaphore, _), value in zip(waits, values):
        eng.wait_ge(semaphore, value)


def make_identity(pool, ident, step):
    pool.memset(ident[:, :], 0.0).then_inc(step, 1)
    pool.wait_ge(step, 1)
    pool.affine_select(out=ident[:, :], in_=ident[:, :], compare_op=ALU.not_equal, fill=1.0, base=0,
                       pattern=[[-1, P]], channel_multiplier=1).then_inc(step, 1)


def pool_rstd(pool, out, total, width, half, step, done):
    pool.tensor_scalar(out, total, 1.0 / width, EPS, ALU.mult, ALU.add).then_inc(step, 1)
    pool.wait_ge(step, done)
    return pool.tensor_tensor(out, out, half, ALU.pow)


def swa_phase(nc, x, w_in, g_pre, sinks, rope, swa_t):
    order = []
    for t in range(-1, TILES + 3):
        order += [("x", t + 1, 0), ("x", t + 1, 1), ("q", t), ("o", t - 3, 0), ("o", t - 3, 1), ("qT", t), ("kv", t),
                  ("a", t - 2, 0), ("a", t - 2, 1), ("a", t - 2, 2), ("a", t - 2, 3), ("kT", t)]
    banks = Banks([4, 5, 6, 7], [use for use in order if 0 <= use[1] < TILES])
    s_banks = Banks([0, 1, 2, 3], [("s", t, j) for t in range(TILES) for j in range(4)])

    RAW = 8
    pieces = [(c, slice(0, QA)) for c in range(KC)] + [(c, slice(QA, WA)) for c in range(KC)]

    with ExitStack() as ctx:
        m = Memory(nc, ctx, "swa")
        ps = m.psum()
        w_hi = m.sb("w_hi", [P, KC, WA], F32R)
        w_lo = m.sb("w_lo", [P, KC, WA], F32R)
        w_raw = m.sb("w_raw", [P, RAW, QA])
        g_col = m.sb("g_col", [P, KC])
        rope_sb = m.sb("rope", [P, TILES, 4 * HD])
        ident = m.sb("ident", [P, P])
        half = m.sb("half", [P, 1])
        sink = m.sb("sink", [P, SH])
        xb = m.sb("x", [P, 2, D])
        junk = m.sb("junk", [P, D], BF16)
        ss = m.sb("ss", [P, 2])
        rstd = m.sb("rstd", [P, 2])
        xt_hi = m.sb("xt_hi", [P, 2, KC, P], F32R)
        xt_lo = m.sb("xt_lo", [P, 2, KC, P], F32R)
        rot_c = m.sb("rot_c", [P, QA])
        rot_s = m.sb("rot_s", [P, QA])
        rot_q = m.sb("rot_q", [P, QA])
        rot_kc = m.sb("rot_kc", [P, KV])
        rot_ks = m.sb("rot_ks", [P, KV])
        rot_k = m.sb("rot_k", [P, KV])
        v_raw = m.sb("v_raw", [P, 2, KV])
        q_hl = m.sb("q_hl", [P, SH // 2, 2, P], F32R)
        q_lh = m.sb("q_lh", [P, SH // 2, 2, P], F32R)
        k_hl = m.sb("k_hl", [P, SG, 2, P], F32R)
        v_hl = m.sb("v_hl", [P, 2, SG, 2 * HD], F32R)
        top = m.sb("top", [P, 2, SH])
        bias = m.sb("bias", [P, 2, SH])
        gap = m.sb("gap", [P, 2, SH])
        sums = m.sb("sums", [P, 2, SH])
        recip = m.sb("recip", [P, 2, SH])
        probs = m.sb("probs", [P, 2, SH, 2 * P])
        at_hi = m.sb("at_hi", [P, 4, 4 * P], F32R)
        at_lo = m.sb("at_lo", [P, 4, 4 * P], F32R)
        o_tmp = m.sb("o_tmp", [P, SH // 2, P])
        o_sum = m.sb("o_sum", [P, 2, SH // 2, P])

        w_loaded = [m.sem(f"w_loaded{n}") for n in range(RAW)]
        w_hi_done, w_lo_done = m.sem("w_hi_done"), m.sem("w_lo_done")
        consts_loaded, consts_made = m.sem("consts_loaded"), m.sem("consts_made")
        rope_loaded = m.sem("rope_loaded")
        zeroed = m.sem("zeroed")
        x_loaded = [m.sem(f"x_loaded{n}") for n in range(2)]
        squared, pool_step, rstd_ready, x_scaled = (m.sem(n) for n in ("squared", "pool_step", "rstd_ready", "x_scaled"))
        x_turned, xt_hi_done, xt_lo_done = (m.sem(n) for n in ("x_turned", "xt_hi_done", "xt_lo_done"))
        q_projected, kv_projected = m.sem("q_projected"), m.sem("kv_projected")
        q_parts, k_parts, q_roped, k_roped = (m.sem(n) for n in ("q_parts", "k_parts", "q_roped", "k_roped"))
        v_copied, v_hi_done, v_split = (m.sem(n) for n in ("v_copied", "v_hi_done", "v_split"))
        q_turned, k_turned, q_hi_done, k_hi_done, q_split, k_split = (
            m.sem(n) for n in ("q_turned", "k_turned", "q_hi_done", "k_hi_done", "q_split", "k_split"))
        scores_read = m.sem("scores_read")
        scored, dve_step, max_ready, exp_done, recip_ready, scaled = (
            m.sem(n) for n in ("scored", "dve_step", "max_ready", "exp_done", "recip_ready", "scaled"))
        a_turned, at_hi_done, at_lo_done = (m.sem(n) for n in ("a_turned", "at_hi_done", "at_lo_done"))
        attended, o_copied, o_added = (m.sem(n) for n in ("attended", "o_copied", "o_added"))
        stored = [m.sem(f"stored{n}") for n in range(2)]
        read_out = {
            "x": (xt_lo_done, lambda t, h: 2 * t + h + 1), "q": (q_parts, lambda t: t + 1),
            "kv": (v_copied, lambda t: t + 1), "s": (scores_read, lambda t, j: 4 * t + j + 1),
            "qT": (q_split, lambda t: t + 1), "kT": (k_split, lambda t: t + 1),
            "a": (at_lo_done, lambda t, j: 4 * t + j + 1), "o": (o_added, lambda t, u: 2 * (SG * t + u + 1)),
        }

        def chunks_seen(k):
            own = 2 * (k % 2)
            return slice(own, own + 1) if k == 0 else (slice(0, 4, 3) if k % 2 == 0 else slice(1, 3))

        with nc.Block() as block:
            @block.sync
            def _(sp):
                w_view = w_in.rearrange("(c p) n -> c p n", p=P)
                with nc.allow_non_contiguous_dma(reason="gains by column"):
                    sp.dma_start(g_col[:, :], g_pre.rearrange("(c p) -> p c", p=P)).then_inc(consts_loaded, 16)
                sp.dma_start(xb[:, 0, :], x[0:P, :]).then_inc(x_loaded[0], 16)
                sp.dma_start(sink[:, :], sinks.unsqueeze(0).broadcast_to([P, SH])).then_inc(consts_loaded, 16)
                sp.dma_start(xb[:, 1, :], x[P:2 * P, :]).then_inc(x_loaded[1], 16)
                for n, (c, cols) in enumerate(pieces):
                    if n >= RAW:
                        sp.wait_ge(w_lo_done, n - RAW + 1)
                    sp.dma_start(w_raw[:, n % RAW, 0:cols.stop - cols.start], w_view[c, :, cols]).then_inc(w_loaded[n % RAW], 16)
                    if n == KC - 1:
                        sp.dma_start(rope_sb[:, :, :], rope.rearrange("(t p) n -> p t n", p=P)).then_inc(rope_loaded, 16)
                def load_x(k, i):
                    wait_apart(sp, (consts_loaded, 32), (x_turned, steady(lambda t: 2 * t - 2, k, i)))
                    sp.dma_start(xb[:, k % 2, :], x[bass.ds(steady(lambda t: t * P, k, i), P), :]).then_inc(x_loaded[k % 2], 16)

                def store(k, i):
                    wait_apart(sp, (consts_loaded, 32), (o_added, steady(lambda t: 2 * SG * (t + 1), k, i)))
                    sp.dma_start(swa_t[:, :, bass.ds(steady(lambda t: t * P, k, i), P)], o_sum[:, k % 2, :, :])\
                        .then_inc(stored[k % 2], 16)

                for k, take in turns(sp):
                    if k >= 0:
                        take(2, load_x)
                    take(-3, store)
                for q in stored:
                    sp.wait_ge(q, 16 * TILES // 2)

            @block.gpsimd
            def _(pool):
                make_identity(pool, ident, consts_made)
                pool.memset(half[:, :], -0.5).then_inc(consts_made, 1)
                pool.wait_ge(consts_made, 3)
                pool.memset(probs[:, :, :, :], 0.0).then_inc(zeroed, 1)

                def rstd_of(k, i):
                    waits = [(squared, steady(lambda t: t + 1, k, i))]
                    if k >= 2:
                        waits.append((x_scaled, steady(lambda t: t - 1, k, i)))
                    wait_apart(pool, (consts_made, 3), *waits)
                    q = k % 2
                    pool_rstd(pool, rstd[:, q:q + 1], ss[:, q:q + 1], D, half[:, :], pool_step,
                              steady(lambda t: t + 1, k, i)).then_inc(rstd_ready, 1)

                def rotate(k, i, parts, turned, out, a, b, roped):
                    pool.wait_ge(parts, steady(lambda t: t + 1, k, i))
                    if k >= 1:
                        pool.wait_ge(turned, steady(lambda t: t, k, i))
                    pool.tensor_tensor(out[:, :], a[:, :], b[:, :], ALU.add).then_inc(roped, 1)

                def scale_probs(k, i):
                    q = k % 2
                    pool.wait_ge(recip_ready, steady(lambda t: t + 1, k, i))
                    pool.tensor_tensor(probs[:, q, :, :], probs[:, q, :, :],
                                       recip[:, q, :].unsqueeze(2).broadcast_to([P, SH, 2 * P]), ALU.mult)\
                        .then_inc(scaled, 1)

                def split_v(k, i):
                    q = k % 2
                    waits = [(v_copied, steady(lambda t: t + 1, k, i))]
                    if k >= 1:
                        waits.append((attended, steady(lambda t: SG * t, k, i)))
                    wait_apart(pool, (consts_made, 3), *waits)
                    v = v_raw[:, q, :].rearrange("p (u d) -> p u d", u=SG)
                    pool.tensor_copy(v_hl[:, q, :, 0:HD], v).then_inc(v_hi_done, 1)
                    pool.wait_ge(v_hi_done, steady(lambda t: t + 1, k, i))
                    pool.tensor_tensor(v_hl[:, q, :, HD:2 * HD], v, v_hl[:, q, :, 0:HD].bitcast(F32), ALU.subtract)\
                        .then_inc(v_split, 1)

                for k, take in turns(pool):
                    take(2, rstd_of)
                    take(0, rotate, q_parts, q_turned, rot_q, rot_c, rot_s, q_roped)
                    take(0, rotate, k_parts, k_turned, rot_k, rot_kc, rot_ks, k_roped)
                    take(-2, split_v)
                    take(-1, scale_probs)

            @block.scalar
            def _(act):
                def square(k, i):
                    q = k % 2
                    act.wait_ge(x_loaded[q], steady(lambda t: 16 * (t // 2 + 1), k, i))
                    if k >= 2:
                        act.wait_ge(rstd_ready, steady(lambda t: t - 1, k, i))
                    act.activation(junk[:, :], xb[:, q, :], ACT.Square, accum_out=ss[:, q:q + 1]).then_inc(squared, 1)

                def turned_hi(k, i):
                    q = k % 2
                    for h in range(2):
                        act.wait_ge(x_turned, steady(lambda t: 2 * t + h + 1, k, i))
                        if k >= 2 and h == 0:
                            act.wait_ge(kv_projected, steady(lambda t: t - 1, k, i))
                        b = banks.bank("x", k, h)
                        act.activation(xt_hi[:, q, 4 * h:4 * h + 4, :], ps[:, b, :].rearrange("p (c n) -> p c n", n=P),
                                       ACT.Copy).then_inc(xt_hi_done, 1)

                def exps(k, i, js):
                    q = k % 2
                    if js[0] == 0:
                        act.wait_ge(max_ready, steady(lambda t: t + 1, k, i))
                        if k == 0:
                            act.wait_ge(zeroed, 1)
                        if k >= 2:
                            act.wait_ge(a_turned, steady(lambda t: 4 * (t - 1), k, i))
                            act.wait_ge(recip_ready, steady(lambda t: t - 1, k, i))
                    for j in js:
                        sc = ps[:, s_banks.bank("s", k, j), :].rearrange("p (h c n) -> p h c n", h=2, c=4)
                        pr = probs[:, q, 2 * j:2 * j + 2, :].rearrange("p h (c n) -> p h c n", c=4)
                        for h in range(2):
                            hh = 2 * j + h
                            seen, own = chunks_seen(k), slice(2 * q, 2 * q + 2)
                            for lo, cs in ((0, seen), (HD, own)):
                                part = slice(lo, lo + HD)
                                last = act.activation(pr[part, h, cs, :], sc[part, h, cs, :], ACT.Exp,
                                                      bias=bias[part, q, hh:hh + 1], accum_out=sums[part, q, hh:hh + 1])
                        last.then_inc(scores_read, 1)
                    if js[-1] == 3:
                        act.activation(gap[:, q, :], gap[:, q, :], ACT.Exp).then_inc(exp_done, 1)

                def hi_q(k, i):
                    act.wait_ge(q_turned, steady(lambda t: t + 1, k, i))
                    src = ps[:, banks.bank("qT", k), :].rearrange("p (j n) -> p j n", n=P)
                    act.activation(q_hl[0:HD, :, 0, :], src[0:HD, :, :], ACT.Copy)
                    act.activation(q_hl[0:HD, :, 1, :], src[HD:P, :, :], ACT.Copy)
                    act.activation(q_lh[HD:P, :, 0, :], src[0:HD, :, :], ACT.Copy)
                    act.activation(q_lh[HD:P, :, 1, :], src[HD:P, :, :], ACT.Copy).then_inc(q_hi_done, 1)

                def hi_k(k, i):
                    q = k % 2
                    act.wait_ge(k_turned, steady(lambda t: t + 1, k, i))
                    src = ps[:, banks.bank("kT", k), 0:P]
                    act.activation(k_hl[0:HD, 0, q, :], src[0:HD, :], ACT.Copy)
                    act.activation(k_hl[0:HD, 1, q, :], src[HD:P, :], ACT.Copy).then_inc(k_hi_done, 1)

                def copy_v(k, i):
                    act.wait_ge(k_parts, steady(lambda t: t + 1, k, i))
                    if k >= 2:
                        act.wait_ge(v_split, steady(lambda t: t - 1, k, i))
                    b = banks.bank("kv", k)
                    act.activation(v_raw[:, k % 2, :], ps[:, b, KV:2 * KV], ACT.Copy).then_inc(v_copied, 1)

                def hi_a(k, i, js):
                    for j in js:
                        act.wait_ge(a_turned, steady(lambda t: 4 * t + j + 1, k, i))
                        if k >= 1 and j == 0:
                            act.wait_ge(attended, steady(lambda t: SG * t, k, i))
                        b = banks.bank("a", k, j)
                        act.activation(at_hi[:, j, :], ps[:, b, :], ACT.Copy).then_inc(at_hi_done, 1)

                def copy_o(k, i):
                    for u in range(SG):
                        act.wait_ge(attended, steady(lambda t: SG * t + u + 1, k, i))
                        if k >= 1 and u == 0:
                            act.wait_ge(o_added, steady(lambda t: 2 * SG * t, k, i))
                        src = ps[:, banks.bank("o", k, u), :].rearrange("p (j e n) -> p j e n", e=2, n=P)
                        act.activation(o_tmp[0:HD, 2 * u:2 * u + 2, :], src[HD:P, :, 0, :], ACT.Copy)
                        act.activation(o_tmp[HD:P, 2 * u:2 * u + 2, :], src[0:HD, :, 1, :], ACT.Copy).then_inc(o_copied, 1)

                act.wait_ge(consts_loaded, 32)
                for k, take in turns(act):
                    take(1, turned_hi)
                    take(-1, hi_k)
                    take(2, square)
                    if k == -1:
                        for n, (c, cols) in enumerate(pieces):
                            act.wait_ge(w_loaded[n % RAW], 16 * (n // RAW + 1))
                            act.activation(w_hi[:, c, cols], w_raw[:, n % RAW, 0:cols.stop - cols.start], ACT.Copy,
                                           scale=g_col[:, c:c + 1]).then_inc(w_hi_done, 1)
                    take(-3, copy_o)
                    take(0, hi_q)
                    take(-1, exps, (0,))
                    take(-2, hi_a, (0,))
                    take(-2, hi_a, (1,))
                    take(-1, exps, (1,))
                    take(0, copy_v)
                    take(-2, hi_a, (2,))
                    take(-2, hi_a, (3,))
                    take(-1, exps, (2,))
                    take(-1, exps, (3,))

            @block.vector
            def _(dve):
                def scale_x(k, i):
                    q = k % 2
                    dve.wait_ge(rstd_ready, steady(lambda t: t + 1, k, i))
                    dve.tensor_scalar(xb[:, q, :], xb[:, q, :], rstd[:, q:q + 1], None, ALU.mult).then_inc(x_scaled, 1)

                def turned_lo(k, i):
                    q = k % 2
                    for h in range(2):
                        dve.wait_ge(xt_hi_done, steady(lambda t: 2 * t + h + 1, k, i))
                        b = banks.bank("x", k, h)
                        dve.tensor_tensor(xt_lo[:, q, 4 * h:4 * h + 4, :], ps[:, b, :].rearrange("p (c n) -> p c n", n=P),
                                          xt_hi[:, q, 4 * h:4 * h + 4, :].bitcast(F32), ALU.subtract)\
                            .then_inc(xt_lo_done, 1)

                def rope_parts(k, i, src, heads, c_out, s_out, scaled_by, tok):
                    cos = rope_sb[:, tok, scaled_by:scaled_by + HD]
                    sin = rope_sb[:, tok, scaled_by + HD:scaled_by + 2 * HD]
                    view = src.rearrange("p (h d) -> p h d", d=HD)
                    dve.tensor_tensor(c_out[:, :].rearrange("p (h d) -> p h d", d=HD), view,
                                      cos.broadcast_to([P, heads, HD]), ALU.mult)
                    for a in range(2):
                        to, frm = slice(a * HD // 2, (a + 1) * HD // 2), slice((1 - a) * HD // 2, (2 - a) * HD // 2)
                        last = dve.tensor_tensor(
                            s_out[:, :].rearrange("p (h d) -> p h d", d=HD)[:, :, to], view[:, :, frm],
                            sin[:, :, to].broadcast_to([P, heads, HD // 2]), ALU.mult)
                    return last

                def rope_q(k, i):
                    dve.wait_ge(q_projected, steady(lambda t: t + 1, k, i))
                    if k >= 1:
                        dve.wait_ge(q_roped, steady(lambda t: t, k, i))
                    tok = bass.ds(steady(lambda t: t, k, i), 1)
                    b = banks.bank("q", k)
                    rope_parts(k, i, ps[:, b, :], SH, rot_c, rot_s, 2 * HD, tok).then_inc(q_parts, 1)

                def rope_k(k, i):
                    dve.wait_ge(kv_projected, steady(lambda t: t + 1, k, i))
                    if k >= 1:
                        dve.wait_ge(k_roped, steady(lambda t: t, k, i))
                    tok = bass.ds(steady(lambda t: t, k, i), 1)
                    rope_parts(k, i, ps[:, banks.bank("kv", k), 0:KV], SG, rot_kc, rot_ks, 0, tok).then_inc(k_parts, 1)

                def maxima(k, i):
                    q = k % 2
                    if k >= 2:
                        dve.wait_ge(exp_done, steady(lambda t: t - 1, k, i))
                    for j in range(4):
                        dve.wait_ge(scored, steady(lambda t: 4 * t + j + 1, k, i))
                        sc = ps[:, s_banks.bank("s", k, j), :].rearrange("p (h c n) -> p h c n", h=2, c=4)
                        for lo, cs in ((0, chunks_seen(k)), (HD, slice(2 * q, 2 * q + 2))):
                            part = slice(lo, lo + HD)
                            last = dve.tensor_reduce(top[part, q, 2 * j:2 * j + 2], sc[part, :, cs, :], AX.XY, ALU.max)
                    last.then_inc(dve_step, 1)
                    dve.wait_ge(dve_step, steady(lambda t: 3 * t + 1, k, i))
                    dve.tensor_tensor(top[:, q, :], top[:, q, :], sink[:, :], ALU.max).then_inc(dve_step, 1)
                    dve.wait_ge(dve_step, steady(lambda t: 3 * t + 2, k, i))
                    dve.tensor_scalar(bias[:, q, :], top[:, q, :], -1.0, None, ALU.mult)
                    dve.tensor_tensor(gap[:, q, :], sink[:, :], top[:, q, :], ALU.subtract).then_inc(max_ready, 1)

                def recips(k, i):
                    q = k % 2
                    dve.wait_ge(exp_done, steady(lambda t: t + 1, k, i))
                    if k >= 2:
                        dve.wait_ge(scaled, steady(lambda t: t - 1, k, i))
                    dve.tensor_tensor(sums[:, q, :], sums[:, q, :], gap[:, q, :], ALU.add).then_inc(dve_step, 1)
                    dve.wait_ge(dve_step, steady(lambda t: 3 * t + 3, k, i))
                    dve.reciprocal(recip[:, q, :], sums[:, q, :]).then_inc(recip_ready, 1)

                def lo_q(k, i):
                    dve.wait_ge(q_hi_done, steady(lambda t: t + 1, k, i))
                    b = banks.bank("qT", k)
                    src = ps[:, b, :].rearrange("p (j n) -> p j n", n=P)
                    even, odd = q_hl[0:HD, :, 0, :].bitcast(F32), q_lh[HD:P, :, 1, :].bitcast(F32)
                    dve.tensor_tensor(q_hl[HD:P, :, 0, :], src[0:HD, :, :], even, ALU.subtract)
                    dve.tensor_tensor(q_lh[0:HD, :, 0, :], src[0:HD, :, :], even, ALU.subtract)
                    dve.tensor_tensor(q_hl[HD:P, :, 1, :], src[HD:P, :, :], odd, ALU.subtract)
                    dve.tensor_tensor(q_lh[0:HD, :, 1, :], src[HD:P, :, :], odd, ALU.subtract).then_inc(q_split, 1)

                def lo_k(k, i):
                    q = k % 2
                    dve.wait_ge(k_hi_done, steady(lambda t: t + 1, k, i))
                    b = banks.bank("kT", k)
                    dve.tensor_tensor(k_hl[HD:P, 0, q, :], ps[0:HD, b, 0:P], k_hl[0:HD, 0, q, :].bitcast(F32), ALU.subtract)
                    dve.tensor_tensor(k_hl[HD:P, 1, q, :], ps[HD:P, b, 0:P], k_hl[0:HD, 1, q, :].bitcast(F32),
                                      ALU.subtract).then_inc(k_split, 1)

                def lo_a(k, i, js):
                    for j in js:
                        dve.wait_ge(at_hi_done, steady(lambda t: 4 * t + j + 1, k, i))
                        b = banks.bank("a", k, j)
                        dve.tensor_tensor(at_lo[:, j, :], ps[:, b, :], at_hi[:, j, :].bitcast(F32), ALU.subtract)\
                            .then_inc(at_lo_done, 1)

                def add_o(k, i):
                    q = k % 2
                    for u in range(SG):
                        dve.wait_ge(o_copied, steady(lambda t: SG * t + u + 1, k, i))
                        if k >= 2 and u == 0:
                            dve.wait_ge(stored[q], steady(lambda t: 16 * (t // 2), k, i))
                        b = banks.bank("o", k, u)
                        src = ps[:, b, :].rearrange("p (j e n) -> p j e n", e=2, n=P)
                        dve.tensor_tensor(o_sum[0:HD, q, 2 * u:2 * u + 2, :], src[0:HD, :, 0, :],
                                          o_tmp[0:HD, 2 * u:2 * u + 2, :], ALU.add).then_inc(o_added, 1)
                        dve.tensor_tensor(o_sum[HD:P, q, 2 * u:2 * u + 2, :], src[HD:P, :, 1, :],
                                          o_tmp[HD:P, 2 * u:2 * u + 2, :], ALU.add).then_inc(o_added, 1)

                for k, take in turns(dve):
                    take(-1, lo_k)
                    take(1, turned_lo)
                    take(0, rope_q)
                    take(2, scale_x)
                    take(-1, maxima)
                    take(-3, add_o)
                    if k == -1:
                        for n, (c, cols) in enumerate(pieces):
                            dve.wait_ge(w_hi_done, n + 1)
                            dve.scalar_tensor_tensor(w_lo[:, c, cols], w_raw[:, n % RAW, 0:cols.stop - cols.start],
                                                     g_col[:, c:c + 1], w_hi[:, c, cols].bitcast(F32),
                                                     ALU.mult, ALU.subtract).then_inc(w_lo_done, 1)
                        dve.wait_ge(rope_loaded, 16)
                    take(0, rope_k)
                    take(0, lo_q)
                    take(-2, lo_a, (0,))
                    take(-2, lo_a, (1,))
                    take(-2, lo_a, (2,))
                    take(-2, lo_a, (3,))
                    take(-1, recips)

            @block.tensor
            def _(pe):
                def free(k, i, kind, *n):
                    group = s_banks if kind == "s" else banks
                    group.free(pe, read_out, k, i, kind, *n)
                    return group.bank(kind, k, *n)

                def turn_x(k, i):
                    pe.wait_ge(x_scaled, steady(lambda t: t + 1, k, i))
                    for h in range(2):
                        b = free(k, i, "x", h)
                        for c in range(4):
                            last = pe.transpose(ps[:, b, c * P:(c + 1) * P],
                                                xb[:, k % 2, (4 * h + c) * P:(4 * h + c + 1) * P], ident[:, :])
                        last.then_inc(x_turned, 1)

                def project(k, i, kind, first, width, done):
                    q = k % 2
                    b = free(k, i, kind)
                    for c in range(KC):
                        if kind == "q" and c % 4 == 0:
                            pe.wait_ge(xt_lo_done, steady(lambda t: 2 * t + c // 4 + 1, k, i))
                        if k == 0:
                            pe.wait_ge(w_lo_done, (0 if kind == "q" else KC) + c + 1)
                        for n, (lhs, rhs) in enumerate(((xt_hi, w_hi), (xt_hi, w_lo), (xt_lo, w_hi))):
                            last = pe.matmul(ps[:, b, 0:width], lhs[:, q, c, :], rhs[:, c, first:first + width],
                                             start=(c == 0 and n == 0), stop=(c == KC - 1 and n == 2))
                    last.then_inc(done, 1)

                def turn_q(k, i):
                    pe.wait_ge(q_roped, steady(lambda t: t + 1, k, i))
                    b = free(k, i, "qT")
                    for j in range(4):
                        last = pe.transpose(ps[:, b, j * P:(j + 1) * P], rot_q[:, j * P:(j + 1) * P], ident[:, :])
                    last.then_inc(q_turned, 1)

                def turn_k(k, i):
                    pe.wait_ge(k_roped, steady(lambda t: t + 1, k, i))
                    b = free(k, i, "kT")
                    pe.transpose(ps[:, b, 0:P], rot_k[:, :], ident[:, :]).then_inc(k_turned, 1)

                def score(k, i):
                    pe.wait_ge(q_split, steady(lambda t: t + 1, k, i))
                    pe.wait_ge(k_split, steady(lambda t: t + 1, k, i))
                    slots = 1 if k == 0 else 2
                    for j in range(4):
                        b = free(k, i, "s", j)
                        for h in range(2):
                            for n, stack in enumerate((q_hl, q_lh)):
                                last = pe.matmul(ps[:, b, 2 * P * h:2 * P * h + slots * P], stack[:, j, h, :],
                                                 k_hl[:, j // 2, 0:slots, :], start=(n == 0), stop=(n == 1))
                        last.then_inc(scored, 1)

                def turn_a(k, i):
                    pe.wait_ge(scaled, steady(lambda t: t + 1, k, i))
                    for j in range(4):
                        u, slot = j // 2, j % 2
                        b = free(k, i, "a", j)
                        for h in range(4):
                            last = pe.transpose(ps[:, b, h * P:(h + 1) * P],
                                                probs[:, k % 2, 4 * u + h, slot * P:(slot + 1) * P], ident[:, :])
                        last.then_inc(a_turned, 1)

                def attend(k, i):
                    pe.wait_ge(v_split, steady(lambda t: t + 1, k, i))
                    slots = (0,) if k == 0 else (0, 1)
                    for u in range(SG):
                        b = free(k, i, "o", u)
                        for slot in slots:
                            pe.wait_ge(at_lo_done, steady(lambda t: 4 * t + 2 * u + slot + 1, k, i))
                            for n, a in enumerate((at_hi, at_lo)):
                                last = pe.matmul(ps[:, b, :], v_hl[:, slot, u, :], a[:, 2 * u + slot, :],
                                                 start=(slot == 0 and n == 0), stop=(slot == slots[-1] and n == 1))
                        last.then_inc(attended, 1)

                pe.wait_ge(consts_made, 2)
                for k, take in turns(pe):
                    take(1, turn_x)
                    take(0, project, "q", 0, QA, q_projected)
                    take(-3, attend)
                    take(-1, score)
                    take(0, turn_q)
                    take(0, project, "kv", QA, 2 * KV, kv_projected)
                    take(-2, turn_a)
                    take(0, turn_k)
        m.end()


def diff_proj(nc, x, w_in, g_pre, rope, q_s, k_s, v_s):
    order = [("x", 0, 0), ("x", 0, 1)]
    for t in range(TILES + 1):
        if t < TILES:
            order.append(("q", t))
        if t >= 1:
            order.append(("kT", t - 1))
        if t < TILES:
            order.append(("k", t))
        if t + 1 < TILES:
            order += [("x", t + 1, 0), ("x", t + 1, 1)]
        if t < TILES:
            order += [("qT", t), ("v", t)]
    banks = Banks(list(range(7)), order)
    first = WA

    RAW = 8
    pieces = [(c, slice(n * DW, (n + 1) * DW)) for n in range(3) for c in range(KC)]

    with ExitStack() as ctx:
        m = Memory(nc, ctx, "dp")
        ps = m.psum()
        w_hi = m.sb("w_hi", [P, KC, WB], F32R)
        w_lo = m.sb("w_lo", [P, KC, WB], F32R)
        w_raw = m.sb("w_raw", [P, RAW, DW])
        g_col = m.sb("g_col", [P, KC])
        rope_sb = m.sb("rope", [P, 2, 4 * HD])
        ident = m.sb("ident", [P, P])
        half = m.sb("half", [P, 1])
        xb = m.sb("x", [P, 2, D])
        junk = m.sb("junk", [P, D], BF16)
        ss = m.sb("ss", [P, 2])
        rstd = m.sb("rstd", [P, 2])
        xt_hi = m.sb("xt_hi", [P, 2, KC, P], F32R)
        xt_lo = m.sb("xt_lo", [P, 2, KC, P], F32R)
        part_c = m.sb("part_c", [P, 2, DW])
        part_s = m.sb("part_s", [P, 2, DW])
        rot = m.sb("rot", [P, 2, DW])
        q_hl = m.sb("q_hl", [P, DH, 2, P], F32R)
        k_hl = m.sb("k_hl", [P, DH, 2, P], F32R)
        v_hl = m.sb("v_hl", [P, 2, DH, 2, VD], F32R)

        w_loaded = [m.sem(f"w_loaded{n}") for n in range(RAW)]
        w_hi_done, w_lo_done = m.sem("w_hi_done"), m.sem("w_lo_done")
        consts_loaded, consts_made = m.sem("consts_loaded"), m.sem("consts_made")
        x_loaded = [m.sem(f"x_loaded{n}") for n in range(2)]
        rope_loaded = [m.sem(f"rope_loaded{n}") for n in range(2)]
        squared, pool_step, rstd_ready, x_scaled = (m.sem(n) for n in ("squared", "pool_step", "rstd_ready", "x_scaled"))
        x_turned, xt_hi_done, xt_lo_done = (m.sem(n) for n in ("x_turned", "xt_hi_done", "xt_lo_done"))
        projected = [m.sem(n) for n in ("q_projected", "k_projected", "v_projected")]
        parts = [m.sem(n) for n in ("q_parts", "k_parts")]
        roped = [m.sem(n) for n in ("q_roped", "k_roped")]
        turned = [m.sem(n) for n in ("q_turned", "k_turned")]
        hi_done = [m.sem(n) for n in ("q_hi_done", "k_hi_done")]
        split = [m.sem(n) for n in ("q_split", "k_split")]
        v_hi_done, v_split = m.sem("v_hi_done"), m.sem("v_split")
        stored = [m.sem(n) for n in ("q_stored", "k_stored")]
        v_stored = [m.sem(f"v_stored{n}") for n in range(2)]
        read_out = {
            "x": (xt_lo_done, lambda t, h: 2 * t + h + 1), "q": (parts[0], lambda t: t + 1),
            "k": (parts[1], lambda t: t + 1), "v": (v_split, lambda t: t + 1),
            "qT": (split[0], lambda t: t + 1), "kT": (split[1], lambda t: t + 1),
        }

        with nc.Block() as block:
            @block.sync
            def _(sp):
                w_view = w_in.rearrange("(c p) n -> c p n", p=P)
                with nc.allow_non_contiguous_dma(reason="gains by column"):
                    sp.dma_start(g_col[:, :], g_pre.rearrange("(c p) -> p c", p=P)).then_inc(consts_loaded, 16)
                for n in range(2):
                    sp.dma_start(xb[:, n, :], x[n * P:(n + 1) * P, :]).then_inc(x_loaded[n], 16)
                    sp.dma_start(rope_sb[:, n, :], rope[n * P:(n + 1) * P, :]).then_inc(rope_loaded[n], 16)
                for n, (c, cols) in enumerate(pieces):
                    if n >= RAW:
                        sp.wait_ge(w_lo_done, n - RAW + 1)
                    sp.dma_start(w_raw[:, n % RAW, :], w_view[c, :, first + cols.start:first + cols.stop])\
                        .then_inc(w_loaded[n % RAW], 16)
                for k, i in tiles(sp):
                    p = k % 2
                    if k >= 1:
                        col = steady(lambda t: (t - 1) * P, k, i)
                        wait_apart(sp, (consts_loaded, 16), (split[1], steady(lambda t: t, k, i)))
                        sp.dma_start(k_s[:, :, :, bass.ds(col, P)], k_hl[:, :, :, :].bitcast(F32)).then_inc(stored[1], 16)
                    wait_apart(sp, (consts_loaded, 16), (split[0], steady(lambda t: t + 1, k, i)))
                    sp.dma_start(q_s[bass.ds(steady(lambda t: t, k, i), 1), :, :, :, :].rearrange("a p h m n -> p (a h) m n"),
                                 q_hl[:, :, :, :].bitcast(F32)).then_inc(stored[0], 16)
                    if k + 2 < TILES:
                        row = steady(lambda t: (t + 2) * P, k, i)
                        wait_apart(sp, (consts_loaded, 16), (x_turned, steady(lambda t: 2 * t + 2, k, i)),
                                   (parts[1], steady(lambda t: t + 1, k, i)))
                        sp.dma_start(xb[:, p, :], x[bass.ds(row, P), :]).then_inc(x_loaded[p], 16)
                        sp.dma_start(rope_sb[:, p, :], rope[bass.ds(row, P), :]).then_inc(rope_loaded[p], 16)
                    wait_apart(sp, (consts_loaded, 16), (v_split, steady(lambda t: t + 1, k, i)))
                    sp.dma_start(v_s[:, :, bass.ds(steady(lambda t: t, k, i), 1), :, :].rearrange("p h t a v -> p h (t a) v"),
                                 v_hl[:, p, :, :, :].bitcast(F32)).then_inc(v_stored[p], 16)
                sp.wait_ge(split[1], TILES)
                sp.dma_start(k_s[:, :, :, (TILES - 1) * P:S], k_hl[:, :, :, :].bitcast(F32)).then_inc(stored[1], 16)
                for s in stored:
                    sp.wait_ge(s, 16 * TILES)
                for s in v_stored:
                    sp.wait_ge(s, 16 * TILES // 2)

            @block.gpsimd
            def _(pool):
                make_identity(pool, ident, consts_made)
                pool.memset(half[:, :], -0.5).then_inc(consts_made, 1)
                pool.wait_ge(consts_made, 3)

                def rstd_of(k, i):
                    waits = [(squared, steady(lambda t: t + 1, k, i))]
                    if k >= 2:
                        waits.append((x_scaled, steady(lambda t: t - 1, k, i)))
                    wait_apart(pool, (consts_made, 3), *waits)
                    q = k % 2
                    pool_rstd(pool, rstd[:, q:q + 1], ss[:, q:q + 1], D, half[:, :], pool_step,
                              steady(lambda t: t + 1, k, i)).then_inc(rstd_ready, 1)

                def rotate(n, k, i):
                    pool.wait_ge(parts[n], steady(lambda t: t + 1, k, i))
                    if k >= 1:
                        pool.wait_ge(turned[n], steady(lambda t: t, k, i))
                    pool.tensor_tensor(rot[:, n, :], part_c[:, n, :], part_s[:, n, :], ALU.add).then_inc(roped[n], 1)

                rstd_of(0, None)
                for k, i in tiles(pool):
                    if k + 1 < TILES:
                        rstd_of(k + 1, i)
                    rotate(0, k, i)
                    rotate(1, k, i)

            @block.scalar
            def _(act):
                def square(k, i):
                    q = k % 2
                    act.wait_ge(x_loaded[q], steady(lambda t: 16 * (t // 2 + 1), k, i))
                    if k >= 2:
                        act.wait_ge(rstd_ready, steady(lambda t: t - 1, k, i))
                    act.activation(junk[:, :], xb[:, q, :], ACT.Square, accum_out=ss[:, q:q + 1]).then_inc(squared, 1)

                def turned_hi(k, i):
                    q = k % 2
                    for h in range(2):
                        act.wait_ge(x_turned, steady(lambda t: 2 * t + h + 1, k, i))
                        if k >= 2 and h == 0:
                            act.wait_ge(projected[2], steady(lambda t: t - 1, k, i))
                        b = banks.bank("x", k, h)
                        act.activation(xt_hi[:, q, 4 * h:4 * h + 4, :], ps[:, b, :].rearrange("p (c n) -> p c n", n=P),
                                       ACT.Copy).then_inc(xt_hi_done, 1)

                def hi_qk(n, k, i):
                    out = (q_hl, k_hl)[n]
                    act.wait_ge(turned[n], steady(lambda t: t + 1, k, i))
                    if k >= 1:
                        act.wait_ge(stored[n], steady(lambda t: 16 * t, k, i))
                    src = ps[:, banks.bank(("qT", "kT")[n], k), :].rearrange("p (h n) -> p h n", n=P)
                    act.activation(out[0:HD, :, 0, :], src[0:HD, :, :], ACT.Copy)
                    act.activation(out[0:HD, :, 1, :], src[HD:P, :, :], ACT.Copy).then_inc(hi_done[n], 1)

                def hi_v(k, i):
                    act.wait_ge(projected[2], steady(lambda t: t + 1, k, i))
                    if k >= 2:
                        act.wait_ge(v_stored[k % 2], steady(lambda t: 16 * (t // 2), k, i))
                    act.activation(v_hl[:, k % 2, :, 0, :], ps[:, banks.bank("v", k), :].rearrange("p (h v) -> p h v", h=DH),
                                   ACT.Copy).then_inc(v_hi_done, 1)

                act.wait_ge(consts_loaded, 16)
                square(0, None)
                turned_hi(0, None)
                for n, (c, cols) in enumerate(pieces):
                    act.wait_ge(w_loaded[n % RAW], 16 * (n // RAW + 1))
                    act.activation(w_hi[:, c, cols], w_raw[:, n % RAW, :], ACT.Copy, scale=g_col[:, c:c + 1])\
                        .then_inc(w_hi_done, 1)
                for k, i in tiles(act):
                    if k >= 1:
                        hi_v(k - 1, i)
                        hi_qk(1, k - 1, i)
                    if k + 1 < TILES:
                        square(k + 1, i)
                    if k + 1 < TILES:
                        turned_hi(k + 1, i)
                    hi_qk(0, k, i)
                hi_v(TILES - 1, None)
                hi_qk(1, TILES - 1, None)

            @block.vector
            def _(dve):
                def scale_x(k, i):
                    q = k % 2
                    dve.wait_ge(rstd_ready, steady(lambda t: t + 1, k, i))
                    dve.tensor_scalar(xb[:, q, :], xb[:, q, :], rstd[:, q:q + 1], None, ALU.mult).then_inc(x_scaled, 1)

                def turned_lo(k, i):
                    q = k % 2
                    for h in range(2):
                        dve.wait_ge(xt_hi_done, steady(lambda t: 2 * t + h + 1, k, i))
                        dve.tensor_tensor(xt_lo[:, q, 4 * h:4 * h + 4, :],
                                          ps[:, banks.bank("x", k, h), :].rearrange("p (c n) -> p c n", n=P),
                                          xt_hi[:, q, 4 * h:4 * h + 4, :].bitcast(F32), ALU.subtract)\
                            .then_inc(xt_lo_done, 1)

                def rope_parts(n, k, i):
                    q = k % 2
                    dve.wait_ge(projected[n], steady(lambda t: t + 1, k, i))
                    if n == 0:
                        dve.wait_ge(rope_loaded[q], steady(lambda t: 16 * (t // 2 + 1), k, i))
                    if k >= 1:
                        dve.wait_ge(roped[n], steady(lambda t: t, k, i))
                    at = 2 * HD * (1 - n)
                    cos, sin = rope_sb[:, q, at:at + HD].unsqueeze(1), rope_sb[:, q, at + HD:at + 2 * HD].unsqueeze(1)
                    view = ps[:, banks.bank(("q", "k")[n], k), :].rearrange("p (h d) -> p h d", d=HD)
                    c_out = part_c[:, n, :].rearrange("p (h d) -> p h d", d=HD)
                    s_out = part_s[:, n, :].rearrange("p (h d) -> p h d", d=HD)
                    heads = 2 * DH
                    dve.tensor_tensor(c_out, view, cos.broadcast_to([P, heads, HD]), ALU.mult)
                    for a in range(2):
                        to, frm = slice(a * HD // 2, (a + 1) * HD // 2), slice((1 - a) * HD // 2, (2 - a) * HD // 2)
                        last = dve.tensor_tensor(s_out[:, :, to], view[:, :, frm],
                                                 sin[:, :, to].broadcast_to([P, heads, HD // 2]), ALU.mult)
                    last.then_inc(parts[n], 1)

                def lo_qk(n, k, i):
                    out = (q_hl, k_hl)[n]
                    dve.wait_ge(hi_done[n], steady(lambda t: t + 1, k, i))
                    src = ps[:, banks.bank(("qT", "kT")[n], k), :].rearrange("p (h n) -> p h n", n=P)
                    dve.tensor_tensor(out[HD:P, :, 0, :], src[0:HD, :, :], out[0:HD, :, 0, :].bitcast(F32), ALU.subtract)
                    dve.tensor_tensor(out[HD:P, :, 1, :], src[HD:P, :, :], out[0:HD, :, 1, :].bitcast(F32), ALU.subtract)\
                        .then_inc(split[n], 1)

                def lo_v(k, i):
                    dve.wait_ge(v_hi_done, steady(lambda t: t + 1, k, i))
                    dve.tensor_tensor(v_hl[:, k % 2, :, 1, :],
                                      ps[:, banks.bank("v", k), :].rearrange("p (h v) -> p h v", h=DH),
                                      v_hl[:, k % 2, :, 0, :].bitcast(F32), ALU.subtract).then_inc(v_split, 1)

                scale_x(0, None)
                turned_lo(0, None)
                for n, (c, cols) in enumerate(pieces):
                    dve.wait_ge(w_hi_done, n + 1)
                    dve.scalar_tensor_tensor(w_lo[:, c, cols], w_raw[:, n % RAW, :], g_col[:, c:c + 1],
                                             w_hi[:, c, cols].bitcast(F32), ALU.mult, ALU.subtract).then_inc(w_lo_done, 1)
                for k, i in tiles(dve):
                    if k >= 1:
                        lo_v(k - 1, i)
                    rope_parts(0, k, i)
                    if k >= 1:
                        lo_qk(1, k - 1, i)
                    if k + 1 < TILES:
                        scale_x(k + 1, i)
                    rope_parts(1, k, i)
                    if k + 1 < TILES:
                        turned_lo(k + 1, i)
                    lo_qk(0, k, i)
                lo_v(TILES - 1, None)
                lo_qk(1, TILES - 1, None)

            @block.tensor
            def _(pe):
                def free(k, i, kind, *n):
                    banks.free(pe, read_out, k, i, kind, *n)
                    return banks.bank(kind, k, *n)

                def turn_x(k, i):
                    pe.wait_ge(x_scaled, steady(lambda t: t + 1, k, i))
                    for h in range(2):
                        b = free(k, i, "x", h)
                        for c in range(4):
                            last = pe.transpose(ps[:, b, c * P:(c + 1) * P],
                                                xb[:, k % 2, (4 * h + c) * P:(4 * h + c + 1) * P], ident[:, :])
                        last.then_inc(x_turned, 1)

                def project(n, k, i):
                    q = k % 2
                    b = free(k, i, "qkv"[n])
                    for c in range(KC):
                        if n == 0 and c % 4 == 0:
                            pe.wait_ge(xt_lo_done, steady(lambda t: 2 * t + c // 4 + 1, k, i))
                        if k == 0:
                            pe.wait_ge(w_lo_done, n * KC + c + 1)
                        for j, (lhs, rhs) in enumerate(((xt_hi, w_hi), (xt_hi, w_lo), (xt_lo, w_hi))):
                            last = pe.matmul(ps[:, b, :], lhs[:, q, c, :], rhs[:, c, n * DW:(n + 1) * DW],
                                             start=(c == 0 and j == 0), stop=(c == KC - 1 and j == 2))
                    last.then_inc(projected[n], 1)

                def turn_qk(n, k, i):
                    pe.wait_ge(roped[n], steady(lambda t: t + 1, k, i))
                    b = free(k, i, ("qT", "kT")[n])
                    for j in range(DH):
                        last = pe.transpose(ps[:, b, j * P:(j + 1) * P], rot[:, n, j * P:(j + 1) * P], ident[:, :])
                    last.then_inc(turned[n], 1)

                pe.wait_ge(consts_made, 2)
                turn_x(0, None)
                for k, i in tiles(pe):
                    project(0, k, i)
                    if k >= 1:
                        turn_qk(1, k - 1, i)
                    project(1, k, i)
                    if k + 1 < TILES:
                        turn_x(k + 1, i)
                    turn_qk(0, k, i)
                    project(2, k, i)
                turn_qk(1, TILES - 1, None)
        m.end()


S_SLOTS, T_SLOTS, A_SLOTS, Q_SLOTS = 5, 2, 4, 4
KINDS = {
    "S": ("PE", (-1.33, -1.82)),
    "R": ("DVE", (-0.33, 0.02)),
    "M": ("DVE", (-1.55,)),
    "E": ("ACT", (1.72, -2.49)),
    "C": ("DVE", (-2.37,)),
    "A": ("POOL", (0.0,)),
    "B": ("DVE", (1.29,)),
    "T": ("PE", (0.04,)),
    "H": ("ACT", (0.17,)),
    "L": ("DVE", (1.99,)),
    "V": ("PE", (1.59,)),
    "O": ("ACT", (1.44,)),
    "P": ("DVE", (1.31,)),
    "Q": ("ACT", (-0.38,)),
    "N": ("POOL", (1.3,)),
}
COMBINED_BY = ("A", "B", "A", "B")


def attention_plan():
    tiles_in_turn = list(range(1, TILES, 2)) + list(range(TILES - 2, -1, -2))
    chunks = [-(-(t + 1) // 4) for t in tiles_in_turn]
    steps = len(chunks)
    heads, hop, own = 3, 0.16, 0.06
    events, turns = {}, {kind: [] for kind in KINDS}

    def add(kind, h, s, *rest, us, after):
        events[kind, h, s, *rest] = us, [e for e in after if e]
        turns[kind].append((kind, h, s, *rest))

    def slot(kind, of, n):
        back = len(turns[of]) - n
        return (kind, *turns[of][back][1:]) if back >= 0 else None

    for h in range(heads):
        for s in range(steps):
            n = chunks[s]
            part = [min(4, tiles_in_turn[s] + 1 - 4 * c) / 4 for c in range(n)]
            last, second_last = divmod(h * steps + s - 1, steps), divmod(h * steps + s - 2, steps)
            for m in range(2):
                for c in range(n):
                    add("S", h, s, m, c, us=max(0.43 * part[c], 0.32), after=[slot("E", "S", S_SLOTS)])
                    add("R", h, s, m, c, us=0.53 * part[c] + (0.34 if c == n - 1 else 0.07), after=[("S", h, s, m, c)])
                add("M", h, s, m, us=0.08, after=[("R", h, s, m, c) for c in range(n)])
                for c in range(n):
                    add("E", h, s, m, c, us=0.57 * part[c] + 0.1,
                        after=[("M", h, s, m), second_last[0] >= 0 and ("T", *second_last, chunks[second_last[1]] - 1)])
            add("C", h, s, us=0.6, after=[("E", h, s, m, c) for m in range(2) for c in range(n)])
            for c in range(n):
                combine = COMBINED_BY[c]
                add(combine, h, s, c, after=[("C", h, s)],
                    us=1.75 * part[c] + 0.3 if combine == "A" else 0.56 * part[c] + 0.1)
                add("T", h, s, c, us=0.43 * part[c], after=[(combine, h, s, c), slot("L", "T", T_SLOTS)])
                add("H", h, s, c, us=0.45 * part[c] + 0.05, after=[("T", h, s, c), slot("V", "H", A_SLOTS)])
                add("L", h, s, c, us=0.53 * part[c] + 0.07, after=[("H", h, s, c)])
                add("V", h, s, c, us=0.87 * part[c], after=[("L", h, s, c), c == 0 and last[0] >= 0 and ("P", *last)])
            add("O", h, s, us=0.25, after=[("V", h, s, n - 1)])
            add("P", h, s, us=0.25, after=[("O", h, s)])
            add("Q", h, s, us=0.3, after=[("P", h, s)])
            add("N", h, s, us=1.3, after=[("Q", h, s)])

    free = {engine: 0.0 for engine, _ in KINDS.values()}
    start, taken = {}, {kind: 0 for kind in KINDS}
    for _ in range(len(events)):
        best = {}
        for kind, (engine, shifts) in KINDS.items():
            if taken[kind] == len(turns[kind]):
                continue
            event = turns[kind][taken[kind]]
            if any(e not in start for e in events[event][1]):
                continue
            ready = max([start[e] + events[e][0] + (own if KINDS[e[0]][0] == engine else hop) for e in events[event][1]] +
                        [free[engine]])
            _, h, s, *rest = event
            pressing = h * steps + s + shifts[rest[0] if len(shifts) > 1 else 0] + 0.1 * (rest[-1] if rest else 0)
            best[engine] = min(best.get(engine, (ready, pressing, event)), (ready, pressing, event))
        time, _, event = min(best.values(), key=lambda b: b[0])
        start[event] = time
        free[KINDS[event[0]][0]] = time + events[event][0]
        taken[event[0]] += 1

    begin = start["S", heads - 1, 0, 0, 0]
    late = {(kind, *rest) for (kind, h, *rest), t in start.items() if h == heads - 2 and t >= begin}
    order = []
    for kind, h, *rest in sorted(start, key=lambda e: start[e]):
        if h == heads - 2 and (kind, *rest) in late:
            order.append((1, kind, *rest))
        elif h == heads - 1 and (kind, *rest) not in late:
            order.append((0, kind, *rest))
    return tiles_in_turn, chunks, order


def diff_attn(nc, q_s, k_s, v_s, lambdas, mixed):
    tiles_in_turn, chunks, order = attention_plan()
    steps = len(tiles_in_turn)
    ordinal, total = {}, {}
    for _, *e in sorted(order, key=lambda e: (e[2], e[0])):
        ordinal[tuple(e)] = total[e[0]] = total.get(e[0], 0) + 1
    S_BANKS, T_BANKS, O_BANK = range(S_SLOTS), range(S_SLOTS, S_SLOTS + T_SLOTS), S_SLOTS + T_SLOTS
    assert total["S"] % len(S_BANKS) == 0 and total["T"] % len(T_BANKS) == 0 and total["T"] % A_SLOTS == 0

    def width(s, c):
        return min(4, tiles_in_turn[s] + 1 - 4 * c) * P

    def tops_count(s):
        return sum(2 for n in chunks[:s] if n > 1)

    with ExitStack() as ctx:
        m_ = Memory(nc, ctx, "da")
        ps = m_.psum()
        keys = m_.sb("keys", [P, DH, 2, S], F32R)
        values = m_.sb("values", [P, DH, TILES, 2 * VD], F32R)
        q_hl = m_.sb("q_hl", [P, Q_SLOTS, 2, P], F32R)
        q_lh = m_.sb("q_lh", [P, Q_SLOTS, 2, P], F32R)
        probs = m_.sb("probs", [P, 2, 2, S])
        at_hi = m_.sb("at_hi", [P, A_SLOTS, 4, P], F32R)
        at_lo = m_.sb("at_lo", [P, A_SLOTS, 4, P], F32R)
        ident = m_.sb("ident", [P, P])
        half = m_.sb("half", [P, 1])
        lam_in = m_.sb("lam_in", [P, 4, HD])
        lam_prod = m_.sb("lam_prod", [P, 2, HD])
        lam_dot = m_.sb("lam_dot", [P, 2])
        neg_lam = m_.sb("neg_lam", [P, 1])
        tops = m_.sb("tops", [P, 4, 2, 4])
        bias = m_.sb("bias", [P, 4, 2])
        sums = m_.sb("sums", [P, 4, 2, 4])
        row_sum = m_.sb("row_sum", [P, 4, 2])
        recip = m_.sb("recip", [P, 4, 2])
        factor = m_.sb("factor", [P, 4])
        o_part = m_.sb("o_part", [P, 2, VD])
        o_row = m_.sb("o_row", [P, 2, VD])
        o_norm = m_.sb("o_norm", [P, 2, VD])
        junk = m_.sb("junk", [P, VD], BF16)
        ss = m_.sb("ss", [P, 2])
        rstd = m_.sb("rstd", [P, 2])

        consts_made, lam_loaded, lam_step = m_.sem("consts_made"), m_.sem("lam_loaded"), m_.sem("lam_step")
        keys_loaded = [m_.sem(f"keys_loaded{c}") for c in range(4)]
        values_loaded = [m_.sem(f"values_loaded{c}") for c in range(4)]
        q_loaded = [m_.sem(f"q_loaded{n}") for n in range(Q_SLOTS)]
        scored, tops_found, bias_ready, exp_done = (m_.sem(n) for n in ("scored", "tops_found", "bias_ready", "exp_done"))
        masked, summed, inverted, factor_ready, pool_scaled, pool_combined = (
            m_.sem(n) for n in ("masked", "summed", "inverted", "factor_ready", "pool_scaled", "pool_combined"))
        combined, turned, hi_done, lo_done, attended = (
            m_.sem(n) for n in ("combined", "turned", "hi_done", "lo_done", "attended"))
        o_copied, o_ready, squared, pool_step, rstd_ready, normed = (
            m_.sem(n) for n in ("o_copied", "o_ready", "squared", "pool_step", "rstd_ready", "normed"))
        stored = [m_.sem(f"stored{n}") for n in range(2)]

        def kind_done(eng, semaphore, h, event):
            eng.wait_ge(semaphore, h * total[event[0]] + ordinal[event])

        def heads(eng, perform):
            for event in order:
                if event[0] == 0:
                    perform(0, *event[1:])
            with eng.Fori(1, DH) as h:
                for ago, *event in order:
                    perform(h - ago if ago else h, *event)
            for ago, *event in order:
                if ago:
                    perform(DH - 1, *event)

        def slot_left(eng, semaphore, h, kind, turn):
            if not isinstance(h, int) or h * total[kind] + turn > 0:
                eng.wait_ge(semaphore, h * total[kind] + turn)

        with nc.Block() as block:
            @block.sync
            def _(sp):
                met = (lam_loaded, 64)
                STORE_LAG = 3

                def load_keys(h, c):
                    at = slice(4 * P * c, 4 * P * (c + 1))
                    sp.dma_start(keys[:, bass.ds(h, 1), :, at].bitcast(F32), k_s[:, bass.ds(h, 1), :, at])\
                        .then_inc(keys_loaded[c], 16)

                def load_values(h, c):
                    at = slice(4 * c, 4 * (c + 1))
                    sp.dma_start(values[:, bass.ds(h, 1), at, :].bitcast(F32),
                                 v_s[:, bass.ds(h, 1), at, :, :].rearrange("p h t a v -> p h t (a v)"))\
                        .then_inc(values_loaded[c], 16)

                def load_q(h, s):
                    slot, t = s % Q_SLOTS, tiles_in_turn[s]
                    src = q_s[t, :, bass.ds(h, 1), :, :].rearrange("p h m n -> p (h m) n")
                    sp.dma_start(q_hl[:, slot, :, :].bitcast(F32), src).then_inc(q_loaded[slot], 16)
                    sp.dma_start(q_lh[0:HD, slot, :, :].bitcast(F32), src[HD:P, :, :]).then_inc(q_loaded[slot], 16)
                    sp.dma_start(q_lh[HD:P, slot, :, :].bitcast(F32), src[0:HD, :, :]).then_inc(q_loaded[slot], 16)

                def store(h, s):
                    row = tiles_in_turn[s] * P
                    wait_apart(sp, met, (normed, h * steps + s + 1))
                    sp.dma_start(mixed[row:row + P, bass.ds(h * VD, VD)], o_norm[:, s % 2, :]).then_inc(stored[s % 2], 16)

                def head(h, first, last):
                    for s in range(steps):
                        if s + Q_SLOTS < steps or not last:
                            wait_apart(sp, met, (scored, h * total["S"] + ordinal["S", s, 1, chunks[s] - 1]))
                            if s + Q_SLOTS < steps:
                                load_q(h, s + Q_SLOTS)
                            else:
                                load_q(h + 1, s + Q_SLOTS - steps)
                        if s >= STORE_LAG:
                            store(h, s - STORE_LAG)
                        elif not first:
                            store(h - 1, steps + s - STORE_LAG)
                        if not last and s % 2 == 1:
                            c = s // 4
                            if s % 4 == 1:
                                wait_apart(sp, met, (keys_loaded[c], 16 * h + 16))
                                load_keys(h + 1, c)
                            else:
                                wait_apart(sp, met, (values_loaded[c], 16 * h + 16))
                                load_values(h + 1, c)

                for n, vec in enumerate(lambdas):
                    sp.dma_start(lam_in[:, n, :], vec.unsqueeze(0).broadcast_to([P, HD])).then_inc(lam_loaded, 16)
                for s in range(Q_SLOTS):
                    load_q(0, s)
                    load_keys(0, s)
                    load_values(0, s)
                sp.wait_ge(*met)
                head(0, True, False)
                with sp.Fori(1, DH - 1) as h:
                    head(h, False, False)
                head(DH - 1, False, True)
                for s in range(steps - STORE_LAG, steps):
                    store(DH - 1, s)
                for q in stored:
                    sp.wait_ge(q, 16 * DH * steps // 2)

            @block.gpsimd
            def _(pool):
                met = (consts_made, 3)
                make_identity(pool, ident, consts_made)
                pool.memset(half[:, :], -0.5).then_inc(consts_made, 1)
                pool.wait_ge(*met)

                def perform(h, what, s, *rest):
                    q, r = s % 2, s % 4
                    if what == "A":
                        c, = rest
                        at = slice(4 * P * c, 4 * P * c + width(s, c))
                        if c == 0:
                            wait_apart(pool, met, (factor_ready, h * steps + s + 1))
                        n = ordinal["A", s, c]
                        pool.tensor_scalar(probs[:, q, 1, at], probs[:, q, 1, at], factor[:, r:r + 1], 1.0,
                                           ALU.mult, ALU.mult).then_inc(pool_scaled, 1)
                        pool.wait_ge(pool_scaled, h * total["A"] + n)
                        pool.tensor_tensor(probs[:, q, 0, at], probs[:, q, 1, at], probs[:, q, 0, at], ALU.add)\
                            .then_inc(pool_combined, 1)
                    elif what == "N":
                        done = h * steps + s + 1
                        wait_apart(pool, met, (squared, done))
                        pool_rstd(pool, rstd[:, q:q + 1], ss[:, q:q + 1], VD, half[:, :], pool_step, done)\
                            .then_inc(rstd_ready, 1)
                        waits = [(rstd_ready, done)]
                        if s >= 2 or not isinstance(h, int) or h > 0:
                            waits.append((stored[q], 16 * (h * (steps // 2) + s // 2)))
                        wait_apart(pool, met, *waits)
                        pool.tensor_scalar(o_norm[:, q, :], o_row[:, q, :], rstd[:, q:q + 1], 1.0, ALU.mult, ALU.mult)\
                            .then_inc(normed, 1)

                heads(pool, perform)

            @block.scalar
            def _(act):
                act.wait_ge(lam_step, 3)
                act.activation(lam_dot[:, :], lam_dot[:, :], ACT.Exp).then_inc(lam_step, 1)

                def perform(h, what, s, *rest):
                    q, r = s % 2, s % 4
                    if what == "E":
                        m, c = rest
                        w = width(s, c)
                        if c == 0:
                            act.wait_ge(bias_ready, h * 2 * steps + 2 * s + m + 1)
                            if m == 0:
                                slot_left(act, turned, h, "T", ordinal["T", s - 2, chunks[s - 2] - 1] if s >= 2 else
                                          ordinal["T", steps + s - 2, chunks[steps + s - 2] - 1] - total["T"])
                        b = S_BANKS[(ordinal["S", s, m, c] - 1) % len(S_BANKS)]
                        act.activation(probs[:, q, m, 4 * P * c:4 * P * c + w], ps[:, b, 0:w], ACT.Exp,
                                       bias=bias[:, r, m:m + 1], accum_out=sums[:, r, m, c:c + 1]).then_inc(exp_done, 1)
                    elif what == "H":
                        c, = rest
                        n = ordinal["T", s, c] - 1
                        kind_done(act, turned, h, ("T", s, c))
                        slot_left(act, attended, h, "V", n + 1 - A_SLOTS)
                        w = width(s, c)
                        act.activation(at_hi[:, n % A_SLOTS, 0:w // P, :],
                                       ps[:, T_BANKS[n % 2], 0:w].rearrange("p (j n) -> p j n", n=P), ACT.Copy)\
                            .then_inc(hi_done, 1)
                    elif what == "O":
                        kind_done(act, attended, h, ("V", s, chunks[s] - 1))
                        act.activation(o_part[:, q, :], ps[:, O_BANK, VD:2 * VD], ACT.Copy,
                                       scale=recip[:, r, 0:1]).then_inc(o_copied, 1)
                    elif what == "Q":
                        act.wait_ge(o_ready, h * steps + s + 1)
                        act.activation(junk[:, :], o_row[:, q, :], ACT.Square, accum_out=ss[:, q:q + 1])\
                            .then_inc(squared, 1)

                heads(act, perform)

            @block.vector
            def _(dve):
                dve.wait_ge(lam_loaded, 64)
                dve.tensor_tensor(lam_prod[:, 0, :], lam_in[:, 0, :], lam_in[:, 1, :], ALU.mult).then_inc(lam_step, 1)
                dve.tensor_tensor(lam_prod[:, 1, :], lam_in[:, 2, :], lam_in[:, 3, :], ALU.mult).then_inc(lam_step, 1)
                dve.wait_ge(lam_step, 2)
                dve.tensor_reduce(lam_dot[:, :], lam_prod[:, :, :], AX.X, ALU.add).then_inc(lam_step, 1)
                dve.wait_ge(lam_step, 4)
                dve.scalar_tensor_tensor(neg_lam[:, :], lam_dot[:, 1:2], LAMBDA_INIT, lam_dot[:, 0:1],
                                         ALU.subtract, ALU.subtract).then_inc(lam_step, 1)
                dve.wait_ge(lam_step, 5)

                def perform(h, what, s, *rest):
                    q, r, n_chunks = s % 2, s % 4, chunks[s]
                    if what == "R":
                        m, c = rest
                        w = width(s, c)
                        b = S_BANKS[(ordinal["S", s, m, c] - 1) % len(S_BANKS)]
                        kind_done(dve, scored, h, ("S", s, m, c))
                        if c == n_chunks - 1:
                            dve.memset(ps[0:HD, b, w - HD:w], NEG).then_inc(masked, 1)
                            dve.wait_ge(masked, h * 2 * steps + 2 * s + m + 1)
                        if n_chunks == 1:
                            dve.tensor_reduce(bias[:, r, m:m + 1], ps[:, b, 0:w], AX.X, ALU.max, negate=True)\
                                .then_inc(bias_ready, 1)
                        else:
                            top = dve.tensor_reduce(tops[:, r, m, c:c + 1], ps[:, b, 0:w], AX.X, ALU.max)
                            if c == n_chunks - 1:
                                top.then_inc(tops_found, 1)
                    elif what == "M" and n_chunks > 1:
                        m, = rest
                        dve.wait_ge(tops_found, h * tops_count(steps) + tops_count(s) + m + 1)
                        dve.tensor_reduce(bias[:, r, m:m + 1], tops[:, r, m, 0:n_chunks], AX.X, ALU.max, negate=True)\
                            .then_inc(bias_ready, 1)
                    elif what == "C":
                        kind_done(dve, exp_done, h, ("E", s, 1, n_chunks - 1))
                        total_of = sums[:, r, :, 0:1]
                        if n_chunks > 1:
                            dve.tensor_reduce(row_sum[:, r, :], sums[:, r, :, 0:n_chunks], AX.X, ALU.add).then_inc(summed, 1)
                            dve.wait_ge(summed, h * tops_count(steps) // 2 + tops_count(s) // 2 + 1)
                            total_of = row_sum[:, r, :].unsqueeze(2)
                        dve.reciprocal(recip[:, r, :].unsqueeze(2), total_of).then_inc(inverted, 1)
                        dve.wait_ge(inverted, h * steps + s + 1)
                        dve.scalar_tensor_tensor(factor[:, r:r + 1], recip[:, r, 1:2], neg_lam[:, 0:1],
                                                 total_of[:, 0, :], ALU.mult, ALU.mult).then_inc(factor_ready, 1)
                    elif what == "B":
                        c, = rest
                        at = slice(4 * P * c, 4 * P * c + width(s, c))
                        if c == 1:
                            dve.wait_ge(factor_ready, h * steps + s + 1)
                        dve.scalar_tensor_tensor(probs[:, q, 0, at], probs[:, q, 1, at], factor[:, r:r + 1],
                                                 probs[:, q, 0, at], ALU.mult, ALU.add).then_inc(combined, 1)
                    elif what == "L":
                        c, = rest
                        n = ordinal["T", s, c] - 1
                        w = width(s, c)
                        kind_done(dve, hi_done, h, ("T", s, c))
                        dve.tensor_tensor(at_lo[:, n % A_SLOTS, 0:w // P, :],
                                          ps[:, T_BANKS[n % 2], 0:w].rearrange("p (j n) -> p j n", n=P),
                                          at_hi[:, n % A_SLOTS, 0:w // P, :].bitcast(F32), ALU.subtract)\
                            .then_inc(lo_done, 1)
                    elif what == "P":
                        dve.wait_ge(o_copied, h * steps + s + 1)
                        if s >= 2 or not isinstance(h, int) or h > 0:
                            dve.wait_ge(normed, h * steps + s - 1)
                        dve.scalar_tensor_tensor(o_row[:, q, :], ps[:, O_BANK, 0:VD], recip[:, r, 0:1],
                                                 o_part[:, q, :], ALU.mult, ALU.add).then_inc(o_ready, 1)

                heads(dve, perform)

            @block.tensor
            def _(pe):
                pe.wait_ge(consts_made, 2)

                def perform(h, what, s, *rest):
                    if what == "S":
                        m, c = rest
                        n, w = ordinal["S", s, m, c] - 1, width(s, c)
                        if m == 0 and c == 0:
                            slot_uses = steps // Q_SLOTS
                            pe.wait_ge(q_loaded[s % Q_SLOTS], 48 * (h * slot_uses + s // Q_SLOTS + 1))
                        if m == 0 and s == chunks.index(c + 1):
                            pe.wait_ge(keys_loaded[c], 16 * h + 16)
                        slot_left(pe, exp_done, h, "S", n + 1 - len(S_BANKS))
                        b = S_BANKS[n % len(S_BANKS)]
                        for j, stack in enumerate((q_hl, q_lh)):
                            last = pe.matmul(ps[:, b, 0:w], stack[:, s % Q_SLOTS, m, :],
                                             keys[:, bass.ds(h, 1), m, 4 * P * c:4 * P * c + w].squeeze(1),
                                             start=(j == 0), stop=(j == 1))
                        last.then_inc(scored, 1)
                    elif what == "T":
                        c, = rest
                        n, w = ordinal["T", s, c] - 1, width(s, c)
                        kind_done(pe, {"A": pool_combined, "B": combined}[COMBINED_BY[c]], h, (COMBINED_BY[c], s, c))
                        slot_left(pe, lo_done, h, "L", n + 1 - len(T_BANKS))
                        for j in range(w // P):
                            at = 4 * P * c + j * P
                            last = pe.transpose(ps[:, T_BANKS[n % 2], j * P:(j + 1) * P],
                                                probs[:, s % 2, 0, at:at + P], ident[:, :])
                        last.then_inc(turned, 1)
                    elif what == "V":
                        c, = rest
                        n = ordinal["V", s, c] - 1
                        kind_done(pe, lo_done, h, ("L", s, c))
                        if s == chunks.index(c + 1):
                            pe.wait_ge(values_loaded[c], 16 * h + 16)
                        if c == 0 and (s > 0 or not isinstance(h, int) or h > 0):
                            pe.wait_ge(o_ready, h * steps + s)
                        for j in range(width(s, c) // P):
                            for i, a in enumerate((at_hi, at_lo)):
                                last = pe.matmul(ps[:, O_BANK, 0:2 * VD], a[:, n % A_SLOTS, j, :],
                                                 values[:, bass.ds(h, 1), 4 * c + j, :].squeeze(1),
                                                 start=(c == 0 and j == 0 and i == 0),
                                                 stop=(4 * c + j == tiles_in_turn[s] and i == 1))
                        last.then_inc(attended, 1)

                heads(pe, perform)
        m_.end()


def out_proj(nc, x, swa_t, mixed, w_out, subln, g_post, g_ffn, x_mid, h_s, h_hl):
    y_order, t_order = [], [("m", 0)]
    for t in range(TILES + 1):
        if t < TILES:
            y_order += [("y", t, 0), ("y", t, 1)]
        if t + 1 < TILES:
            t_order.append(("m", t + 1))
        if t >= 1:
            t_order += [("h", t - 1, 0), ("h", t - 1, 1)]
    y_banks, t_banks = Banks([0, 1, 2, 3], y_order), Banks([4, 5, 6], t_order)
    SC = QA // P
    HW = D // 2
    RAW = 8
    pieces = [(c, slice(n * HW, (n + 1) * HW)) for n in range(2) for c in range(KC)]

    with ExitStack() as ctx:
        m = Memory(nc, ctx, "op")
        ps = m.psum()
        w_hi = m.sb("w_hi", [P, KC, D], F32R)
        w_lo = m.sb("w_lo", [P, KC, D], F32R)
        w_raw = m.sb("w_raw", [P, RAW, HW])
        sub_col = m.sb("sub_col", [P, 1])
        post_row = m.sb("post_row", [P, D])
        ffn_row = m.sb("ffn_row", [P, D])
        ident = m.sb("ident", [P, P])
        half = m.sb("half", [P, 1])
        xb = m.sb("x", [P, 2, D])
        swa_in = m.sb("swa_in", [P, 2, SC, P])
        mix_in = m.sb("mix_in", [P, 2, DW])
        mt_hi = m.sb("mt_hi", [P, 2, KC, P], F32R)
        mt_lo = m.sb("mt_lo", [P, 2, KC, P], F32R)
        y_junk = m.sb("y_junk", [P, D], BF16)
        x_junk = m.sb("x_junk", [P, D], BF16)
        y_ss = m.sb("y_ss", [P, 2, 2])
        y_rstd = m.sb("y_rstd", [P, 2])
        x_ss = m.sb("x_ss", [P, 2])
        x_rstd = m.sb("x_rstd", [P, 2])
        y_norm = m.sb("y_norm", [P, 2, D])
        x_new = m.sb("x_new", [P, 2, D])
        h_row = m.sb("h_row", [P, D])
        ht = m.sb("ht", [P, 2, KC, 2, P], F32R)

        w_loaded = [m.sem(f"w_loaded{n}") for n in range(RAW)]
        w_hi_done, w_lo_done = m.sem("w_hi_done"), m.sem("w_lo_done")
        consts_loaded, consts_made, sub_scaled = m.sem("consts_loaded"), m.sem("consts_made"), m.sem("sub_scaled")
        in_loaded = [m.sem(f"in_loaded{n}") for n in range(2)]
        x_loaded = [m.sem(f"x_loaded{n}") for n in range(2)]
        m_turned, swa_hi, swa_lo, m_hi, m_lo = (m.sem(n) for n in ("m_turned", "swa_hi", "swa_lo", "m_hi", "m_lo"))
        multiplied, y_squared, y_normed, pool_step, y_rstd_ready = (
            m.sem(n) for n in ("multiplied", "y_squared", "y_normed", "pool_step", "y_rstd_ready"))
        x_added, x_squared, x_rstd_ready, h_ready = (m.sem(n) for n in ("x_added", "x_squared", "x_rstd_ready", "h_ready"))
        h_turned, h_hi, h_lo = (m.sem(n) for n in ("h_turned", "h_hi", "h_lo"))
        x_stored = [m.sem(f"x_stored{n}") for n in range(2)]
        h_stored = [m.sem(f"h_stored{n}") for n in range(2)]
        rows_loaded = m.sem("rows_loaded")
        h_fetched = [m.sem(f"h_fetched{n}") for n in range(2)]
        read_out = {"y": (y_normed, lambda t, n: 2 * t + n + 1), "m": (m_lo, lambda t: t + 1),
                    "h": (h_lo, lambda t, n: 2 * t + n + 1)}

        with nc.Block() as block:
            @block.sync
            def _(sp):
                met = (consts_loaded, 16)

                def load_in(k, i, ahead):
                    p = k % 2
                    at = steady(lambda t: (t + ahead) * P, k, i)
                    sp.dma_start(swa_in[:, p, :, :], swa_t[:, :, bass.ds(at, P)]).then_inc(in_loaded[p], 16)
                    sp.dma_start(mix_in[:, p, :], mixed[bass.ds(at, P), :]).then_inc(in_loaded[p], 16)

                def store_tile(sp, k, i):
                    p = k % 2
                    at = steady(lambda t: t * P, k, i)
                    wait_apart(sp, (consts_loaded, 16), (x_added, steady(lambda t: t + 1, k, i)))
                    sp.dma_start(x_mid[bass.ds(at, P), :], x_new[:, p, :]).then_inc(x_stored[p], 16)
                    wait_apart(sp, (consts_loaded, 16), (h_lo, steady(lambda t: 2 * t + 2, k, i)))
                    sp.dma_start(h_s[:, :, :, bass.ds(at, P)], ht[:, p, :, :, :].bitcast(F32)).then_inc(h_stored[p], 16)

                with nc.allow_non_contiguous_dma(reason="gains by column"):
                    sp.dma_start(sub_col[:, :], subln.rearrange("(c p) -> p c", p=P)).then_inc(consts_loaded, 16)
                for n in range(2):
                    load_in(n, None, 0)
                for n, (c, cols) in enumerate(pieces):
                    if n >= RAW:
                        sp.wait_ge(w_lo_done, n - RAW + 1)
                    sp.dma_start(w_raw[:, n % RAW, :], w_out[c * P:(c + 1) * P, cols]).then_inc(w_loaded[n % RAW], 16)
                    if n == KC - 1:
                        sp.dma_start(post_row[:, :], g_post.unsqueeze(0).broadcast_to([P, D])).then_inc(rows_loaded, 16)
                        sp.dma_start(ffn_row[:, :], g_ffn.unsqueeze(0).broadcast_to([P, D])).then_inc(rows_loaded, 16)
                for n in range(2):
                    sp.dma_start(xb[:, n, :], x[n * P:(n + 1) * P, :]).then_inc(x_loaded[n], 16)
                for k, i in tiles(sp):
                    p = k % 2
                    if k + 2 < TILES:
                        wait_apart(sp, met, (swa_lo, steady(lambda t: t + 1, k, i)), (m_turned, steady(lambda t: t + 1, k, i)))
                        load_in(k, i, 2)
                    if k >= 1:
                        store_tile(sp, k - 1, i)
                        if k + 1 < TILES:
                            at = steady(lambda t: (t + 1) * P, k, i)
                            sp.dma_start(xb[:, 1 - p, :], x[bass.ds(at, P), :]).then_inc(x_loaded[1 - p], 16)
                    if k in (5, TILES - 2):
                        n = int(k > 5)
                        for s in h_stored:
                            sp.wait_ge(s, 16 * BT // 2)
                        half_of = slice(n * KC // 2, (n + 1) * KC // 2)
                        sp.dma_start(h_hl[:, half_of, :, :].bitcast(F32), h_s[:, half_of, :, 0:TB]).then_inc(h_fetched[n], 16)
                store_tile(sp, TILES - 1, None)
                for s in h_fetched:
                    sp.wait_ge(s, 16)
                for s in x_stored + h_stored:
                    sp.wait_ge(s, 16 * TILES // 2)

            @block.gpsimd
            def _(pool):
                make_identity(pool, ident, consts_made)
                pool.memset(half[:, :], -0.5).then_inc(consts_made, 1)
                pool.wait_ge(consts_made, 3)

                def split_swa(k, i):
                    q = k % 2
                    pool.wait_ge(swa_hi, steady(lambda t: t + 1, k, i))
                    pool.tensor_tensor(mt_lo[:, q, 0:SC, :], swa_in[:, q, :, :], mt_hi[:, q, 0:SC, :].bitcast(F32),
                                       ALU.subtract).then_inc(swa_lo, 1)

                def y_rstd_of(k, i):
                    q = k % 2
                    pool.wait_ge(y_squared, steady(lambda t: 2 * t + 2, k, i))
                    if k >= 2:
                        pool.wait_ge(y_normed, steady(lambda t: 2 * t - 2, k, i))
                    pool.tensor_tensor(y_rstd[:, q:q + 1], y_ss[:, q, 0:1], y_ss[:, q, 1:2], ALU.add).then_inc(pool_step, 1)
                    wait_apart(pool, (consts_made, 3), (pool_step, steady(lambda t: 3 * t + 1, k, i)))
                    pool_rstd(pool, y_rstd[:, q:q + 1], y_rstd[:, q:q + 1], D, half[:, :], pool_step,
                              steady(lambda t: 3 * t + 2, k, i)).then_inc(y_rstd_ready, 1)

                def add_x(k, i):
                    q = k % 2
                    pool.wait_ge(x_loaded[q], steady(lambda t: 16 * (t // 2 + 1), k, i))
                    if k >= 2:
                        pool.wait_ge(x_stored[q], steady(lambda t: 16 * (t // 2), k, i))
                        pool.wait_ge(h_ready, steady(lambda t: t - 1, k, i))
                    pool.wait_ge(y_normed, steady(lambda t: 2 * t + 2, k, i))
                    pool.tensor_tensor(x_new[:, q, :], y_norm[:, q, :], xb[:, q, :], ALU.add).then_inc(x_added, 1)

                def x_rstd_of(k, i):
                    q = k % 2
                    waits = [(x_squared, steady(lambda t: t + 1, k, i))]
                    if k >= 2:
                        waits.append((h_ready, steady(lambda t: t - 1, k, i)))
                    wait_apart(pool, (consts_made, 3), *waits)
                    pool_rstd(pool, x_rstd[:, q:q + 1], x_ss[:, q:q + 1], D, half[:, :], pool_step,
                              steady(lambda t: 3 * t + 3, k, i)).then_inc(x_rstd_ready, 1)

                split_swa(0, None)
                for k, i in tiles(pool):
                    if k >= 1:
                        y_rstd_of(k - 1, i)
                        add_x(k - 1, i)
                    if k + 1 < TILES:
                        split_swa(k + 1, i)
                    if k >= 1:
                        x_rstd_of(k - 1, i)
                y_rstd_of(TILES - 1, None)
                add_x(TILES - 1, None)
                x_rstd_of(TILES - 1, None)

            @block.scalar
            def _(act):
                def hi_m(k, i):
                    q = k % 2
                    act.wait_ge(in_loaded[q], steady(lambda t: 32 * (t // 2 + 1), k, i))
                    if k >= 2:
                        act.wait_ge(multiplied, steady(lambda t: 2 * t - 2, k, i))
                    act.activation(mt_hi[:, q, 0:SC, :], swa_in[:, q, :, :], ACT.Copy).then_inc(swa_hi, 1)
                    act.wait_ge(m_turned, steady(lambda t: t + 1, k, i))
                    act.activation(mt_hi[:, q, SC:KC, :], ps[:, t_banks.bank("m", k), :].rearrange("p (c n) -> p c n", n=P),
                                   ACT.Copy).then_inc(m_hi, 1)

                def square_y(k, i):
                    q = k % 2
                    for n in range(2):
                        act.wait_ge(multiplied, steady(lambda t: 2 * t + n + 1, k, i))
                        if k >= 1 and n == 0:
                            act.wait_ge(y_rstd_ready, steady(lambda t: t, k, i))
                        act.activation(y_junk[:, n * HW:(n + 1) * HW], ps[:, y_banks.bank("y", k, n), :], ACT.Square,
                                       accum_out=y_ss[:, q, n:n + 1]).then_inc(y_squared, 1)

                def square_x(k, i):
                    q = k % 2
                    act.wait_ge(x_added, steady(lambda t: t + 1, k, i))
                    if k >= 1:
                        act.wait_ge(x_rstd_ready, steady(lambda t: t, k, i))
                    act.activation(x_junk[:, :], x_new[:, q, :], ACT.Square, accum_out=x_ss[:, q:q + 1]).then_inc(x_squared, 1)

                def hi_h(k, i):
                    q = k % 2
                    for n in range(2):
                        act.wait_ge(h_turned, steady(lambda t: 2 * t + n + 1, k, i))
                        if k >= 2 and n == 0:
                            act.wait_ge(h_stored[q], steady(lambda t: 16 * (t // 2), k, i))
                        act.activation(ht[:, q, 4 * n:4 * n + 4, 0, :],
                                       ps[:, t_banks.bank("h", k, n), :].rearrange("p (c n) -> p c n", n=P), ACT.Copy)\
                            .then_inc(h_hi, 1)

                act.wait_ge(consts_loaded, 16)
                act.wait_ge(sub_scaled, 1)
                hi_m(0, None)
                for n, (c, cols) in enumerate(pieces):
                    act.wait_ge(w_loaded[n % RAW], 16 * (n // RAW + 1))
                    act.activation(w_hi[:, c, cols], w_raw[:, n % RAW, :], ACT.Copy, scale=1.0 if c < SC else sub_col[:, 0:1])\
                        .then_inc(w_hi_done, 1)
                for k, i in tiles(act):
                    if k >= 1:
                        square_y(k - 1, i)
                    if k + 1 < TILES:
                        hi_m(k + 1, i)
                    if k >= 1:
                        square_x(k - 1, i)
                        hi_h(k - 1, i)
                square_y(TILES - 1, None)
                square_x(TILES - 1, None)
                hi_h(TILES - 1, None)

            @block.vector
            def _(dve):
                def lo_m(k, i):
                    q = k % 2
                    dve.wait_ge(m_hi, steady(lambda t: t + 1, k, i))
                    dve.tensor_tensor(mt_lo[:, q, SC:KC, :], ps[:, t_banks.bank("m", k), :].rearrange("p (c n) -> p c n", n=P),
                                      mt_hi[:, q, SC:KC, :].bitcast(F32), ALU.subtract).then_inc(m_lo, 1)

                def norm_y(k, i):
                    q = k % 2
                    dve.wait_ge(y_rstd_ready, steady(lambda t: t + 1, k, i))
                    if k >= 2:
                        dve.wait_ge(x_added, steady(lambda t: t - 1, k, i))
                    for n in range(2):
                        at = slice(n * HW, (n + 1) * HW)
                        dve.scalar_tensor_tensor(y_norm[:, q, at], ps[:, y_banks.bank("y", k, n), :], y_rstd[:, q:q + 1],
                                                 post_row[:, at], ALU.mult, ALU.mult).then_inc(y_normed, 1)

                def norm_x(k, i):
                    q = k % 2
                    dve.wait_ge(x_rstd_ready, steady(lambda t: t + 1, k, i))
                    if k >= 1:
                        dve.wait_ge(h_turned, steady(lambda t: 2 * t, k, i))
                    dve.scalar_tensor_tensor(h_row[:, :], x_new[:, q, :], x_rstd[:, q:q + 1], ffn_row[:, :],
                                             ALU.mult, ALU.mult).then_inc(h_ready, 1)

                def lo_h(k, i):
                    q = k % 2
                    for n in range(2):
                        dve.wait_ge(h_hi, steady(lambda t: 2 * t + n + 1, k, i))
                        dve.tensor_tensor(ht[:, q, 4 * n:4 * n + 4, 1, :],
                                          ps[:, t_banks.bank("h", k, n), :].rearrange("p (c n) -> p c n", n=P),
                                          ht[:, q, 4 * n:4 * n + 4, 0, :].bitcast(F32), ALU.subtract).then_inc(h_lo, 1)

                dve.wait_ge(consts_loaded, 16)
                dve.tensor_scalar(sub_col[:, :], sub_col[:, :], 1.0 - LAMBDA_INIT, None, ALU.mult).then_inc(sub_scaled, 1)
                dve.wait_ge(sub_scaled, 1)
                lo_m(0, None)
                for n, (c, cols) in enumerate(pieces):
                    dve.wait_ge(w_hi_done, n + 1)
                    dve.scalar_tensor_tensor(w_lo[:, c, cols], w_raw[:, n % RAW, :], 1.0 if c < SC else sub_col[:, 0:1],
                                             w_hi[:, c, cols].bitcast(F32), ALU.mult, ALU.subtract).then_inc(w_lo_done, 1)
                dve.wait_ge(rows_loaded, 32)
                for k, i in tiles(dve):
                    if k >= 1:
                        norm_y(k - 1, i)
                    if k + 1 < TILES:
                        lo_m(k + 1, i)
                    if k >= 1:
                        norm_x(k - 1, i)
                        lo_h(k - 1, i)
                norm_y(TILES - 1, None)
                norm_x(TILES - 1, None)
                lo_h(TILES - 1, None)

            @block.tensor
            def _(pe):
                def turn_m(k, i):
                    pe.wait_ge(in_loaded[k % 2], steady(lambda t: 32 * (t // 2 + 1), k, i))
                    t_banks.free(pe, read_out, k, i, "m")
                    for j in range(DW // P):
                        last = pe.transpose(ps[:, t_banks.bank("m", k), j * P:(j + 1) * P],
                                            mix_in[:, k % 2, j * P:(j + 1) * P], ident[:, :])
                    last.then_inc(m_turned, 1)

                def multiply(n, k, i):
                    q = k % 2
                    if n == 0:
                        pe.wait_ge(swa_lo, steady(lambda t: t + 1, k, i))
                    y_banks.free(pe, read_out, k, i, "y", n)
                    for c in range(KC):
                        if n == 0 and c == SC:
                            pe.wait_ge(m_lo, steady(lambda t: t + 1, k, i))
                        if k == 0:
                            pe.wait_ge(w_lo_done, n * KC + c + 1)
                        for j, (lhs, rhs) in enumerate(((mt_hi, w_hi), (mt_hi, w_lo), (mt_lo, w_hi))):
                            last = pe.matmul(ps[:, y_banks.bank("y", k, n), :], lhs[:, q, c, :],
                                             rhs[:, c, n * HW:(n + 1) * HW],
                                             start=(c == 0 and j == 0), stop=(c == KC - 1 and j == 2))
                    last.then_inc(multiplied, 1)

                def turn_h(k, i):
                    pe.wait_ge(h_ready, steady(lambda t: t + 1, k, i))
                    for n in range(2):
                        t_banks.free(pe, read_out, k, i, "h", n)
                        for j in range(4):
                            at = (4 * n + j) * P
                            last = pe.transpose(ps[:, t_banks.bank("h", k, n), j * P:(j + 1) * P], h_row[:, at:at + P],
                                                ident[:, :])
                        last.then_inc(h_turned, 1)

                pe.wait_ge(consts_made, 2)
                turn_m(0, None)
                for k, i in tiles(pe):
                    multiply(0, k, i)
                    if k + 1 < TILES:
                        turn_m(k + 1, i)
                    multiply(1, k, i)
                    if k >= 1:
                        turn_h(k - 1, i)
                turn_h(TILES - 1, None)
        m.end()


def ffn(nc, h_s, h_hl, x_mid, w_gate, w_up, w_down, g_post, out):
    HW = D // 2
    UP = 2 * FC
    DOWN = FC
    UNITS = UP + DOWN
    R = 4
    slot_uses = [len(range(s, UNITS, R)) for s in range(R)]
    ENDS = (UP + DOWN // 2 - 1, UNITS - 1)
    USED = UNITS - len(ENDS)

    with ExitStack() as ctx:
        m = Memory(nc, ctx, "ff")
        ps = m.psum()
        g_hi = m.sb("g_hi", [P, FC, TB], F32R)
        g_lo = m.sb("g_lo", [P, FC, TB], F32R)
        w_raw = m.sb("w_raw", [P, R, D])
        w_hi = m.sb("w_hi", [P, R, D], F32R)
        w_lo = m.sb("w_lo", [P, R, D], F32R)
        y = m.sb("y", [P, BT, D])
        xm = m.sb("xm", [P, D])
        post_row = m.sb("post_row", [P, D])
        silu = m.sb("silu", [P, 2, TB])
        gated = m.sb("gated", [P, 2, TB])
        junk = m.sb("junk", [P, BT, HW], BF16)
        half = m.sb("half", [P, BT])
        ss = m.sb("ss", [P, 2, BT])
        rstd = m.sb("rstd", [P, BT])

        consts_made, post_loaded = m.sem("consts_made"), m.sem("post_loaded")
        h_loaded = m.sem("h_loaded")
        w_loaded = [m.sem(f"w_loaded{n}") for n in range(R)]
        w_hi_done, w_split, unit_used = m.sem("w_hi_done"), m.sem("w_split"), m.sem("unit_used")
        silu_done, gate_done, g_hi_done, g_split = (m.sem(n) for n in ("silu_done", "gate_done", "g_hi_done", "g_split"))
        y_done, y_squared, y_copied = m.sem("y_done"), m.sem("y_squared"), m.sem("y_copied")
        pool_step, rstd_ready, y_normed = m.sem("pool_step"), m.sem("rstd_ready"), m.sem("y_normed")
        xm_loaded, x_added, dve_added = m.sem("xm_loaded"), m.sem("x_added"), m.sem("dve_added")
        stored, last_stored = m.sem("stored"), m.sem("last_stored")

        def used(b, u):
            if u in ENDS:
                return y_done, (b * 2 + ENDS.index(u) + 1) * BT
            return unit_used, b * USED + u + 1 - sum(e < u for e in ENDS)

        def blocks(eng, body):
            body(0, True, False)
            with eng.Fori(1, BLOCKS - 1) as b:
                body(b, False, False)
            body(BLOCKS - 1, False, True)

        def pairs(eng, body):
            body(0, True)
            with eng.Fori(1, FC // 2) as j:
                body(j, False)

        with nc.Block() as block:
            @block.sync
            def _(sp):
                met = (post_loaded, 16)

                def load_h(b):
                    sp.dma_start(h_hl[:, :, :, :].bitcast(F32), h_s[:, :, :, bass.ds(b * TB, TB)]).then_inc(h_loaded, 16)

                def body(b, first, last):
                    def up_pair(j, peeled):
                        for u in range(4):
                            w = (w_gate, w_up)[u % 2]
                            if not (first and peeled):
                                wait_apart(sp, met, (w_split, b * UNITS if peeled else b * UNITS + 4 * j + u - R + 1))
                            sp.dma_start(w_raw[:, u, :], w[bass.ds(2 * j + u // 2, 1), :, :].rearrange("f p n -> p (f n)"))\
                                .then_inc(w_loaded[u], 16)

                    up_pair(0, True)
                    if first:
                        sp.dma_start(post_row[:, :], g_post.unsqueeze(0).broadcast_to([P, D])).then_inc(post_loaded, 16)
                        sp.wait_ge(*met)
                    with sp.Fori(1, FC // 2) as j:
                        up_pair(j, False)
                    for d in range(DOWN):
                        u = UP + d
                        wait_apart(sp, met, (w_split, b * UNITS + u - R + 1))
                        sp.dma_start(w_raw[:, u % R, :], w_down[d // (FC // 2), d % (FC // 2), :, :])\
                            .then_inc(w_loaded[u % R], 16)
                        if d == R + 2 and not last:
                            wait_apart(sp, met, (unit_used, b * USED + UP))
                            load_h(b + 1)
                    if last:
                        sp.wait_ge(w_split, BLOCKS * UNITS)
                        for j in range(BT):
                            sp.dma_start(w_raw[:, j, :], x_mid[b * TB + j * P:b * TB + (j + 1) * P, :])\
                                .then_inc(w_loaded[j], 16)
                        for j in range(BT):
                            added = (x_added, b * BT + j // 2 + 1) if j % 2 == 0 else (dve_added, j // 2 + 1)
                            sp.wait_ge(*added)
                            sp.dma_start(out[b * TB + j * P:b * TB + (j + 1) * P, :], y[:, j, :]).then_inc(last_stored, 16)
                        sp.wait_ge(stored, 16 * (TILES - BT))
                        sp.wait_ge(last_stored, 16 * BT)

                blocks(sp, body)

            @block.gpsimd
            def _(pool):
                met = (consts_made, 1)
                pool.memset(half[:, :], -0.5).then_inc(consts_made, 1)
                pool.wait_ge(*met)
                pool.memset(junk[:, 0, 0:1], 0.0).then_inc(g_split, 1)

                def body(b, first, last):
                    def split_g(f, q):
                        wait_apart(pool, met, (g_hi_done, b * FC + f + 1))
                        pool.tensor_tensor(g_lo[:, bass.ds(f, 1), :].squeeze(1), gated[:, q, :],
                                           g_hi[:, bass.ds(f, 1), :].squeeze(1).bitcast(F32), ALU.subtract).then_inc(g_split, 1)

                    with pool.Fori(0, FC // 2) as j:
                        for q in range(2):
                            split_g(2 * j + q, q)
                    pool.wait_ge(y_squared, (b + 1) * 2 * BT)
                    if not first:
                        pool.wait_ge(y_normed, b * BT)
                    pool.tensor_tensor(rstd[:, :], ss[:, 0, :], ss[:, 1, :], ALU.add).then_inc(pool_step, 1)
                    wait_apart(pool, met, (pool_step, 2 * b + 1))
                    pool_rstd(pool, rstd[:, :], rstd[:, :], D, half[:, :], pool_step, 2 * b + 2).then_inc(rstd_ready, 1)
                    if last:
                        for j in range(0, BT, 2):
                            pool.wait_ge(w_loaded[j], 16 * (BLOCKS * slot_uses[j] + 1))
                            pool.wait_ge(y_normed, b * BT + j + 1)
                            pool.tensor_tensor(y[:, j, :], y[:, j, :], w_raw[:, j, :], ALU.add).then_inc(x_added, 1)
                        return
                    for j in range(BT):
                        row = b * TB + j * P
                        wait_apart(pool, met, (x_added, b * BT + j))
                        pool.dma_start(xm[:, :], x_mid[bass.ds(row, P), :]).then_inc(xm_loaded, 16)
                        pool.wait_ge(xm_loaded, 16 * (b * BT + j + 1))
                        pool.wait_ge(y_normed, b * BT + j + 1)
                        pool.tensor_tensor(y[:, j, :], y[:, j, :], xm[:, :], ALU.add).then_inc(x_added, 1)
                        wait_apart(pool, met, (x_added, b * BT + j + 1))
                        pool.dma_start(out[bass.ds(row, P), :], y[:, j, :]).then_inc(stored, 16)

                blocks(pool, body)

            @block.scalar
            def _(act):
                def hi_unit(b, slot, turn, semaphore, count):
                    act.wait_ge(w_loaded[slot], 16 * (b * slot_uses[slot] + turn + 1))
                    act.wait_ge(semaphore, count)
                    act.activation(w_hi[:, slot, :], w_raw[:, slot, :], ACT.Copy).then_inc(w_hi_done, 1)

                def silu_of(b, f, q):
                    act.wait_ge(unit_used, b * USED + 2 * f + 1)
                    act.activation(silu[:, q, :], ps[:, 2 * q, :], ACT.Silu).then_inc(silu_done, 1)
                    wait_apart(act, (post_loaded, 16), (gate_done, b * FC + f + 1), (y_done, b * 2 * BT))
                    act.activation(g_hi[:, bass.ds(f, 1), :].squeeze(1), gated[:, q, :], ACT.Copy).then_inc(g_hi_done, 1)

                def square(b, n):
                    for j in range(BT):
                        act.wait_ge(y_done, b * 2 * BT + n * BT + j + 1)
                        if j == 0:
                            act.wait_ge(y_squared, (b * 2 + n) * BT)
                            if n == 0:
                                act.wait_ge(rstd_ready, b)
                        act.activation(junk[:, j, :], ps[:, (4 if n == 0 else 0) + j, :], ACT.Square,
                                       accum_out=ss[:, n, j:j + 1]).then_inc(y_squared, 1)

                def body(b, first, last):
                    def up_pair(j, peeled):
                        for u in range(4):
                            if not peeled:
                                hi_unit(b, u, j, unit_used, b * USED + 4 * j + u - R + 1)
                            elif u > 0:
                                hi_unit(b, u, j, y_done, b * 2 * BT)
                            if u % 2 == 1 and not peeled:
                                silu_of(b, 2 * j - 2 + u // 2, u // 2)

                    pairs(act, up_pair)
                    for d in range(DOWN):
                        u = UP + d
                        hi_unit(b, u % R, u // R, *used(b, u - R))
                        if d in (1, 3):
                            silu_of(b, FC - 2 + d // 2, d // 2)
                        if d == FC // 2 + R - 1:
                            square(b, 0)
                    if not last:
                        hi_unit(b + 1, 0, 0, *used(b, UNITS - 2))
                    square(b, 1)

                act.wait_ge(w_loaded[0], 16)
                act.activation(w_hi[:, 0, :], w_raw[:, 0, :], ACT.Copy).then_inc(w_hi_done, 1)
                blocks(act, body)

            @block.vector
            def _(dve):
                def split_unit(slot, count):
                    dve.wait_ge(w_hi_done, count)
                    dve.tensor_tensor(w_lo[:, slot, :], w_raw[:, slot, :], w_hi[:, slot, :].bitcast(F32), ALU.subtract)\
                        .then_inc(w_split, 1)

                def gate(b, f, q):
                    dve.wait_ge(silu_done, b * FC + f + 1)
                    dve.wait_ge(unit_used, b * USED + 2 * f + 2)
                    dve.wait_ge(g_split, b * FC + f - q + 1)
                    dve.tensor_tensor(gated[:, q, :], silu[:, q, :], ps[:, 2 * q + 1, :], ALU.mult).then_inc(gate_done, 1)

                def copy_y(b, n):
                    for j in range(BT):
                        dve.wait_ge(y_squared, b * 2 * BT + n * BT + j + 1)
                        if n == 0 and j == 0:
                            dve.wait_ge(stored, 16 * BT * b)
                        dve.tensor_copy(y[:, j, n * HW:(n + 1) * HW], ps[:, (4 if n == 0 else 0) + j, :]).then_inc(y_copied, 1)

                def norm_y(b, j):
                    if j == 0:
                        dve.wait_ge(post_loaded, 16)
                        dve.wait_ge(rstd_ready, b + 1)
                        dve.wait_ge(y_copied, (b + 1) * 2 * BT)
                    dve.scalar_tensor_tensor(y[:, j, :], y[:, j, :], rstd[:, j:j + 1], post_row[:, :], ALU.mult, ALU.mult)\
                        .then_inc(y_normed, 1)

                def body(b, first, last):
                    def up_pair(j, peeled):
                        for u in range(4):
                            if not (peeled and u == 0):
                                split_unit(u, b * UNITS + 4 * j + u + 1)
                            if u % 2 == 1 and not peeled:
                                gate(b, 2 * j - 2 + u // 2, u // 2)
                            if peeled and not first:
                                norm_y(b - 1, u)

                    pairs(dve, up_pair)
                    for d in range(DOWN):
                        u = UP + d
                        split_unit(u % R, b * UNITS + u + 1)
                        if d in (1, 3):
                            gate(b, FC - 2 + d // 2, d // 2)
                        if d == FC // 2 + R - 1:
                            copy_y(b, 0)
                    if not last:
                        split_unit(0, (b + 1) * UNITS + 1)
                    copy_y(b, 1)

                split_unit(0, 1)
                blocks(dve, body)
                for j in range(BT):
                    norm_y(BLOCKS - 1, j)
                    if j % 2 == 1:
                        dve.wait_ge(y_normed, (BLOCKS - 1) * BT + j + 1)
                        dve.wait_ge(w_loaded[j], 16 * (BLOCKS * slot_uses[j] + 1))
                        dve.tensor_tensor(y[:, j, :], y[:, j, :], w_raw[:, j, :], ALU.add).then_inc(dve_added, 1)

            @block.tensor
            def _(pe):
                def multiply_up(b, j, u, peeled):
                    pe.wait_ge(w_split, b * UNITS + 4 * j + u + 1)
                    if peeled:
                        pe.wait_ge(y_copied, b * 2 * BT)
                    else:
                        pe.wait_ge(gate_done, b * FC + 2 * j + u // 2 - 1)
                    for c in range(KC):
                        at = slice(c * P, (c + 1) * P)
                        for n, (w, a) in enumerate(((w_hi, 0), (w_hi, 1), (w_lo, 0))):
                            last = pe.matmul(ps[:, u, :], w[:, u, at], h_hl[:, c, a, :],
                                             start=(c == 0 and n == 0), stop=(c == KC - 1 and n == 2))
                    last.then_inc(unit_used, 1)

                def body(b, first, last):
                    if not first:
                        pe.wait_ge(h_loaded, 16 * b)

                    def up_pair(j, peeled):
                        for u in range(4):
                            multiply_up(b, j, u, peeled)

                    pairs(pe, up_pair)
                    for d in range(DOWN):
                        u = UP + d
                        n, pair = d // (FC // 2), d % (FC // 2)
                        pe.wait_ge(w_split, b * UNITS + u + 1)
                        if pair == 0:
                            if n == 0:
                                pe.wait_ge(y_copied, b * 2 * BT)
                            else:
                                pe.wait_ge(gate_done, (b + 1) * FC)
                        if n == 0:
                            pe.wait_ge(g_split, b * FC + 2 * pair + 2 + 1)
                        for j in range(BT):
                            bank = (4 if n == 0 else 0) + j
                            for e in range(2):
                                f = 2 * pair + e
                                rhs = slice(e * HW, (e + 1) * HW)
                                for i, (g, w) in enumerate(((g_hi, w_hi), (g_hi, w_lo), (g_lo, w_hi))):
                                    last = pe.matmul(ps[:, bank, :], g[:, f, j * P:(j + 1) * P], w[:, u % R, rhs],
                                                     start=(f == 0 and i == 0), stop=(f == FC - 1 and i == 2))
                            if pair == FC // 2 - 1:
                                last.then_inc(y_done, 1)
                        if pair < FC // 2 - 1:
                            last.then_inc(unit_used, 1)

                blocks(pe, body)
        m.end()


def hybrid_block(nc, x, w_in, sinks, lambda_q1, lambda_k1, lambda_q2, lambda_k2, subln, w_out, g_mix_pre, g_mix_post,
                 g_ffn_pre, g_ffn_post, w_gate, w_up, w_down, rope, out):
    def scratch(name, shape):
        return nc.dram_tensor(name, shape, F32, kind="Internal").ap()

    swa_t = scratch("swa_t", (P, QA // P, S))
    q_s = scratch("q_s", (TILES, P, DH, 2, P))
    k_s = scratch("k_s", (P, DH, 2, S))
    v_s = scratch("v_s", (P, DH, TILES, 2, P))
    mixed = scratch("mixed", (S, DW))
    x_mid = scratch("x_mid", (S, D))
    h_s = scratch("h_s", (P, KC, 2, S))
    swa_phase(nc, x, w_in, g_mix_pre, sinks, rope, swa_t)
    diff_proj(nc, x, w_in, g_mix_pre, rope, q_s, k_s, v_s)
    diff_attn(nc, q_s, k_s, v_s, [lambda_q1, lambda_k1, lambda_q2, lambda_k2], mixed)
    with nc.sbuf_tensor("h_hl", [P, KC, 2, TB], F32R) as h_hl:
        out_proj(nc, x, swa_t, mixed, w_out, subln, g_mix_post, g_ffn_pre, x_mid, h_s, h_hl)
        ffn(nc, h_s, h_hl, x_mid, w_gate, w_up, w_down, g_ffn_post, out)


def rope_table():
    inv = 1.0 / (10000.0 ** (np.arange(0, HD, 2, dtype=np.float32) / HD))
    angle = np.arange(S, dtype=np.float32)[:, None] * inv.astype(np.float32)[None, :]
    cos, sin = np.cos(angle), np.sin(angle)
    table = np.concatenate([cos, cos, -sin, sin], axis=1).astype(np.float32)
    return np.concatenate([table, table * np.float32(SCALE)], axis=1)


_INS = ['x', 'w_in', 'swa_sinks', 'diff_lambda_q1', 'diff_lambda_k1', 'diff_lambda_q2', 'diff_lambda_k2', 'diff_subln',
        'w_out', 'norm_mix_pre', 'norm_mix_post', 'norm_ffn_pre', 'norm_ffn_post', 'w_gate', 'w_up', 'w_down']


def kernel(**inputs):
    import numpy as _np
    import concourse.bacc as _bacc
    from concourse import mybir as _mybir
    from concourse.bass_utils import run_bass_kernel_spmd as _run

    laid_out = {name: _np.asarray(inputs[name])[0] for name in _INS}
    for name in ('w_gate', 'w_up'):
        laid_out[name] = laid_out[name].reshape(KC, P, FC, P).transpose(2, 1, 0, 3).reshape(FC, P, D)
    laid_out['w_down'] = laid_out['w_down'].reshape(FC // 2, 2, P, 2, D // 2).transpose(3, 0, 2, 1, 4)\
        .reshape(2, FC // 2, P, D)
    laid_out['rope'] = rope_table()

    nc = _bacc.Bacc("TRN2", target_bir_lowering=False, num_devices=1)
    arrays, args = {}, []
    for name in _INS + ['rope']:
        a = _np.ascontiguousarray(laid_out[name])
        arrays[f"in_{name}_dram"] = a
        args.append(nc.dram_tensor(f"in_{name}_dram", a.shape, _mybir.dt.from_np(a.dtype), kind="ExternalInput").ap())
    args.append(nc.dram_tensor("out_0_dram", (S, D), _mybir.dt.float32, kind="ExternalOutput").ap())
    hybrid_block(nc, *args)
    r = _run(nc, [arrays], core_ids=[0])
    return r.results[0]["out_0_dram"].reshape(1, S, D)
```
